# Optimizing a Trainium2 kernel written in Bass

```python
import jax, jax.numpy as jnp
from jax import lax
import numpy as np

D_MODEL = 1024
BATCH = 1
SEQ = 1024
DEPTH = 1

N_META = 16
CHUNK = 128
HGRN_HEADS = 4
HGRN_HEAD_DIM = 128
HGRN_WIDTH = HGRN_HEADS * HGRN_HEAD_DIM
CONV_GROUPS = 4
CONV_WIDTH_CH = 512
CONV_K = 3
MIX_WIDTH = HGRN_WIDTH + CONV_WIDTH_CH
IN_PROJ_WIDTH = 4 * HGRN_WIDTH + 3 * CONV_WIDTH_CH
N_EXPERTS = 64
TOP_K = 8
EXPERT_FF = 256
SHARED_FF = 256
ROUTED_SCALE = 2.5
EXPERT_BLOCK = 128
EPS = 1e-6

kernel_name = 'hymba_hgrn2_shortconv_moe'

def rmsnorm(x, g):
    xf = x.astype(jnp.float32)
    y = xf * lax.rsqrt(jnp.mean(xf * xf, axis=-1, keepdims=True) + EPS)
    return (y * g.astype(jnp.float32)).astype(x.dtype)

def group_rmsnorm(x, g, n_groups):
    shp = x.shape
    xf = x.astype(jnp.float32).reshape(shp[:-1] + (n_groups, shp[-1] // n_groups))
    y = xf * lax.rsqrt(jnp.mean(xf * xf, axis=-1, keepdims=True) + EPS)
    return (y.reshape(shp) * g.astype(jnp.float32)).astype(x.dtype)

def hgrn2_mixer(q, f_pre, i_val, g_out, lb, norm_g):
    bsz, t_len, _ = q.shape
    lb = lb.astype(jnp.float32)
    z = f_pre.astype(jnp.float32)
    log_f = jnp.log(lb + (1.0 - lb) * jax.nn.sigmoid(z))
    k = (1.0 - lb) * jax.nn.sigmoid(-z)
    pad = CHUNK - N_META

    def to_chunks(a):
        a = jnp.pad(a.astype(jnp.float32), ((0, 0), (pad, 0), (0, 0)))
        n = a.shape[1] // CHUNK
        return a.reshape(bsz, n, CHUNK, HGRN_HEADS, HGRN_HEAD_DIM).transpose(1, 0, 3, 2, 4)

    qc, kc, vc, lfc = to_chunks(q), to_chunks(k), to_chunks(i_val), to_chunks(log_f)
    causal = jnp.tril(jnp.ones((CHUNK, CHUNK), dtype=bool))

    def step(state, inp):
        qb, kb, vb, lfb = inp
        b = jnp.cumsum(lfb, axis=2)
        diff = b[:, :, :, None, :] - b[:, :, None, :, :]
        decay = jnp.exp(jnp.where(causal[:, :, None], diff, -jnp.inf))
        scores = jnp.einsum('bhtd,bhsd,bhtsd->bhts', qb, kb, decay)
        o = (jnp.einsum('bhts,bhsv->bhtv', scores, vb)
             + jnp.einsum('bhtd,bhdv->bhtv', qb * jnp.exp(b), state))
        b_last = b[:, :, -1:, :]
        state = (jnp.exp(b_last[:, :, 0, :])[..., None] * state
                 + jnp.einsum('bhsd,bhsv->bhdv', kb * jnp.exp(b_last - b), vb))
        return state, o

    s0 = jnp.zeros((bsz, HGRN_HEADS, HGRN_HEAD_DIM, HGRN_HEAD_DIM), jnp.float32)
    _, o = lax.scan(step, s0, (qc, kc, vc, lfc))
    n = o.shape[0]
    o = o.transpose(1, 0, 3, 2, 4).reshape(bsz, n * CHUNK, HGRN_WIDTH)[:, pad:]
    o = group_rmsnorm(o, norm_g, HGRN_HEADS) * jax.nn.silu(g_out.astype(jnp.float32))
    return o.astype(q.dtype)

def short_conv_mixer(b_gate, c_gate, v, conv_w, norm_g):
    u = c_gate * v
    y = lax.conv_general_dilated(
        u, conv_w[:, None, :].astype(u.dtype), window_strides=(1,),
        padding=[(CONV_K - 1, 0)], dimension_numbers=('NWC', 'WIO', 'NWC'),
        feature_group_count=CONV_WIDTH_CH)
    return group_rmsnorm(b_gate * y, norm_g, CONV_GROUPS)

def swiglu(x, w_gate, w_up, w_down):
    return (jax.nn.silu(x @ w_gate) * (x @ w_up)) @ w_down

def moe_ffn(xn, w_router, router_bias, w_gate_e, w_up_e, w_down_e, w_gate_s, w_up_s, w_down_s):
    bsz, t_len, d = xn.shape
    xt = xn.reshape(-1, d)
    n_tok = xt.shape[0]
    scores = jax.nn.sigmoid((xt @ w_router).astype(jnp.float32))
    _, top_idx = lax.top_k(scores + router_bias.astype(jnp.float32), TOP_K)
    top_s = jnp.take_along_axis(scores, top_idx, axis=-1)
    gates = top_s / jnp.sum(top_s, axis=-1, keepdims=True) * ROUTED_SCALE

    m = n_tok * TOP_K
    flat_e = top_idx.reshape(-1)
    flat_tok = jnp.repeat(jnp.arange(n_tok, dtype=jnp.int32), TOP_K)
    flat_g = gates.reshape(-1)
    order = jnp.argsort(flat_e, stable=True)
    e_sorted, tok_sorted, g_sorted = flat_e[order], flat_tok[order], flat_g[order]
    counts = jnp.bincount(flat_e, length=N_EXPERTS)
    starts = jnp.cumsum(counts) - counts
    padded = (counts + EXPERT_BLOCK - 1) // EXPERT_BLOCK * EXPERT_BLOCK
    pad_ends = jnp.cumsum(padded)
    pad_starts = pad_ends - padded
    dest = pad_starts[e_sorted] + jnp.arange(m, dtype=jnp.int32) - starts[e_sorted]
    n_blocks = -(-m // EXPERT_BLOCK) + N_EXPERTS
    rows = n_blocks * EXPERT_BLOCK
    src_tok = jnp.zeros((rows,), jnp.int32).at[dest].set(tok_sorted)
    row_gate = jnp.zeros((rows,), jnp.float32).at[dest].set(g_sorted)
    block_expert = jnp.minimum(
        jnp.searchsorted(pad_ends, jnp.arange(n_blocks) * EXPERT_BLOCK, side='right'),
        N_EXPERTS - 1)

    def expert_block(args):
        tok_idx, g, e = args
        xb = xt[tok_idx]
        yb = swiglu(xb, w_gate_e[e], w_up_e[e], w_down_e[e])
        return yb * g[:, None].astype(yb.dtype)

    y_rows = lax.map(expert_block, (src_tok.reshape(n_blocks, EXPERT_BLOCK),
                                    row_gate.reshape(n_blocks, EXPERT_BLOCK),
                                    block_expert))
    routed = jnp.zeros_like(xt).at[src_tok].add(y_rows.reshape(rows, d))
    shared = swiglu(xt, w_gate_s, w_up_s, w_down_s)
    return (routed + shared).reshape(bsz, t_len, d)

def setup_inputs(seed: int = 0) -> dict:
    key = jax.random.key(seed)
    ks = jax.random.split(key, 20)
    nrm = jax.random.normal
    return {
        'x': nrm(ks[0], (BATCH, SEQ, D_MODEL), jnp.float32),
        'meta_tokens': nrm(ks[1], (N_META, D_MODEL), jnp.float32),
        'norm_mix_g': 1.0 + 0.02 * nrm(ks[2], (DEPTH, D_MODEL), jnp.float32),
        'w_in': nrm(ks[3], (DEPTH, D_MODEL, IN_PROJ_WIDTH), jnp.float32) * D_MODEL ** -0.5,
        'lb_table': 0.5 * nrm(ks[4], (DEPTH + 1, HGRN_WIDTH), jnp.float32),
        'hgrn_norm_g': 1.0 + 0.02 * nrm(ks[5], (DEPTH, HGRN_WIDTH), jnp.float32),
        'conv_w': nrm(ks[6], (DEPTH, CONV_K, CONV_WIDTH_CH), jnp.float32) * CONV_K ** -0.5,
        'conv_norm_g': 1.0 + 0.02 * nrm(ks[7], (DEPTH, CONV_WIDTH_CH), jnp.float32),
        'w_out': nrm(ks[8], (DEPTH, MIX_WIDTH, D_MODEL), jnp.float32) * MIX_WIDTH ** -0.5,
        'norm_ffn_g': 1.0 + 0.02 * nrm(ks[9], (DEPTH, D_MODEL), jnp.float32),
        'w_router': nrm(ks[10], (DEPTH, D_MODEL, N_EXPERTS), jnp.float32) * D_MODEL ** -0.5,
        'router_bias': 0.01 * nrm(ks[11], (DEPTH, N_EXPERTS), jnp.float32),
        'w_gate_e': nrm(ks[12], (DEPTH, N_EXPERTS, D_MODEL, EXPERT_FF), jnp.float32) * D_MODEL ** -0.5,
        'w_up_e': nrm(ks[13], (DEPTH, N_EXPERTS, D_MODEL, EXPERT_FF), jnp.float32) * D_MODEL ** -0.5,
        'w_down_e': nrm(ks[14], (DEPTH, N_EXPERTS, EXPERT_FF, D_MODEL), jnp.float32) * EXPERT_FF ** -0.5,
        'w_gate_s': nrm(ks[15], (DEPTH, D_MODEL, SHARED_FF), jnp.float32) * D_MODEL ** -0.5,
        'w_up_s': nrm(ks[16], (DEPTH, D_MODEL, SHARED_FF), jnp.float32) * D_MODEL ** -0.5,
        'w_down_s': nrm(ks[17], (DEPTH, SHARED_FF, D_MODEL), jnp.float32) * SHARED_FF ** -0.5,
        'norm_final_g': 1.0 + 0.02 * nrm(ks[18], (D_MODEL,), jnp.float32),
    }

def reference(x, meta_tokens, norm_mix_g, w_in, lb_table, hgrn_norm_g, conv_w, conv_norm_g,
              w_out, norm_ffn_g, w_router, router_bias, w_gate_e, w_up_e, w_down_e,
              w_gate_s, w_up_s, w_down_s, norm_final_g):
    bsz = x.shape[0]
    meta = jnp.broadcast_to(meta_tokens.astype(x.dtype)[None], (bsz, N_META, D_MODEL))
    h = jnp.concatenate([meta, x], axis=1)
    lower_bounds = jnp.cumsum(jax.nn.softmax(lb_table.astype(jnp.float32), axis=0), axis=0)
    split_at = np.cumsum([HGRN_WIDTH] * 4 + [CONV_WIDTH_CH] * 3)[:-1].tolist()
    for l in range(DEPTH):
        xn = rmsnorm(h, norm_mix_g[l])
        proj = xn @ w_in[l]
        q, f_pre, i_val, g_out, b_gate, c_gate, v = jnp.split(proj, split_at, axis=-1)
        y_hgrn = hgrn2_mixer(q, f_pre, i_val, g_out, lower_bounds[l], hgrn_norm_g[l])
        y_conv = short_conv_mixer(b_gate, c_gate, v, conv_w[l], conv_norm_g[l])
        h = h + jnp.concatenate([y_hgrn, y_conv], axis=-1) @ w_out[l]
        h = h + moe_ffn(rmsnorm(h, norm_ffn_g[l]), w_router[l], router_bias[l],
                        w_gate_e[l], w_up_e[l], w_down_e[l],
                        w_gate_s[l], w_up_s[l], w_down_s[l])
    return rmsnorm(h, norm_final_g)[:, N_META:]


_drawn_inputs = setup_inputs


def setup_inputs(seed=0):
    import zlib

    import numpy as np

    out = dict(_drawn_inputs(seed))
    spreads = {}
    factors = {}
    for name, (base, spread) in spreads.items():
        noise = np.random.default_rng([zlib.crc32(name.encode()), seed]).standard_normal(out[name].shape)
        drawn = base * np.exp(spread * noise) if base else spread * noise
        out[name] = __import__('jax').numpy.asarray(drawn.astype(out[name].dtype))
    for name, factor in factors.items():
        out[name] = (out[name] * factor).astype(out[name].dtype)
    return out
```

```python
import concourse.bass as bass
from concourse import mybir
from contextlib import ExitStack

F32 = mybir.dt.float32
I32 = mybir.dt.int32
ALU = mybir.AluOpType
ACT = mybir.ActivationFunctionType

P = 128
D = 1024
KT = D // P
T = 1024
TT = T // P
META = 16
ALL = META + T
HEADS = 4
HW = HEADS * P
E_N = 64
TOPK = 8
FF = 256
EPS = 1e-6
LEVELS = [64, 32, 16, 8, 4, 2, 1]
Z_LOW = -80.0


class Chain:

    def __init__(self, engine, sem):
        self.engine, self.sem, self.base, self.k = engine, sem, 0, 0

    def __call__(self, ins):
        ins.then_inc(self.sem, 1)
        self.k += 1
        self.engine.wait_ge(self.sem, self.base + self.k)

    def enter(self, i, steps):
        self.start = self.base + self.k
        self.steps, self.base, self.k = steps, i * steps + self.start, 0

    def leave(self, turns):
        assert self.k == self.steps, (self.k, self.steps)
        self.base, self.k = self.start + turns * self.steps, 0


def bcast(ap, n):
    return ap.rearrange("p (a o) -> p a o", o=1).to_broadcast([ap.shape[0], ap.shape[1], n])


def setup(nc, ctx, ins, K):
    def sb(name, shape, dt=F32):
        return ctx.enter_context(nc.sbuf_tensor(name, shape, dt))
    K.ident = sb("ident", [P, P])
    K.ones = sb("ones", [P, P])
    K.xT = sb("xT", [P, KT, ALL])
    K.eps = sb("eps", [P, 1])


def phase_norm(nc, ins, K):
    x = ins["x"].rearrange("b (j p) n -> p (b j) n", p=P)
    with ExitStack() as ctx:
        def sb(name, shape, dt=F32):
            return ctx.enter_context(nc.sbuf_tensor(name, shape, dt))
        xt = sb("xt", [P, TT + 1, D])
        junk = [sb(f"junk{i}", [P, D]) for i in range(2)]
        ss = sb("ss", [P, TT + 1])
        rstd = sb("rstd", [P, TT + 1])
        xs = [sb(f"xs{i}", [P, D]) for i in range(2)]
        gmix = sb("gmix", [P, KT])
        pt = [ctx.enter_context(nc.psum_tensor(f"pt{i}", [P, 4, P], F32)) for i in range(4)]
        sem = lambda n: ctx.enter_context(nc.semaphore(n))
        s_x = [sem(f"x_in{j}") for j in range(TT + 1)]
        s_g = sem("gmix_in")
        s_c = sem("consts_set")
        s_c0 = sem("consts_cleared")
        s_ss = sem("squares_summed")
        s_ms = sem("mean_square")
        s_rt = sem("root")
        s_rs = sem("rstd_ready")
        s_xs = sem("x_scaled")
        s_tr = sem("x_transposed")
        s_ev = sem("xT_stored")
        block = ctx.enter_context(nc.Block())
        order = [TT] + list(range(TT))

        @block.sync
        def _(sp):
            sp.dma_start(xt[0:META, TT, :], ins["meta_tokens"]).then_inc(s_x[TT], 16)
            for j in range(TT):
                sp.dma_start(xt[:, j, :], x[:, j, :]).then_inc(s_x[j], 16)
            sp.dma_start(gmix[:, :], ins["norm_mix_g"].rearrange("l (p t) -> p (l t)", t=KT)).then_inc(s_g, 16)

        @block.gpsimd
        def _(pool):
            pool.memset(K.ident[:, :], 0.0).then_inc(s_c0, 1)
            pool.memset(K.ones[:, :], 1.0).then_inc(s_c, 1)
            pool.memset(K.eps[:, :], EPS).then_inc(s_c, 1)
            pool.memset(ss[:, :], 1.0).then_inc(s_c, 1)
            pool.wait_ge(s_c0, 1)
            pool.affine_select(out=K.ident[:, :], in_=K.ident[:, :], compare_op=ALU.not_equal, fill=1.0,
                               base=0, pattern=[[-1, P]], channel_multiplier=1).then_inc(s_c, 1)

        @block.scalar
        def _(act):
            act.wait_ge(s_c, 4)
            for c, j in enumerate(order):
                n = META if j == TT else P
                act.wait_ge(s_x[j], 16)
                if c >= 2:
                    act.wait_ge(s_ss, c - 1)
                act.activation(junk[c % 2][0:n, :], xt[0:n, j, :], ACT.Square,
                               accum_out=ss[0:n, j:j + 1]).then_inc(s_ss, 1)
            act.wait_ge(s_ss, TT + 1)
            act.activation(rstd[:, :], ss[:, :], ACT.Sqrt, bias=K.eps[:, 0:1], scale=1.0 / D).then_inc(s_rt, 1)
            act.wait_ge(s_rs, 1)
            for c, j in enumerate(order):
                n = META if j == TT else P
                if c >= 2:
                    act.wait_ge(s_tr, c - 1)
                act.activation(xs[c % 2][0:n, :], xt[0:n, j, :], ACT.Copy, scale=rstd[0:n, j:j + 1]).then_inc(s_xs, 1)

        @block.vector
        def _(dve):
            dve.wait_ge(s_rt, 1)
            dve.reciprocal(rstd[:, :], rstd[:, :]).then_inc(s_rs, 1)
            dve.wait_ge(s_g, 16)
            for c, j in enumerate(order):
                n = META if j == TT else P
                col = 0 if j == TT else META + j * P
                dve.wait_ge(s_tr, c + 1)
                for half in range(2):
                    last = dve.tensor_tensor(K.xT[:, 4 * half:4 * half + 4, col:col + n],
                                             pt[2 * (c % 2) + half][:, :, 0:n],
                                             bcast(gmix[:, 4 * half:4 * half + 4], n), ALU.mult)
                last.then_inc(s_ev, 1)

        @block.tensor
        def _(pe):
            pe.wait_ge(s_c, 4)
            for c, j in enumerate(order):
                n = META if j == TT else P
                pe.wait_ge(s_xs, c + 1)
                if c >= 2:
                    pe.wait_ge(s_ev, c - 1)
                rows = xs[c % 2][0:n, :].rearrange("p (k t) -> p t k", t=KT)
                for t in range(KT):
                    last = pe.transpose(pt[2 * (c % 2) + t // 4][:, t % 4, 0:n], rows[:, t, :], K.ident[0:n, 0:n])
                last.then_inc(s_tr, 1)


def phase_mix(nc, ctx_out, ins, K):
    w_in = ins["w_in"].rearrange("l (p t) n -> p (l t) n", t=KT)
    COL_Q, COL_F, COL_I, COL_GB, COL_CV = 0, HW, 2 * HW, 3 * HW, 5 * HW

    def keep(name, shape, dt=F32):
        return ctx_out.enter_context(nc.sbuf_tensor(name, shape, dt))
    K.QO = keep("QO", [P, HEADS, T])
    K.CV = keep("CV", [P, 2 * HEADS, ALL])
    K.GB = keep("GB", [P, 2 * HEADS, T])
    with ExitStack() as ctx:
        def sb(name, shape, dt=F32):
            return ctx.enter_context(nc.sbuf_tensor(name, shape, dt))

        def ps(name, shape):
            return ctx.enter_context(nc.psum_tensor(name, shape, F32))
        sem = lambda n: ctx.enter_context(nc.semaphore(n))
        FP = sb("FP", [P, HEADS, ALL])
        VT = sb("VT", [P, TT, HW])
        VM = sb("VM", [META, HW])
        wi = sb("wi", [P, KT, HW])
        spare = wi[:, :, :].rearrange("p t n -> p (t n)")
        wbuf = [sb(f"wbuf{i}", [P, KT, P])[:, :, :] for i in range(2)] + \
            [spare[:, D * i:D * i + D].rearrange("p (t n) -> p t n", t=KT) for i in range(2)]
        lbt = sb("lbt", [P, 2, HEADS])
        lbw = sb("lbw", [P, 5, HEADS])
        masks = sb("masks", [P, len(LEVELS), HEADS * 64], I32)
        restart = sb("restart", [P, HEADS, P])
        names = ("Z", "EZ", "SG", "KK", "BB", "QS", "QE", "DK", "KE", "KTS", "VC", "ST", "SCT")
        Z, EZ, SG, KK, BB, QS, QE, DK, KE, KTS, VC, ST, SCT = (sb(n, [P, HEADS, P]) for n in names)
        FV, LF = Z, EZ
        DD, WW = ([spare[:, 2 * D + HW * (2 * k + i):2 * D + HW * (2 * k + i + 1)].rearrange("p (h t) -> p h t", h=HEADS)
                   for i in range(2)] for k in range(2))
        blast = sb("blast", [P, HEADS])
        oml, lb = lbw[:, 3, :], lbw[:, 2, :]
        bank = [ps(f"bank{i}", [P, 512]) for i in range(2)]
        bankm = ps("bankm", [P, 512])
        sc = [ps(f"sc{i}", [P, HEADS * P]) for i in range(2)]
        kt_ps, o_ps, st_ps = ps("kt_ps", [P, HEADS, P]), ps("o_ps", [P, HEADS, P]), ps("st_ps", [P, HEADS, P])

        s_wi, s_lb = sem("wi_in"), sem("lb_in")
        s_w = [sem(f"w_in{i}") for i in range(4)]
        s_wfree = [sem(f"w_free{i}") for i in range(4)]
        s_mm, s_out = sem("projected"), sem("projection_stored")
        s_cst0, s_cst = sem("masks_cleared"), sem("masks_set")
        s_d, s_a, s_t = sem("dve_steps"), sem("act_steps"), sem("turns")
        s_lbx, s_lbe = sem("lb_shifted"), sem("lb_exp")
        s_ez, s_zz, s_fv, s_lf = sem("exp_z"), sem("z_held"), sem("f_ready"), sem("log_f")
        s_cp = sem("chunk_copied")
        s_dd, s_ww0, s_ww, s_s, s_p = sem("decay_logs"), sem("decays"), sem("factors"), sem("scores"), sem("scores_kept")
        s_de, s_ee = sem("end_logs"), sem("end_decays")
        s_ke, s_kt, s_kts = sem("k_end"), sem("k_end_turned"), sem("k_end_stored")
        s_kq = sem("kq_ready")
        s_o, s_oev, s_st, s_stk = sem("o_ready"), sem("o_stored"), sem("state_term"), sem("state_kept")
        block = ctx.enter_context(nc.Block())
        L1, L2 = HEADS, TT
        V_GROUPS = TT + 1

        @block.sync
        def _(sp):
            sp.dma_start(wi[:, :, :], w_in[:, :, COL_I:COL_I + HW]).then_inc(s_wi, 16)
            sp.dma_start(lbt[:, :, :], ins["lb_table"].rearrange("l (h p) -> p l h", p=P),
                         allow_slow_non_contiguous=True).then_inc(s_lb, 16)
            with sp.Fori(0, L1) as i:
                for s, col in ((0, COL_F), (1, COL_Q)):
                    sp.wait_ge(s_wfree[s], i + 1)
                    sp.sem_inc(s_t, 1)
                    sp.dma_start(wbuf[s][:, :, :], w_in[:, :, bass.ds(i * P + col, P)]).then_inc(s_w[s], 16)
            with sp.Fori(0, L2) as i:
                for s, col in ((2, COL_CV), (3, COL_GB)):
                    sp.wait_ge(s_wfree[s], i + 1)
                    sp.sem_inc(s_t, 1)
                    sp.dma_start(wbuf[s][:, :, :], w_in[:, :, bass.ds(i * P + col, P)]).then_inc(s_w[s], 16)

        @block.gpsimd
        def _(pool):
            pool.memset(restart[:, :, :], 1.0).then_inc(s_cst0, 1)
            pool.memset(masks[:, :, :], 1).then_inc(s_cst0, 1)
            pool.wait_ge(s_cst0, 2)
            pool.memset(restart[:, :, 0:1], 0.0).then_inc(s_cst, 1)
            for l, half in enumerate(LEVELS):
                n = 64 // half
                m = masks[:, l, :].rearrange("p (h b r) -> p h b r", h=HEADS, r=half)
                pool.affine_select(out=m, in_=m, compare_op=ALU.is_ge, fill=0.0, base=0,
                                   pattern=[[0, HEADS], [-2 * half, n], [0, half]], channel_multiplier=1).then_inc(s_cst0, 1)
                pool.wait_ge(s_cst0, 3 + l)
                pool.affine_select(out=m, in_=m, compare_op=ALU.is_ge, fill=0.0, base=half - 1,
                                   pattern=[[0, HEADS], [2 * half, n], [0, half]], channel_multiplier=-1).then_inc(s_cst, 1)

        @block.tensor
        def _(pe):
            done = [0]

            def group(out, n, lhs, rhs):
                for t in range(KT):
                    last = pe.matmul(out, lhs(t), rhs(t), start=(t == 0), stop=(t == KT - 1))
                last.then_inc(s_mm, 1)

            pe.wait_ge(s_wi, 16)
            for j in range(V_GROUPS):
                if j >= 2:
                    pe.wait_ge(s_out, j - 1)
                n, col = (P, META + j * P) if j < TT else (META, 0)
                group(bank[j % 2][0:n, :], n, lambda t: K.xT[:, t, col:col + n], lambda t: wi[:, t, :])

            def project(s, b, base):
                cols = slice(META + 512 * b, META + 512 * b + 512)
                pe.wait_ge(s_out, base - 1)
                group(bank[b][:, :], 512, lambda t: wbuf[s][:, t, :], lambda t: K.xT[:, t, cols])

            def project_meta(s, base):
                pe.wait_ge(s_out, base - 1)
                group(bankm[:, 0:META], META, lambda t: wbuf[s][:, t, :], lambda t: K.xT[:, t, 0:META])

            pe.wait_ge(s_mm, V_GROUPS)
            for s in range(4):
                pe.sem_inc(s_wfree[s], 1)
            with pe.Fori(0, L1) as i:
                base = i * 5 + V_GROUPS
                pe.wait_ge(s_w[0], i * 16 + 16)
                project_meta(0, base)
                project(0, 0, base + 1)
                project(0, 1, base + 2)
                pe.sem_inc(s_t, 1)
                pe.wait_ge(s_mm, base + 3)
                pe.sem_inc(s_wfree[0], 1)
                pe.wait_ge(s_w[1], i * 16 + 16)
                project(1, 0, base + 3)
                project(1, 1, base + 4)
                pe.wait_ge(s_mm, base + 5)
                pe.sem_inc(s_wfree[1], 1)

            pe.wait_ge(s_ke, 1)
            for h in range(HEADS):
                last = pe.transpose(kt_ps[0:META, h, :], KE[:, h, 0:META], K.ident[:, :])
            last.then_inc(s_kt, 1)
            pe.wait_ge(s_kts, 1)
            for h in range(HEADS):
                last = pe.matmul(st_ps[:, h, :], KTS[0:META, h, :], VM[:, h * P:(h + 1) * P], start=True, stop=True)
            last.then_inc(s_st, 1)

            with pe.Fori(0, L2) as i:
                base = i * 5 + V_GROUPS + 5 * L1
                NS = len(LEVELS) + 1

                def level(l):
                    if l == 0:
                        pe.wait_ge(s_kq, i + 1)
                        pe.wait_ge(s_p, i * NS + 1)
                        for h in range(HEADS):
                            last = pe.matmul(sc[0][:, h * P:(h + 1) * P], KK[:, h, :], QS[:, h, :], start=True, stop=True)
                    else:
                        half = LEVELS[l - 1]
                        pe.wait_ge(s_ww, i * len(LEVELS) + l)
                        pe.wait_ge(s_p, i * NS + l)
                        W = WW[l % 2]
                        for h in range(HEADS):
                            late = W[:, h, :].rearrange("p (b z r) -> p b z r", z=2, r=half)[:, :, 1, :]
                            last = pe.matmul(sc[l % 2][:, h * 64:(h + 1) * 64], W[:, h, :], late, start=True, stop=True)
                    last.then_inc(s_s, 1)

                pe.wait_ge(s_w[2], i * 16 + 16)
                project_meta(2, base)
                project(2, 0, base + 1)
                level(0)
                level(1)
                project(2, 1, base + 2)
                pe.wait_ge(s_mm, base + 3)
                pe.sem_inc(s_wfree[2], 1)
                level(2)
                level(3)
                pe.wait_ge(s_w[3], i * 16 + 16)
                project(3, 0, base + 3)
                level(4)
                level(5)
                level(6)
                pe.wait_ge(s_ke, i + 2)
                for h in range(HEADS):
                    last = pe.transpose(kt_ps[:, h, :], KE[:, h, :], K.ident[:, :])
                last.then_inc(s_kt, 1)
                project(3, 1, base + 4)
                pe.wait_ge(s_mm, base + 5)
                pe.sem_inc(s_wfree[3], 1)
                level(7)
                pe.wait_ge(s_kts, i + 2)
                for h in range(HEADS):
                    last = pe.matmul(st_ps[:, h, :], KTS[:, h, :], VC[:, h, :], start=True, stop=True)
                last.then_inc(s_st, 1)
                pe.wait_ge(s_p, i * NS + NS + 1)
                pe.wait_ge(s_stk, i + 1)
                for h in range(HEADS):
                    pe.matmul(o_ps[:, h, :], VC[:, h, :], SCT[:, h, :], start=True, stop=False)
                    last = pe.matmul(o_ps[:, h, :], ST[:, h, :], QE[:, h, :], start=False, stop=True)
                last.then_inc(s_o, 1)

        @block.scalar
        def _(act):
            for j in range(V_GROUPS):
                act.wait_ge(s_mm, j + 1)
                if j < TT:
                    act.copy(VT[:, j, :], bank[j % 2][:, :]).then_inc(s_out, 1)
                else:
                    act.copy(VM[:, :], bank[j % 2][0:META, :]).then_inc(s_out, 1)
            act.wait_ge(s_lbx, 1)
            act.activation(lbw[:, 0:2, :], lbw[:, 0:2, :], ACT.Exp).then_inc(s_lbe, 1)

            def store(base, k, out, src):
                act.wait_ge(s_mm, base + k)
                act.sem_inc(s_t, 1)
                act.copy(out, src).then_inc(s_out, 1)

            with act.Fori(0, L1) as i:
                base = i * 5 + V_GROUPS
                store(base, 1, FP[:, bass.ds(i, 1), 0:META], bankm[:, 0:META])
                store(base, 2, FP[:, bass.ds(i, 1), META:META + 512], bank[0][:, :])
                store(base, 3, FP[:, bass.ds(i, 1), META + 512:ALL], bank[1][:, :])
                store(base, 4, K.QO[:, bass.ds(i, 1), 0:512], bank[0][:, :])
                store(base, 5, K.QO[:, bass.ds(i, 1), 512:T], bank[1][:, :])

            def logs(n, turn):
                act.wait_ge(s_zz, turn)
                act.activation(EZ[:, :, 0:n], Z[:, :, 0:n], ACT.Exp, scale=-1.0).then_inc(s_ez, 1)
                act.wait_ge(s_fv, turn)
                act.activation(LF[:, :, 0:n], FV[:, :, 0:n], ACT.Ln).then_inc(s_lf, 1)

            logs(META, 1)
            act.wait_ge(s_de, 1)
            act.activation(DK[:, :, 0:META], DK[:, :, 0:META], ACT.Exp).then_inc(s_ee, 1)
            act.wait_ge(s_kt, 1)
            act.copy(KTS[0:META, :, :], kt_ps[0:META, :, :]).then_inc(s_kts, 1)

            with act.Fori(0, L2) as i:
                base = i * 5 + V_GROUPS + 5 * L1
                act.wait_ge(s_oev, i + 1)
                act.sem_inc(s_t, 1)
                act.copy(QS[:, :, :], K.QO[:, :, bass.ds(i * P, P)]).then_inc(s_cp, 1)
                act.copy(VC[:, :, :].rearrange("p h v -> p (h v)"), VT[:, bass.ds(i, 1), :]).then_inc(s_cp, 1)
                logs(P, i + 2)
                store(base, 1, K.CV[:, bass.ds(i, 1), 0:META], bankm[:, 0:META])
                act.wait_ge(s_de, i + 2)
                act.activation(DK[:, :, :], DK[:, :, :], ACT.Exp)
                act.activation(QE[:, :, :], BB[:, :, :], ACT.Exp).then_inc(s_ee, 1)

                def decays(l):
                    act.wait_ge(s_dd, i * len(LEVELS) + l + 1)
                    if l >= 2:
                        act.wait_ge(s_s, i * (len(LEVELS) + 1) + l)
                    act.activation(WW[(l + 1) % 2][:, :, :], DD[l % 2][:, :, :], ACT.Exp).then_inc(s_ww0, 1)

                decays(0)
                store(base, 2, K.CV[:, bass.ds(i, 1), META:META + 512], bank[0][:, :])
                decays(1)
                decays(2)
                store(base, 3, K.CV[:, bass.ds(i, 1), META + 512:ALL], bank[1][:, :])
                decays(3)
                decays(4)
                store(base, 4, K.GB[:, bass.ds(i, 1), 0:512], bank[0][:, :])
                decays(5)
                decays(6)
                act.wait_ge(s_kt, i + 2)
                act.copy(KTS[:, :, :], kt_ps[:, :, :]).then_inc(s_kts, 1)
                store(base, 5, K.GB[:, bass.ds(i, 1), 512:T], bank[1][:, :])
                act.wait_ge(s_o, i + 1)
                act.sem_inc(s_t, 1)
                act.copy(K.QO[:, :, bass.ds(i * P, P)], o_ps[:, :, :]).then_inc(s_oev, 1)

        @block.vector
        def _(dve):
            step = Chain(dve, s_d)
            tt, ts, stt = nc.vector.tensor_tensor, nc.vector.tensor_scalar, nc.vector.scalar_tensor_tensor
            dve.wait_ge(s_lb, 16)
            step(tt(lbw[:, 4, :], lbt[:, 0, :], lbt[:, 1, :], ALU.max))
            tt(lbw[:, 0, :], lbt[:, 0, :], lbw[:, 4, :], ALU.subtract)
            tt(lbw[:, 1, :], lbt[:, 1, :], lbw[:, 4, :], ALU.subtract).then_inc(s_lbx, 1)
            dve.wait_ge(s_lbe, 1)
            step(tt(lbw[:, 4, :], lbw[:, 0, :], lbw[:, 1, :], ALU.add))
            step(nc.vector.reciprocal(lbw[:, 4, :], lbw[:, 4, :]))
            step(tt(lbw[:, 2, :], lbw[:, 0, :], lbw[:, 4, :], ALU.mult))
            step(ts(lbw[:, 3, :], lbw[:, 2, :], -1.0, 1.0, ALU.mult, ALU.add))

            def gates(n, src, turn):
                step(ts(Z[:, :, 0:n], src, Z_LOW, None, ALU.max))
                dve.sem_inc(s_zz, 1)
                dve.wait_ge(s_ez, turn)
                step(ts(SG[:, :, 0:n], EZ[:, :, 0:n], 1.0, None, ALU.add))
                step(nc.vector.reciprocal(SG[:, :, 0:n], SG[:, :, 0:n]))
                tt(FV[:, :, 0:n], SG[:, :, 0:n], bcast(oml, n), ALU.mult)
                step(tt(KK[:, :, 0:n], EZ[:, :, 0:n], SG[:, :, 0:n], ALU.mult))
                tt(FV[:, :, 0:n], FV[:, :, 0:n], bcast(lb, n), ALU.add).then_inc(s_fv, 1)
                step(tt(KK[:, :, 0:n], KK[:, :, 0:n], bcast(oml, n), ALU.mult))
                dve.wait_ge(s_lf, turn)

            def end_log(n):
                step(tt(DK[:, :, 0:n], BB[:, :, n - 1:n].to_broadcast([P, HEADS, n]), BB[:, :, 0:n], ALU.subtract))
                dve.sem_inc(s_de, 1)

            dve.wait_ge(s_out, V_GROUPS + 5 * L1)
            dve.wait_ge(s_cst, 1 + len(LEVELS))
            gates(META, FP[:, :, 0:META], 1)
            for h in range(HEADS):
                last = nc.vector.tensor_tensor_scan(BB[:, h, 0:META], restart[:, h, 0:META], LF[:, h, 0:META], 0.0,
                                                    ALU.mult, ALU.add)
            step(last)
            end_log(META)
            dve.wait_ge(s_ee, 1)
            step(tt(KE[:, :, 0:META], KK[:, :, 0:META], DK[:, :, 0:META], ALU.mult))
            dve.sem_inc(s_ke, 1)
            dve.wait_ge(s_st, 1)
            step(nc.vector.tensor_copy(ST[:, :, :], st_ps[:, :, :]))
            dve.sem_inc(s_stk, 1)
            dve.sem_inc(s_oev, 1)
            dve.sem_inc(s_p, 1)

            def halves(x, half):
                v = x.rearrange("p h (b z r) -> p (h b) z r", z=2, r=half)
                return v[:, :, 0, :], v[:, :, 1, :]

            with dve.Fori(0, L2) as i:
                step.enter(i, 18)
                NL = len(LEVELS)
                dve.wait_ge(s_oev, i + 1)
                dve.sem_inc(s_t, 1)
                gates(P, FP[:, :, bass.ds(i * P + META, P)], i + 2)
                step(nc.vector.tensor_tensor_scan(BB[:, :, :].rearrange("p h t -> p (h t)"),
                                                  restart[:, :, :].rearrange("p h t -> p (h t)"),
                                                  LF[:, :, :].rearrange("p h t -> p (h t)"), 0.0, ALU.mult, ALU.add))
                dve.wait_ge(s_cp, i * 2 + 2)
                dve.sem_inc(s_kq, 1)
                end_log(P)

                def logs(l):
                    half = LEVELS[l]
                    n = HEADS * 64 // half
                    (b0, b1), (d0, d1) = halves(BB[:, :, :], half), halves(DD[l % 2], half)
                    ref = b0[:, :, half - 1:half].to_broadcast([P, n, half])
                    tt(d0, ref, b0, ALU.subtract)
                    tt(d1, b1, ref, ALU.subtract).then_inc(s_dd, 1)

                def factors(l):
                    half = LEVELS[l]
                    w0, w1 = halves(WW[(l + 1) % 2], half)
                    dve.wait_ge(s_ww0, i * NL + l + 1)
                    tt(w0, w0, halves(KK[:, :, :], half)[0], ALU.mult)
                    tt(w1, w1, halves(QS[:, :, :], half)[1], ALU.mult).then_inc(s_ww, 1)

                def keep_scores(l):
                    half = LEVELS[l]
                    dve.wait_ge(s_s, i * (NL + 1) + l + 2)
                    dve.sem_inc(s_t, 1)
                    _, late = halves(SCT[:, :, :], half)
                    bank_v = sc[(l + 1) % 2][:, 0:HEADS * 64].rearrange("p (b r) -> p b r", r=half)
                    mask_v = masks[:, l, :].rearrange("p (b r) -> p b r", r=half)
                    step(nc.vector.copy_predicated(late, mask_v, bank_v))
                    dve.sem_inc(s_p, 1)

                logs(0)
                logs(1)
                dve.wait_ge(s_s, i * (NL + 1) + 1)
                step(tt(SCT[:, :, :], sc[0][:, :].rearrange("p (h t) -> p h t", h=HEADS),
                        K.ident[:, :].rearrange("p (o t) -> p o t", o=1).to_broadcast([P, HEADS, P]), ALU.mult))
                dve.sem_inc(s_p, 1)
                dve.wait_ge(s_ee, i + 2)
                step(nc.vector.tensor_copy(blast[:, :].rearrange("p (h o) -> p h o", o=1), QE[:, :, P - 1:P]))
                tt(QE[:, :, :], QE[:, :, :], QS[:, :, :], ALU.mult)
                step(tt(KE[:, :, :], KK[:, :, :], DK[:, :, :], ALU.mult))
                dve.sem_inc(s_ke, 1)
                for l in range(NL):
                    factors(l)
                    if l + 2 < NL:
                        logs(l + 2)
                    if l >= 1:
                        keep_scores(l - 1)
                keep_scores(NL - 1)
                dve.wait_ge(s_st, i + 2)
                dve.wait_ge(s_o, i + 1)
                for h in range(HEADS):
                    last = stt(ST[:, h, :], ST[:, h, :], blast[:, h:h + 1], st_ps[:, h, :], ALU.mult, ALU.add)
                step(last)
                dve.sem_inc(s_stk, 1)
            step.leave(L2)
CAP = 160
CAP1 = CAP - P
ITEMS = E_N + (T * TOPK) // CAP + 3
MORE = -(-T // CAP) - 1
ROUTED_SCALE = 2.5


def phase_out(nc, ins, K, h2_d, xn2_d):
    w_out = ins["w_out"].rearrange("l (c p) n -> p (l c) n", p=P)
    x = ins["x"].rearrange("b (j p) n -> p (b j) n", p=P)
    G, B = K.GB[:, 0:HEADS, :], K.GB[:, HEADS:2 * HEADS, :]
    C, V = K.CV[:, 0:HEADS, :], K.CV[:, HEADS:2 * HEADS, :]
    with ExitStack() as ctx:
        def sb(name, shape, dt=F32):
            return ctx.enter_context(nc.sbuf_tensor(name, shape, dt))

        def ps(name, shape):
            return ctx.enter_context(nc.psum_tensor(name, shape, F32))
        sem = lambda n: ctx.enter_context(nc.semaphore(n))
        wo = sb("wo", [P, KT, D])
        gffn = sb("gffn", [P, D])
        cw = sb("cw", [P, 3, HEADS])
        ng = sb("ng", [P, 2, HEADS])
        H = [sb(f"H{i}", [P, D]) for i in range(2)]
        X2 = [sb(f"X2{i}", [P, D]) for i in range(2)]
        sg = sb("sg", [P, D])
        zrow = sb("zrow", [P, D])
        Y = [sb(f"Y{i}", [P, 2 * HEADS, P]) for i in range(2)]
        SQ = sb("SQ", [P, 2 * HEADS, P])
        RT = sb("RT", [P, 2 * HEADS, P])
        taps = [sb(f"tap{i}", [P, HEADS, P]) for i in range(3)]
        sh = sb("sh", [P, 2 * TT])
        junk = sb("junk2", [P, D])
        ms = [ps(f"ms{i}", [P, HEADS, P]) for i in range(2)]
        op = [ps(f"op{i}", [P, 512]) for i in range(2)]
        tr = [ps(f"tr{i}", [P, 4, P]) for i in range(2)]
        s_wo, s_c, s_z = sem("wo_in"), sem("vectors_in"), sem("zero_row")
        s_h = [sem(f"h_in{i}") for i in range(2)]
        s_sig, s_gate = sem("sigmoids"), sem("gates_on")
        s_pool, s_u, s_conv = sem("pool_steps"), sem("u_ready"), sem("conv_ready")
        s_yc, s_sq, s_ms, s_rt = sem("conv_gated"), sem("squares"), sem("mean_squares"), sem("roots")
        s_y, s_op, s_h2 = sem("mixed"), sem("out_projected"), sem("residual_added")
        s_s2, s_r2, s_x2 = sem("squares_summed2"), sem("root2"), sem("xn2_ready")
        s_t2, s_e2, s_st = sem("xn2_turned"), sem("xn2_kept"), sem("rows_written")
        s_d = sem("dve_steps2")
        block = ctx.enter_context(nc.Block())
        h2v = h2_d[0:T, :].rearrange("(j p) n -> p j n", p=P)
        xn2v = xn2_d[0:T, :].rearrange("(j p) n -> p j n", p=P)

        @block.sync
        def _(sp):
            for k in range(2):
                sp.dma_start(H[k][:, :], x[:, k, :]).then_inc(s_h[k], 16)
            sp.dma_start(cw[:, :, :].rearrange("p k h -> p (k h)"), ins["conv_w"].rearrange("l k (h p) -> p (l k h)", p=P),
                         allow_slow_non_contiguous=True).then_inc(s_c, 16)
            for k, name in enumerate(("hgrn_norm_g", "conv_norm_g")):
                sp.dma_start(ng[:, k, :], ins[name].rearrange("l (h p) -> p (l h)", p=P),
                             allow_slow_non_contiguous=True).then_inc(s_c, 16)
            sp.dma_start(wo[:, :, :], w_out).then_inc(s_wo, 16)
            sp.dma_start(gffn[:, :], ins["norm_ffn_g"].to_broadcast([P, D])).then_inc(s_c, 16)
            sp.wait_ge(s_z, 1)
            for base in range(T, T + CAP, P):
                n = min(P, T + CAP - base)
                sp.dma_start(xn2_d[base:base + n, :], zrow[0:n, :]).then_inc(s_st, 16)
                sp.dma_start(h2_d[base:base + n, :], zrow[0:n, :]).then_inc(s_st, 16)
            for j in range(TT):
                sp.wait_ge(s_x2, j + 1)
                sp.dma_start(h2v[:, j, :], H[j % 2][:, :]).then_inc(s_st, 16)
                sp.dma_start(xn2v[:, j, :], X2[j % 2][:, :]).then_inc(s_st, 16)
                if j + 2 < TT:
                    sp.wait_ge(s_st, 16 * (4 + 2 * (j + 1)))
                    sp.dma_start(H[j % 2][:, :], x[:, j + 2, :]).then_inc(s_h[j % 2], 16)
            sp.wait_ge(s_st, 16 * (4 + 2 * TT))

        @block.gpsimd
        def _(pool):
            pool.memset(zrow[:, :], 0.0).then_inc(s_z, 1)
            pool.wait_ge(s_c, 64)
            n = 0
            last = None
            for a in range(META - 2, ALL, 257):
                u = slice(a, min(a + 257, ALL))
                last = pool.tensor_tensor(C[:, :, u], C[:, :, u], V[:, :, u], ALU.mult)
            last.then_inc(s_pool, 1)
            n += 1
            for j in range(TT):
                pool.wait_ge(s_pool, n)
                if j:
                    pool.wait_ge(s_yc, j)
                for k in range(3):
                    u = C[:, :, META - 2 + k + j * P:META - 2 + k + j * P + P]
                    pool.tensor_tensor(taps[k][:, :, :], u, bcast(cw[:, k, :], P), ALU.mult).then_inc(s_pool, 1)
                n += 3
                pool.wait_ge(s_pool, n)
                pool.tensor_tensor(taps[0][:, :, :], taps[0][:, :, :], taps[1][:, :, :], ALU.add).then_inc(s_pool, 1)
                n += 1
                pool.wait_ge(s_pool, n)
                pool.tensor_tensor(taps[2][:, :, :], taps[0][:, :, :], taps[2][:, :, :], ALU.add).then_inc(s_conv, 1)

        @block.tensor
        def _(pe):
            def means(j):
                pe.wait_ge(s_sq, 2 * (j + 1))
                if j:
                    pe.wait_ge(s_rt, j)
                for k in range(2):
                    last = pe.matmul(ms[k][:, :, :].rearrange("p h t -> p (h t)"), K.ones[:, :],
                                     SQ[:, HEADS * k:HEADS * k + HEADS, :].rearrange("p h t -> p (h t)"), start=True, stop=True)
                last.then_inc(s_ms, 1)

            def turn(j):
                pe.wait_ge(s_x2, j + 1)
                if j:
                    pe.wait_ge(s_e2, j)
                rows = X2[j % 2][:, :].rearrange("p (k t) -> p t k", t=KT)
                for t in range(KT):
                    last = pe.transpose(tr[t // 4][:, t % 4, :], rows[:, t, :], K.ident[:, :])
                last.then_inc(s_t2, 1)

            means(0)
            pe.wait_ge(s_wo, 16)
            for j in range(TT):
                if j + 1 < TT:
                    means(j + 1)
                pe.wait_ge(s_y, j + 1)
                if j:
                    pe.wait_ge(s_h2, j)
                for half in range(2):
                    for c in range(KT):
                        last = pe.matmul(op[half][:, :], Y[j % 2][:, c, :], wo[:, c, 512 * half:512 * half + 512],
                                         start=(c == 0), stop=(c == KT - 1))
                last.then_inc(s_op, 1)
                if j:
                    turn(j - 1)
            turn(TT - 1)

        @block.scalar
        def _(act):
            for h in range(HEADS):
                if h:
                    act.wait_ge(s_gate, h)
                act.activation(sg[:, :], G[:, h, :], ACT.Sigmoid).then_inc(s_sig, 1)

            def squares(j):
                if j:
                    act.wait_ge(s_ms, j)
                act.activation(SQ[:, 0:HEADS, :], K.QO[:, :, j * P:j * P + P], ACT.Square).then_inc(s_sq, 1)
                act.wait_ge(s_yc, j + 1)
                act.activation(SQ[:, HEADS:2 * HEADS, :], Y[j % 2][:, HEADS:2 * HEADS, :], ACT.Square).then_inc(s_sq, 1)

            def roots(j):
                act.wait_ge(s_ms, j + 1)
                if j:
                    act.wait_ge(s_y, j)
                for k in range(2):
                    last = act.activation(RT[:, HEADS * k:HEADS * k + HEADS, :], ms[k][:, :, :], ACT.Sqrt,
                                          bias=K.eps[:, 0:1], scale=1.0 / P)
                last.then_inc(s_rt, 1)

            squares(0)
            roots(0)
            for j in range(TT):
                if j + 1 < TT:
                    squares(j + 1)
                    roots(j + 1)
                if j:
                    act.wait_ge(s_t2, j)
                    for k in range(2):
                        last = act.copy(K.xT[:, 4 * k:4 * k + 4, (j - 1) * P:j * P], tr[k][:, :, :])
                    last.then_inc(s_e2, 1)
                act.wait_ge(s_h2, j + 1)
                if j:
                    act.wait_ge(s_s2, j)
                act.activation(junk[:, :], H[j % 2][:, :], ACT.Square, accum_out=sh[:, j:j + 1]).then_inc(s_s2, 1)
                act.wait_ge(s_s2, j + 1)
                act.activation(sh[:, TT + j:TT + j + 1], sh[:, j:j + 1], ACT.Sqrt, bias=K.eps[:, 0:1], scale=1.0 / D).then_inc(s_r2, 1)
            act.wait_ge(s_t2, TT)
            for k in range(2):
                last = act.copy(K.xT[:, 4 * k:4 * k + 4, (TT - 1) * P:T], tr[k][:, :, :])
            last.then_inc(s_e2, 1)

        @block.vector
        def _(dve):
            step = Chain(dve, s_d)
            tt, stt = nc.vector.tensor_tensor, nc.vector.scalar_tensor_tensor
            dve.wait_ge(s_c, 64)
            for h in range(HEADS):
                dve.wait_ge(s_sig, h + 1)
                stt(G[:, h, :], G[:, h, :], ng[:, 0, h:h + 1], sg[:, :], ALU.mult, ALU.mult).then_inc(s_gate, 1)

            def conv_gate(j):
                dve.wait_ge(s_conv, j + 1)
                if j >= 2:
                    dve.wait_ge(s_op, j - 1)
                tt(Y[j % 2][:, HEADS:2 * HEADS, :], taps[2][:, :, :], B[:, :, j * P:j * P + P], ALU.mult).then_inc(s_yc, 1)

            def mix(j):
                dve.wait_ge(s_rt, j + 1)
                tt_y = Y[j % 2]
                nc.vector.reciprocal(RT[:, 0:HEADS, :], RT[:, 0:HEADS, :])
                step(nc.vector.reciprocal(RT[:, HEADS:, :], RT[:, HEADS:, :]))
                tt(tt_y[:, 0:HEADS, :], K.QO[:, :, j * P:j * P + P], RT[:, 0:HEADS, :], ALU.mult)
                step(tt(tt_y[:, HEADS:, :], tt_y[:, HEADS:, :], RT[:, HEADS:, :], ALU.mult))
                tt(tt_y[:, 0:HEADS, :], tt_y[:, 0:HEADS, :], G[:, :, j * P:j * P + P], ALU.mult)
                tt(tt_y[:, HEADS:, :], tt_y[:, HEADS:, :], bcast(ng[:, 1, :], P), ALU.mult).then_inc(s_y, 1)

            conv_gate(0)
            dve.wait_ge(s_gate, HEADS)
            mix(0)
            for j in range(TT):
                if j + 1 < TT:
                    conv_gate(j + 1)
                    mix(j + 1)
                dve.wait_ge(s_op, j + 1)
                dve.wait_ge(s_h[j % 2], 16 * (j // 2 + 1))
                for half in range(2):
                    cols = slice(512 * half, 512 * half + 512)
                    last = tt(H[j % 2][:, cols], H[j % 2][:, cols], op[half][:, :], ALU.add)
                last.then_inc(s_h2, 1)
                dve.wait_ge(s_r2, j + 1)
                step(nc.vector.reciprocal(sh[:, TT + j:TT + j + 1], sh[:, TT + j:TT + j + 1]))
                if j >= 2:
                    dve.wait_ge(s_t2, j - 1)
                    dve.wait_ge(s_st, 16 * (4 + 2 * (j - 1)))
                stt(X2[j % 2][:, :], H[j % 2][:, :], sh[:, TT + j:TT + j + 1], gffn[:, :], ALU.mult, ALU.mult).then_inc(s_x2, 1)


def phase_route(nc, ctx_out, ins, K, h2_d, acc_d, tbl_d):
    def keep(name, shape, dt=F32):
        return ctx_out.enter_context(nc.sbuf_tensor(name, shape, dt))
    K.idx = [keep("idx0", [P, ITEMS], I32), keep("idx1", [CAP1, ITEMS], I32)]
    K.gate = [keep("gate0", [P, ITEMS]), keep("gate1", [CAP1, ITEMS])]
    K.expert = keep("expert", [1, ITEMS], I32)
    K.pairs = keep("pairs", [1, 1], I32)
    NE = TT * E_N
    with ExitStack() as ctx:
        def sb(name, shape, dt=F32):
            return ctx.enter_context(nc.sbuf_tensor(name, shape, dt))

        def ps(name, shape):
            return ctx.enter_context(nc.psum_tensor(name, shape, F32))
        sem = lambda n: ctx.enter_context(nc.semaphore(n))
        wr = sb("wr", [P, KT, E_N])
        bias = sb("bias", [P, E_N])
        wgs, wus = sb("wgs", [P, KT, FF]), sb("wus", [P, KT, FF])
        wds = sb("wds", [P, 2, D])
        SC, BI, RE, MK, GT, SL, T1 = (sb(n, [P, TT, E_N]) for n in ("SC", "BI", "RE", "MK", "GT", "SL", "T1"))
        MS = sb("MS", [P, TT, E_N])
        m8 = sb("m8", [P, TT, TOPK])
        s8 = sb("s8", [P, TT, TOPK])
        si = sb("si", [P, TT * TOPK], I32)
        junk = sb("junk3", [P, E_N])
        pay = sb("pay", [P, TT, TOPK, 2])
        gs = sb("gs", [P, TT])
        before = sb("before", [P, P])
        cnt, ext, inc, b0, ba = (sb(n, [P, E_N]) for n in ("cnt", "ext", "inc", "b0", "ba"))
        e0 = sb("e0", [P, E_N])
        zero = sb("zero", [P, E_N])
        pidx = sb("pidx", [P, 1])
        tex = sb("tex", [P, 1])
        exrow = sb("exrow", [1, ITEMS])
        twos = sb("twos", [1, 32])
        pr = sb("pr", [1, 1])
        tj = sb("tj", [1, 32])
        fill = sb("fill", [ITEMS, CAP, 2])
        tbl = sb("tbl", [ITEMS, CAP, 2])
        hs = sb("hs", [P, 2, T])
        sgs = sb("sgs", [P, 512])
        H = [sb(f"HH{i}", [P, D]) for i in range(2)]
        lg, rk, ct = ps("lg", [P, TT, E_N]), ps("rk", [P, TT, E_N]), ps("ct", [P, 512])
        gp, up = ps("gp", [P, 512]), ps("up", [P, 512])
        yp = [ps(f"yp{i}", [P, 512]) for i in range(2)]
        tp = ps("tp", [P, 512])
        s_w, s_ws, s_wd = sem("router_in"), sem("shared_in"), sem("shared_down_in")
        s_k0, s_k = sem("patterns_cleared"), sem("patterns_set")
        s_fi, s_fo = sem("table_blank"), sem("table_blank_written")
        s_lg, s_sc, s_mk, s_rk = sem("logits"), sem("sigmoids_r"), sem("chosen"), sem("ranks")
        s_pay, s_sca, s_ti = sem("payload"), sem("table_scattered"), sem("table_in")
        s_tp, s_tk, s_ex, s_er = sem("table_turned"), sem("table_kept"), sem("experts_counted"), sem("experts_row")
        s_gu, s_sg, s_gv, s_hs = sem("gate_up"), sem("sig_shared"), sem("silu_shared"), sem("hidden_shared")
        s_y, s_a, s_ao = sem("shared_out"), sem("acc_tile"), sem("acc_written")
        s_h = [sem(f"h2_in{i}") for i in range(2)]
        s_d = sem("dve_steps3")
        s_up = sem("up_done")
        block = ctx.enter_context(nc.Block())
        h2v = h2_d[0:T, :].rearrange("(j p) n -> p j n", p=P)
        accv = acc_d[0:T, :].rearrange("(j p) n -> p j n", p=P)
        tbl_rows = tbl_d.rearrange("(i c) w -> i (c w)", c=CAP)

        @block.sync
        def _(sp):
            sp.dma_start(wr[:, :, :], ins["w_router"].rearrange("l (p t) n -> p (l t) n", t=KT)).then_inc(s_w, 16)
            sp.dma_start(bias[:, :], ins["router_bias"].to_broadcast([P, E_N])).then_inc(s_w, 16)
            sp.dma_start(wgs[:, :, :], ins["w_gate_s"].rearrange("l (p t) n -> p (l t) n", t=KT)).then_inc(s_ws, 16)
            sp.dma_start(wus[:, :, :], ins["w_up_s"].rearrange("l (p t) n -> p (l t) n", t=KT)).then_inc(s_ws, 16)
            sp.dma_start(wds[:, :, :], ins["w_down_s"].rearrange("l (f p) n -> p (l f) n", p=P)).then_inc(s_wd, 16)
            sp.wait_ge(s_fi, 2)
            sp.dma_start(tbl_rows, fill[:, :, :].rearrange("i c w -> i (c w)")).then_inc(s_fo, 16)
            sp.dma_start(acc_d[T:T + CAP, :], h2_d[T:T + CAP, :]).then_inc(s_ao, 16)
            for j in range(TT):
                if j >= 2:
                    sp.wait_ge(s_ao, 16 * j)
                sp.dma_start(H[j % 2][:, :], h2v[:, j, :]).then_inc(s_h[j % 2], 16)
                if j:
                    sp.wait_ge(s_a, j)
                    sp.dma_start(accv[:, j - 1, :], H[(j - 1) % 2][:, :]).then_inc(s_ao, 16)
            sp.wait_ge(s_a, TT)
            sp.dma_start(accv[:, TT - 1, :], H[(TT - 1) % 2][:, :]).then_inc(s_ao, 16)
            sp.wait_ge(s_ao, 16 * (TT + 1))
            sp.wait_ge(s_sca, 16 * TT * TOPK)
            sp.dma_start(tbl[:, :, :].rearrange("i c w -> i (c w)"), tbl_rows).then_inc(s_ti, 16)
            sp.wait_ge(s_ti, 16)

        @block.gpsimd
        def _(pool):
            pool.memset(before[:, :], 1.0).then_inc(s_k0, 1)
            pool.memset(fill[:, :, 1:2], 0.0).then_inc(s_fi, 1)
            pool.iota(fill[:, :, 0], [[1, CAP]], base=T, channel_multiplier=0, allow_small_or_imprecise_dtypes=True).then_inc(s_fi, 1)
            pool.memset(zero[:, :], 0.0).then_inc(s_k, 1)
            pool.iota(e0[:, :], [[CAP, E_N]], base=0, channel_multiplier=0, allow_small_or_imprecise_dtypes=True).then_inc(s_k, 1)
            pool.iota(pidx[:, :], [[0, 1]], base=0, channel_multiplier=1, allow_small_or_imprecise_dtypes=True).then_inc(s_k, 1)
            pool.iota(exrow[:, 0:E_N], [[1, E_N]], base=0, channel_multiplier=0, allow_small_or_imprecise_dtypes=True).then_inc(s_k, 1)
            pool.iota(twos[:, :], [[2, 32]], base=0, channel_multiplier=0, allow_small_or_imprecise_dtypes=True).then_inc(s_k, 1)
            pool.iota(pay[:, :, :, 0], [[P, TT], [0, TOPK]], base=0, channel_multiplier=1,
                      allow_small_or_imprecise_dtypes=True).then_inc(s_k, 1)
            pool.wait_ge(s_k0, 1)
            pool.affine_select(out=before[:, :], in_=before[:, :], compare_op=ALU.is_gt, fill=0.0,
                               base=0, pattern=[[1, P]], channel_multiplier=-1).then_inc(s_k, 1)
            pool.wait_ge(s_fo, 16)
            for j in range(TT):
                pool.wait_ge(s_pay, j + 1)
                for k in range(TOPK):
                    pool.indirect_dma_start(tbl_d, bass.IndirectOffsetOnAxis(ap=si[:, j * TOPK + k:j * TOPK + k + 1], axis=0),
                                            pay[:, j, k, :], None).then_inc(s_sca, 16)
            pool.wait_ge(s_sca, 16 * TT * TOPK)

        @block.tensor
        def _(pe):
            pe.wait_ge(s_w, 32)
            for j in range(TT):
                for t in range(KT):
                    last = pe.matmul(lg[:, j, :], K.xT[:, t, j * P:j * P + P], wr[:, t, :], start=(t == 0), stop=(t == KT - 1))
            last.then_inc(s_lg, 1)

            def hidden(b, f):
                g = 2 * b + f
                if g:
                    pe.wait_ge(s_hs, g)
                for w, out in ((wgs, gp), (wus, up)):
                    for t in range(KT):
                        last = pe.matmul(out[:, :], w[:, t, f * P:f * P + P], K.xT[:, t, 512 * b:512 * b + 512],
                                         start=(t == 0), stop=(t == KT - 1))
                    last.then_inc(s_gu if out is gp else s_up, 1)

            pe.wait_ge(s_ws, 32)
            hidden(0, 0)
            pe.wait_ge(s_k, 7)
            pe.wait_ge(s_mk, 1)
            for j in range(TT):
                last = pe.matmul(rk[:, j, :], before[:, :], MK[:, j, :], start=True, stop=(j == 0))
                if j:
                    last = pe.matmul(rk[:, j, :], K.ones[:, :], MS[:, j - 1, :], start=False, stop=True)
            last = pe.matmul(ct[:, 0:E_N], K.ones[:, :], MS[:, TT - 1, :], start=True, stop=True)
            last.then_inc(s_rk, 1)
            hidden(0, 1)
            pe.wait_ge(s_ex, 1)
            pe.matmul(tp[0:1, 0:ITEMS - E_N], tex[:, 0:1], K.ident[:, 0:ITEMS - E_N], start=True, stop=True).then_inc(s_er, 1)
            hidden(1, 0)
            hidden(1, 1)
            pe.wait_ge(s_wd, 16)
            for j in range(TT):
                if j % 4 == 0:
                    pe.wait_ge(s_hs, 2 * (j // 4) + 2)
                if j:
                    pe.wait_ge(s_a, j)
                for half in range(2):
                    for f in range(2):
                        last = pe.matmul(yp[half][:, :], hs[:, f, j * P:j * P + P], wds[:, f, 512 * half:512 * half + 512],
                                         start=(f == 0), stop=(f == 1))
                last.then_inc(s_y, 1)
            pe.wait_ge(s_ti, 16)
            pe.wait_ge(s_tk, 1)
            for k in range(2):
                pe.transpose(tp[0:P, k * ITEMS:(k + 1) * ITEMS], tbl[:, 0:P, k], K.ident[0:ITEMS, 0:ITEMS])
                last = pe.transpose(tp[0:CAP1, (2 + k) * ITEMS:(3 + k) * ITEMS], tbl[:, P:CAP, k], K.ident[0:ITEMS, 0:ITEMS])
            last.then_inc(s_tp, 1)

        @block.scalar
        def _(act):
            act.wait_ge(s_lg, 1)
            act.activation(SC[:, :, :], lg[:, :, :], ACT.Sigmoid).then_inc(s_sc, 1)
            for g in range(4):
                act.wait_ge(s_gu, g + 1)
                if g:
                    act.wait_ge(s_gv, g)
                act.activation(sgs[:, :], gp[:, :], ACT.Sigmoid).then_inc(s_sg, 1)

        @block.vector
        def _(dve):
            step = Chain(dve, s_d)
            tt, ts, stt = nc.vector.tensor_tensor, nc.vector.tensor_scalar, nc.vector.scalar_tensor_tensor

            def shared(g):
                b, f = divmod(g, 2)
                dve.wait_ge(s_sg, g + 1)
                tt(sgs[:, :], sgs[:, :], gp[:, :], ALU.mult).then_inc(s_gv, 1)
                dve.wait_ge(s_gv, g + 1)
                dve.wait_ge(s_up, g + 1)
                tt(hs[:, f, 512 * b:512 * b + 512], sgs[:, :], up[:, :], ALU.mult).then_inc(s_hs, 1)

            def over_tiles(v):
                return v[:, :].rearrange("p (o e) -> p o e", o=1).to_broadcast([P, TT, E_N])

            dve.wait_ge(s_k, 7)
            dve.wait_ge(s_w, 32)
            dve.wait_ge(s_sc, 1)
            step(tt(BI[:, :, :], SC[:, :, :], over_tiles(bias), ALU.add))
            for j in range(TT):
                last = nc.vector.max(m8[:, j, :], BI[:, j, :])
            step(last)
            for j in range(TT):
                last = nc.vector.match_replace(RE[:, j, :], m8[:, j, :], BI[:, j, :], -1e30)
            step(last)
            step(tt(MK[:, :, :], RE[:, :, :], BI[:, :, :], ALU.not_equal))
            step(nc.vector.tensor_copy(MS[:, 0, :], MK[:, 0, :]))
            for j in range(1, TT):
                step(tt(MS[:, j, :], MS[:, j - 1, :], MK[:, j, :], ALU.add))
            dve.sem_inc(s_mk, 1)
            step(tt(GT[:, :, :], SC[:, :, :], MK[:, :, :], ALU.mult))
            step(nc.vector.reduce_sum(gs[:, :], GT[:, :, :], mybir.AxisListType.X))
            step(nc.vector.reciprocal(gs[:, :], gs[:, :]))
            step(tt(GT[:, :, :], GT[:, :, :], bcast(gs[:, :], E_N), ALU.mult))
            step(ts(GT[:, :, :], GT[:, :, :], ROUTED_SCALE, None, ALU.mult))
            dve.wait_ge(s_rk, 1)
            step(nc.vector.tensor_copy(cnt[:, :], ct[:, 0:E_N]))
            step(ts(ext[:, :], cnt[:, :], float(CAP), None, ALU.is_gt))
            for m in range(2, MORE + 1):
                step(stt(ext[:, :], cnt[:, :], float(m * CAP), ext[:, :], ALU.is_gt, ALU.add))
            step(nc.vector.tensor_tensor_scan(inc[:, :], ext[:, :], zero[:, :], 0.0, ALU.add, ALU.add))
            step(tt(b0[:, :], inc[:, :], ext[:, :], ALU.subtract))
            step(ts(b0[:, :], b0[:, :], float(CAP), float((E_N - 1) * CAP), ALU.mult, ALU.add))
            step(tt(ba[:, :], b0[:, :], e0[:, :], ALU.subtract))
            step(ts(T1[:, :, :], rk[:, :, :], float(CAP), None, ALU.is_ge))
            step(tt(T1[:, :, :], T1[:, :, :], over_tiles(ba), ALU.mult))
            step(tt(T1[:, :, :], T1[:, :, :], over_tiles(e0), ALU.add))
            step(tt(SL[:, :, :], rk[:, :, :], T1[:, :, :], ALU.add))
            step(stt(SL[:, :, :], SL[:, :, :], 1.0, MK[:, :, :], ALU.add, ALU.mult))
            step(ts(SL[:, :, :], SL[:, :, :], -1.0, None, ALU.add))
            for j in range(TT):
                last = nc.vector.max(s8[:, j, :], SL[:, j, :])
            step(last)
            step(nc.vector.tensor_copy(si[:, :], s8[:, :, :].rearrange("p j k -> p (j k)")))
            for j in range(TT):
                for k in range(TOPK):
                    step(stt(junk[:, :], SL[:, j, :], s8[:, j, k:k + 1], GT[:, j, :], ALU.is_equal, ALU.mult,
                             accum_out=pay[:, j, k, 1:2]))
                dve.sem_inc(s_pay, 1)
                if j == 0:
                    step(ts(junk[:, :], inc[:, :], pidx[:, 0:1], None, ALU.is_le))
                    step(nc.vector.reduce_sum(tex[:, :], junk[:, :], mybir.AxisListType.X))
                    step(ts(tex[:, :], tex[:, :], float(E_N - 1), None, ALU.min))
                    dve.sem_inc(s_ex, 1)
                    shared(0)
                if j == 3:
                    shared(1)
            dve.wait_ge(s_er, 1)
            step(nc.vector.tensor_copy(exrow[:, E_N:ITEMS], tp[0:1, 0:ITEMS - E_N]))
            step(nc.vector.tensor_copy(K.expert[:, :], exrow[:, :]))
            step(ts(tj[:, :], twos[:, :], inc[0:1, E_N - 1:E_N], None, ALU.is_lt))
            step(nc.vector.reduce_sum(pr[:, :], tj[:, :], mybir.AxisListType.X))
            step(ts(pr[:, :], pr[:, :], float(E_N // 2), None, ALU.add))
            step(nc.vector.tensor_copy(K.pairs[:, :], pr[:, :]))
            dve.sem_inc(s_tk, 1)
            shared(2)
            shared(3)
            for j in range(TT):
                dve.wait_ge(s_y, j + 1)
                dve.wait_ge(s_h[j % 2], 16 * (j // 2 + 1))
                for half in range(2):
                    cols = slice(512 * half, 512 * half + 512)
                    last = tt(H[j % 2][:, cols], H[j % 2][:, cols], yp[half][:, :], ALU.add)
                last.then_inc(s_a, 1)
            dve.wait_ge(s_tp, 1)
            for k, n in ((0, P), (1, CAP1)):
                nc.vector.tensor_copy(K.idx[k][:, :], tp[0:n, 2 * k * ITEMS:(2 * k + 1) * ITEMS])
                step(nc.vector.tensor_copy(K.gate[k][:, :], tp[0:n, (2 * k + 1) * ITEMS:(2 * k + 2) * ITEMS]))


def phase_experts(nc, ins, K, xn2_d, acc_d):
    wg_d = ins["w_gate_e"].rearrange("l e (p t) f -> p (l e) t f", t=KT)
    wu_d = ins["w_up_e"].rearrange("l e (p t) f -> p (l e) t f", t=KT)
    wd_d = ins["w_down_e"].rearrange("l e (f p) n -> p (l e) f n", p=P)
    with ExitStack() as ctx:
        def sb(name, shape, dt=F32):
            return ctx.enter_context(nc.sbuf_tensor(name, shape, dt))

        def ps(name, shape):
            return ctx.enter_context(nc.psum_tensor(name, shape, F32))
        sem = lambda n: ctx.enter_context(nc.semaphore(n))
        two = range(2)
        WG = [sb(f"WG{i}", [P, KT, FF]) for i in two]
        WU = [sb(f"WU{i}", [P, KT, FF]) for i in two]
        WD = [sb(f"WD{i}", [P, 2, D]) for i in two]
        XG = [(sb(f"XG{i}", [P, D]), sb(f"XH{i}", [CAP1, D])) for i in two]
        XE = [sb(f"XE{i}", [P, KT, CAP]) for i in two]
        SS = sb("SS", [P, 2, CAP])
        HE = [sb(f"HE{i}", [P, 2, CAP]) for i in two]
        YE = [(sb(f"YE{i}", [P, D]), sb(f"YF{i}", [CAP1, D])) for i in two]
        gi = [(sb(f"gi{i}", [P, 1], I32), sb(f"gj{i}", [CAP1, 1], I32)) for i in two]
        si = [(sb(f"sia{i}", [P, 1], I32), sb(f"sib{i}", [CAP1, 1], I32)) for i in two]
        gt = [(sb(f"gta{i}", [P, 1]), sb(f"gtb{i}", [CAP1, 1])) for i in two]
        gp, up = ps("gpe", [P, 2, CAP]), ps("upe", [P, 2, CAP])
        xp = [ps(f"xp{i}", [P, 3, CAP]) for i in two]
        yp = [[ps(f"ype{r}{h}", [P, 512]) for h in two] for r in two]
        s_wgu = [sem(f"gate_up_in{i}") for i in two]
        s_wd = [sem(f"down_in{i}") for i in two]
        s_gufree, s_dfree = sem("gate_up_free"), sem("down_free")
        s_pi, s_g = sem("pool_copies"), [sem(f"gathered{i}") for i in two]
        s_gt, s_ad, s_free = sem("gates_set"), sem("rows_added"), sem("rows_free")
        s_tp, s_te, s_td = sem("x_turned"), sem("x_kept_act"), sem("x_kept_dve")
        s_gg, s_uu, s_ss, s_sv, s_he = sem("gate_done"), sem("up_done_e"), sem("sig_e"), sem("silu_e"), sem("hidden_e")
        s_y, s_ya, s_yd = sem("y_done"), sem("y_kept_act"), sem("y_kept_dve")
        turn = {e: sem(f"turn_{e}") for e in ("sp", "pool", "act", "dve", "pe")}
        block = ctx.enter_context(nc.Block())
        ROWS = (P, CAP1)
        LIMIT = ITEMS // 2 - 1

        def pairs(engine):
            return engine.value_load(K.pairs[0:1, 0:1], min_val=E_N // 2, max_val=LIMIT)

        @block.sync
        def _(sp):
            with sp.Fori(0, pairs(sp)) as i:
                for q in two:
                    n = i * 2 + q
                    e = sp.value_load(K.expert[0:1, bass.ds(n, 1)], min_val=0, max_val=E_N - 1)
                    sp.wait_ge(s_gufree, n + 1)
                    sp.sem_inc(turn["sp"], 1)
                    sp.dma_start(WG[q][:, :, :], wg_d[:, bass.ds(e, 1), :, :]).then_inc(s_wgu[q], 16)
                    sp.dma_start(WU[q][:, :, :], wu_d[:, bass.ds(e, 1), :, :]).then_inc(s_wgu[q], 16)
                    sp.wait_ge(s_dfree, n + 1)
                    sp.sem_inc(turn["sp"], 1)
                    sp.dma_start(WD[q][:, :, :], wd_d[:, bass.ds(e, 1), :, :]).then_inc(s_wd[q], 16)

        @block.gpsimd
        def _(pool):
            def gather(q, n, first):
                for r in two:
                    pool.tensor_copy(gt[q][r][:, :], K.gate[r][:, bass.ds(n, 1)])
                    pool.tensor_copy(gi[q][r][:, :], K.idx[r][:, bass.ds(n, 1)]).then_inc(s_pi, 1)
                pool.sem_inc(turn["pool"], 1)
                pool.wait_ge(s_pi, first + 2)
                pool.sem_inc(s_gt, 1)
                for r in two:
                    pool.indirect_dma_start(XG[q][r][:, :], None, xn2_d, bass.IndirectOffsetOnAxis(ap=gi[q][r][:, :], axis=0)) \
                        .then_inc(s_g[q], 16)

            gather(0, 0, 0)
            gather(1, 1, 2)
            pool.sem_inc(s_free, 2)
            with pool.Fori(0, pairs(pool)) as i:
                for q in two:
                    n = i * 2 + q
                    pool.wait_ge(s_ya, n + 2)
                    pool.sem_inc(turn["pool"], 1)
                    pool.wait_ge(s_yd, n + 2)
                    pool.sem_inc(turn["pool"], 1)
                    for r in two:
                        pool.tensor_copy(si[q][r][:, :], K.idx[r][:, bass.ds(n, 1)]).then_inc(s_pi, 1)
                    pool.wait_ge(s_pi, n * 4 + 6)
                    pool.sem_inc(turn["pool"], 1)
                    for r in two:
                        pool.indirect_dma_start(acc_d, bass.IndirectOffsetOnAxis(ap=si[q][r][:, :], axis=0), YE[q][r][:, :], None,
                                                compute_op=ALU.add).then_inc(s_ad, 16)
                    pool.wait_ge(s_g[q], i * 32 + 32)
                    pool.sem_inc(turn["pool"], 1)
                    pool.wait_ge(s_tp, n * 3 + 3)
                    gather_at = n * 4 + 6
                    pool.sem_inc(turn["pool"], 1)
                    gather(q, n + 2, gather_at)
                    pool.wait_ge(s_ad, n * 32 + 32)
                    pool.sem_inc(s_free, 1)
            total = pairs(pool)
            for q in two:
                pool.wait_ge(s_g[q], total * 32 + 32)
                pool.sem_inc(turn["pool"], 1)

        @block.tensor
        def _(pe):
            pe.sem_inc(s_gufree, 2)
            pe.sem_inc(s_dfree, 2)

            def turned(q, n, gathers):
                pe.wait_ge(s_g[q], gathers)
                for c in range(3):
                    tiles = range(3 * c, min(3 * c + 3, KT))
                    if c == 0:
                        pe.wait_ge(s_te, n * 2 + 1)
                    elif c == 1:
                        pe.wait_ge(s_td, n + 1)
                    else:
                        pe.wait_ge(s_te, n * 2 + 2)
                    for t in tiles:
                        for r, (a, b) in enumerate(((0, P), (P, CAP))):
                            rows = XG[q][r][:, :].rearrange("p (k t) -> p t k", t=KT)
                            last = pe.transpose(xp[c % 2][:, t - 3 * c, a:b], rows[:, t, :], K.ident[0:b - a, 0:b - a])
                    last.then_inc(s_tp, 1)

            turned(0, 0, 32)
            with pe.Fori(0, pairs(pe)) as i:
                for q in two:
                    n = i * 2 + q
                    pe.wait_ge(s_te, n * 2 + 3)
                    pe.wait_ge(s_td, n + 2)
                    pe.wait_ge(s_wgu[q], i * 32 + 32)
                    pe.wait_ge(s_he, n + 1)
                    for w, out, s_out in ((WG[q], gp, s_gg), (WU[q], up, s_uu)):
                        for f in two:
                            for t in range(KT):
                                last = pe.matmul(out[:, f, :], w[:, t, f * P:f * P + P], XE[q][:, t, :], start=(t == 0), stop=(t == KT - 1))
                        last.then_inc(s_out, 1)
                    turned(1 - q, n + 1, (i + q) * 32 + 32)
                    pe.wait_ge(s_uu, n + 1)
                    pe.sem_inc(s_gufree, 1)
                    pe.wait_ge(s_he, n + 2)
                    pe.wait_ge(s_wd[q], i * 16 + 16)
                    pe.wait_ge(s_ya, n + 1)
                    pe.wait_ge(s_yd, n + 1)
                    for r, (a, b) in enumerate(((0, P), (P, CAP))):
                        for half in two:
                            for f in two:
                                last = pe.matmul(yp[r][half][0:b - a, :], HE[q][:, f, a:b], WD[q][:, f, 512 * half:512 * half + 512],
                                                 start=(f == 0), stop=(f == 1))
                            last.then_inc(s_y, 1)
                    pe.wait_ge(s_y, n * 4 + 4)
                    pe.sem_inc(s_dfree, 1)

        @block.scalar
        def _(act):
            act.sem_inc(s_te, 1)
            act.sem_inc(s_ya, 1)

            def keep(q, n, first):
                for c in (0, 2):
                    act.wait_ge(s_tp, n * 3 + c + 1)
                    tiles = slice(3 * c, min(3 * c + 3, KT))
                    act.copy(XE[q][:, tiles, :], xp[0][:, 0:tiles.stop - tiles.start, :]).then_inc(s_te, 1)

            keep(0, 0, 0)
            with act.Fori(0, pairs(act)) as i:
                for q in two:
                    n = i * 2 + q
                    act.wait_ge(s_gg, n + 1)
                    act.wait_ge(s_he, n + 1)
                    act.activation(SS[:, :, :], gp[:, :, :], ACT.Sigmoid).then_inc(s_ss, 1)
                    keep(1 - q, n + 1, 0)
                    act.wait_ge(s_gt, n + 1)
                    act.wait_ge(s_free, n + 1)
                    for r in two:
                        act.wait_ge(s_y, n * 4 + 2 * r + 1)
                        last = act.activation(YE[q][r][:, 0:512], yp[r][0][0:ROWS[r], :], ACT.Copy, scale=gt[q][r][:, 0:1])
                    last.then_inc(s_ya, 1)

        @block.vector
        def _(dve):
            dve.sem_inc(s_td, 1)
            dve.sem_inc(s_yd, 1)
            dve.sem_inc(s_he, 1)

            def keep(q, n):
                dve.wait_ge(s_tp, n * 3 + 2)
                dve.sem_inc(turn["dve"], 1)
                nc.vector.tensor_copy(XE[q][:, 3:6, :], xp[1][:, :, :]).then_inc(s_td, 1)

            keep(0, 0)
            with dve.Fori(0, pairs(dve)) as i:
                for q in two:
                    n = i * 2 + q
                    dve.wait_ge(s_ss, n + 1)
                    nc.vector.tensor_tensor(SS[:, :, :], SS[:, :, :], gp[:, :, :], ALU.mult).then_inc(s_sv, 1)
                    dve.wait_ge(s_uu, n + 1)
                    dve.wait_ge(s_sv, n + 1)
                    nc.vector.tensor_tensor(HE[q][:, :, :], SS[:, :, :], up[:, :, :], ALU.mult).then_inc(s_he, 1)
                    keep(1 - q, n + 1)
                    dve.wait_ge(s_gt, n + 1)
                    dve.wait_ge(s_free, n + 1)
                    for r in two:
                        dve.wait_ge(s_y, n * 4 + 2 * r + 2)
                        last = nc.vector.tensor_scalar(YE[q][r][:, 512:D], yp[r][1][0:ROWS[r], :], gt[q][r][:, 0:1], None, ALU.mult)
                    last.then_inc(s_yd, 1)


def phase_final(nc, ins, K, acc_d, out):
    with ExitStack() as ctx:
        def sb(name, shape, dt=F32):
            return ctx.enter_context(nc.sbuf_tensor(name, shape, dt))
        sem = lambda n: ctx.enter_context(nc.semaphore(n))
        A = [sb(f"A{j}", [P, D]) for j in range(TT)]
        junk = [sb(f"junkf{i}", [P, D]) for i in range(2)]
        ss, rt = sb("ssf", [P, TT]), sb("rtf", [P, TT])
        gf = sb("gf", [P, D])
        s_a = [sem(f"acc_in{j}") for j in range(TT)]
        s_gf, s_s, s_r, s_rc, s_o, s_out = sem("gfinal_in"), sem("squares_f"), sem("roots_f"), sem("recips_f"), sem("rows_f"), sem("out_written")
        block = ctx.enter_context(nc.Block())
        accv = acc_d[0:T, :].rearrange("(j p) n -> p j n", p=P)
        outv = out.rearrange("b (j p) n -> p (b j) n", p=P)

        @block.sync
        def _(sp):
            for j in range(TT):
                sp.dma_start(A[j][:, :], accv[:, j, :]).then_inc(s_a[j], 16)
                if j == 0:
                    sp.dma_start(gf[:, :], ins["norm_final_g"].rearrange("(o n) -> o n", o=1).to_broadcast([P, D])).then_inc(s_gf, 16)
            for j in range(TT):
                sp.wait_ge(s_o, j + 1)
                sp.dma_start(outv[:, j, :], A[j][:, :]).then_inc(s_out, 16)
            sp.wait_ge(s_out, 16 * TT)

        @block.scalar
        def _(act):
            for j in range(TT):
                act.wait_ge(s_a[j], 16)
                if j >= 2:
                    act.wait_ge(s_s, j - 1)
                act.activation(junk[j % 2][:, :], A[j][:, :], ACT.Square, accum_out=ss[:, j:j + 1]).then_inc(s_s, 1)
                act.wait_ge(s_s, j + 1)
                act.activation(rt[:, j:j + 1], ss[:, j:j + 1], ACT.Sqrt, bias=K.eps[:, 0:1], scale=1.0 / D).then_inc(s_r, 1)

        @block.vector
        def _(dve):
            dve.wait_ge(s_gf, 16)
            for j in range(TT):
                dve.wait_ge(s_r, j + 1)
                nc.vector.reciprocal(rt[:, j:j + 1], rt[:, j:j + 1]).then_inc(s_rc, 1)
                dve.wait_ge(s_rc, j + 1)
                nc.vector.scalar_tensor_tensor(A[j][:, :], A[j][:, :], rt[:, j:j + 1], gf[:, :], ALU.mult, ALU.mult).then_inc(s_o, 1)


def build(nc, ins, out):
    h2_d = nc.dram_tensor("h2_rows", (T + CAP, D), F32, kind="Internal").ap()
    xn2_d = nc.dram_tensor("xn2_rows", (T + CAP, D), F32, kind="Internal").ap()
    acc_d = nc.dram_tensor("acc_rows", (T + CAP, D), F32, kind="Internal").ap()
    tbl_d = nc.dram_tensor("slot_table", (ITEMS * CAP, 2), F32, kind="Internal").ap()

    class Kept:
        pass
    K = Kept()
    with ExitStack() as ctx:
        setup(nc, ctx, ins, K)
        with ExitStack() as mix:
            phase_norm(nc, ins, K)
            phase_mix(nc, mix, ins, K)
            phase_out(nc, ins, K, h2_d, xn2_d)
        phase_route(nc, ctx, ins, K, h2_d, acc_d, tbl_d)
        phase_experts(nc, ins, K, xn2_d, acc_d)
        phase_final(nc, ins, K, acc_d, out)


_INS = ["x", "meta_tokens", "norm_mix_g", "w_in", "lb_table", "hgrn_norm_g", "conv_w", "conv_norm_g", "w_out", "norm_ffn_g",
        "w_router", "router_bias", "w_gate_e", "w_up_e", "w_down_e", "w_gate_s", "w_up_s", "w_down_s", "norm_final_g"]


def kernel(**inputs):
    import numpy as np
    import concourse.bacc as bacc
    from concourse.bass_utils import run_bass_kernel_spmd

    nc = bacc.Bacc("TRN2", target_bir_lowering=False, num_devices=1)
    arrays, ins = {}, {}
    for name in _INS:
        a = np.ascontiguousarray(inputs[name])
        arrays[f"in_{name}"] = a
        ins[name] = nc.dram_tensor(f"in_{name}", a.shape, mybir.dt.from_np(a.dtype), kind="ExternalInput").ap()
    out = nc.dram_tensor("out_0", (1, T, D), F32, kind="ExternalOutput").ap()
    build(nc, ins, out)
    r = run_bass_kernel_spmd(nc, [arrays], core_ids=[0])
    return r.results[0]["out_0"]
```

```python
import concourse.bass as bass
from concourse import mybir
from contextlib import ExitStack

F32 = mybir.dt.float32
F32R = mybir.dt.float32r
I32 = mybir.dt.int32
ALU = mybir.AluOpType
ACT = mybir.ActivationFunctionType

P = 128
D = 1024
KT = D // P
T = 1024
TT = T // P
META = 16
ALL = META + T
HEADS = 4
HW = HEADS * P
E_N = 64
TOPK = 8
FF = 256
EPS = 1e-6
LEVELS = [64, 32, 16, 8, 4, 2, 1]
CAP = 168
CAP1 = CAP - P
ITEMS = E_N + (T * TOPK) // CAP + 3
MORE = -(-T // CAP) - 1
ROUTED_SCALE = 2.5
Z_LOW = -80.0


class Chain:

    def __init__(self, engine, sem):
        self.engine, self.sem, self.base, self.k = engine, sem, 0, 0

    def __call__(self, ins):
        ins.then_inc(self.sem, 1)
        self.k += 1
        self.engine.wait_ge(self.sem, self.base + self.k)

    def enter(self, i, steps):
        self.start = self.base + self.k
        self.steps, self.base, self.k = steps, i * steps + self.start, 0

    def leave(self, turns):
        assert self.k == self.steps, (self.k, self.steps)
        self.base, self.k = self.start + turns * self.steps, 0


def bcast(ap, n):
    return ap.rearrange("p (a o) -> p a o", o=1).to_broadcast([ap.shape[0], ap.shape[1], n])


def setup(nc, ctx, ins, K):
    def sb(name, shape, dt=F32):
        return ctx.enter_context(nc.sbuf_tensor(name, shape, dt))
    K.ident = sb("ident", [P, P])
    K.ones = sb("ones", [P, P])
    K.idx = [sb("idx0", [P, ITEMS], I32), sb("idx1", [CAP1, ITEMS], I32)]
    K.gate = [sb("gate0", [P, ITEMS]), sb("gate1", [CAP1, ITEMS])]
    K.expert = sb("expert", [1, ITEMS], I32)
    K.pairs = sb("pairs", [1, 1], I32)
    K.eps = sb("eps", [P, 1])


def phase_norm(nc, ins, K):
    x = ins["x"].rearrange("b (j p) n -> p (b j) n", p=P)
    with ExitStack() as ctx:
        def sb(name, shape, dt=F32):
            return ctx.enter_context(nc.sbuf_tensor(name, shape, dt))
        xt = sb("xt", [P, TT + 1, D])
        junk = [sb(f"junk{i}", [P, D]) for i in range(2)]
        ss = sb("ss", [P, TT + 1])
        rstd = sb("rstd", [P, TT + 1])
        xs = [sb(f"xs{i}", [P, D]) for i in range(2)]
        gmix = sb("gmix", [P, KT])
        pt = [ctx.enter_context(nc.psum_tensor(f"pt{i}", [P, 4, P], F32)) for i in range(4)]
        sem = lambda n: ctx.enter_context(nc.semaphore(n))
        s_x = [sem(f"x_in{j}") for j in range(TT + 1)]
        s_g = sem("gmix_in")
        s_c = sem("consts_set")
        s_c0 = sem("consts_cleared")
        s_ss = sem("squares_summed")
        s_ms = sem("mean_square")
        s_rt = sem("root")
        s_rs = sem("rstd_ready")
        s_xs = sem("x_scaled")
        s_tr = sem("x_transposed")
        s_ev = sem("xT_stored")
        block = ctx.enter_context(nc.Block())
        order = [TT] + list(range(TT))

        @block.sync
        def _(sp):
            sp.dma_start(xt[0:META, TT, :], ins["meta_tokens"]).then_inc(s_x[TT], 16)
            for j in range(TT):
                sp.dma_start(xt[:, j, :], x[:, j, :]).then_inc(s_x[j], 16)
            sp.dma_start(gmix[:, :], ins["norm_mix_g"].rearrange("l (p t) -> p (l t)", t=KT)).then_inc(s_g, 16)

        @block.gpsimd
        def _(pool):
            pool.memset(K.ident[:, :], 0.0).then_inc(s_c0, 1)
            pool.memset(K.ones[:, :], 1.0).then_inc(s_c, 1)
            pool.memset(K.eps[:, :], EPS).then_inc(s_c, 1)
            pool.memset(ss[:, :], 1.0).then_inc(s_c, 1)
            pool.wait_ge(s_c0, 1)
            pool.affine_select(out=K.ident[:, :], in_=K.ident[:, :], compare_op=ALU.not_equal, fill=1.0,
                               base=0, pattern=[[-1, P]], channel_multiplier=1).then_inc(s_c, 1)

        @block.scalar
        def _(act):
            act.wait_ge(s_c, 4)
            for c, j in enumerate(order):
                n = META if j == TT else P
                act.wait_ge(s_x[j], 16)
                if c >= 2:
                    act.wait_ge(s_ss, c - 1)
                act.activation(junk[c % 2][0:n, :], xt[0:n, j, :], ACT.Square,
                               accum_out=ss[0:n, j:j + 1]).then_inc(s_ss, 1)
            act.wait_ge(s_ss, TT + 1)
            act.activation(rstd[:, :], ss[:, :], ACT.Sqrt, bias=K.eps[:, 0:1], scale=1.0 / D).then_inc(s_rt, 1)
            act.wait_ge(s_rs, 1)
            for c, j in enumerate(order):
                n = META if j == TT else P
                if c >= 2:
                    act.wait_ge(s_tr, c - 1)
                act.activation(xs[c % 2][0:n, :], xt[0:n, j, :], ACT.Copy, scale=rstd[0:n, j:j + 1]).then_inc(s_xs, 1)

        @block.vector
        def _(dve):
            dve.wait_ge(s_rt, 1)
            dve.reciprocal(rstd[:, :], rstd[:, :]).then_inc(s_rs, 1)
            dve.wait_ge(s_g, 16)
            for c, j in enumerate(order):
                n = META if j == TT else P
                col = 0 if j == TT else META + j * P
                dve.wait_ge(s_tr, c + 1)
                for half in range(2):
                    last = dve.tensor_tensor(K.xT[:, 4 * half:4 * half + 4, col:col + n],
                                             pt[2 * (c % 2) + half][:, :, 0:n],
                                             bcast(gmix[:, 4 * half:4 * half + 4], n), ALU.mult)
                last.then_inc(s_ev, 1)

        @block.tensor
        def _(pe):
            pe.wait_ge(s_c, 4)
            for c, j in enumerate(order):
                n = META if j == TT else P
                pe.wait_ge(s_xs, c + 1)
                if c >= 2:
                    pe.wait_ge(s_ev, c - 1)
                rows = xs[c % 2][0:n, :].rearrange("p (k t) -> p t k", t=KT)
                for t in range(KT):
                    last = pe.transpose(pt[2 * (c % 2) + t // 4][:, t % 4, 0:n], rows[:, t, :], K.ident[0:n, 0:n])
                last.then_inc(s_tr, 1)


def phase_mix(nc, ctx_out, ins, K):
    w_in = ins["w_in"].rearrange("l (p t) n -> p (l t) n", t=KT)
    COL_Q, COL_F, COL_I, COL_GB, COL_CV = 0, HW, 2 * HW, 3 * HW, 5 * HW

    def keep(name, shape, dt=F32):
        return ctx_out.enter_context(nc.sbuf_tensor(name, shape, dt))
    K.QO = keep("QO", [P, HEADS, T])
    K.CV = keep("CV", [P, 2 * HEADS, ALL])
    K.GB = keep("GB", [P, 2 * HEADS, T])
    with ExitStack() as ctx:
        def sb(name, shape, dt=F32):
            return ctx.enter_context(nc.sbuf_tensor(name, shape, dt))

        def ps(name, shape):
            return ctx.enter_context(nc.psum_tensor(name, shape, F32))
        sem = lambda n: ctx.enter_context(nc.semaphore(n))
        FP = sb("FP", [P, HEADS, ALL])
        VT = sb("VT", [P, TT, HW])
        VM = sb("VM", [META, HW])
        wi = sb("wi", [P, KT, HW])
        spare = wi[:, :, :].rearrange("p t n -> p (t n)")
        wbuf = [sb(f"wbuf{i}", [P, KT, P])[:, :, :] for i in range(2)] + \
            [spare[:, D * i:D * i + D].rearrange("p (t n) -> p t n", t=KT) for i in range(2)]
        lbt = sb("lbt", [P, 2, HEADS])
        lbw = sb("lbw", [P, 5, HEADS])
        masks = sb("masks", [P, len(LEVELS), HEADS * 64], mybir.dt.int16)
        restart = sb("restart", [P, HEADS, P])
        names = ("Z", "EZ", "SG", "KK", "BB", "QS", "QE", "DK", "KE", "KTS", "VC", "ST", "SCT")
        Z, EZ, SG, KK, BB, QS, QE, DK, KE, KTS, VC, ST, SCT = (sb(n, [P, HEADS, P]) for n in names)
        FV, LF = Z, EZ
        DD, WW = ([spare[:, 2 * D + HW * (2 * k + i):2 * D + HW * (2 * k + i + 1)].rearrange("p (h t) -> p h t", h=HEADS)
                   for i in range(2)] for k in range(2))
        blast = sb("blast", [P, HEADS])
        oml, lb = lbw[:, 3, :], lbw[:, 2, :]
        bank = [ps(f"bank{i}", [P, 512]) for i in range(2)]
        bankm = ps("bankm", [P, 512])
        sc = [ps(f"sc{i}", [P, HEADS * P]) for i in range(2)]
        kt_ps, o_ps, st_ps = ps("kt_ps", [P, HEADS, P]), ps("o_ps", [P, HEADS, P]), ps("st_ps", [P, HEADS, P])

        s_wi, s_lb = sem("wi_in"), sem("lb_in")
        s_w = [sem(f"w_in{i}") for i in range(4)]
        s_wfree = [sem(f"w_free{i}") for i in range(4)]
        s_mm, s_out = sem("projected"), sem("projection_stored")
        s_cst0, s_cst = sem("masks_cleared"), sem("masks_set")
        s_d, s_a, s_t = sem("dve_steps"), sem("act_steps"), sem("turns")
        s_lbx, s_lbe = sem("lb_shifted"), sem("lb_exp")
        s_ez, s_zz, s_fv, s_lf = sem("exp_z"), sem("z_held"), sem("f_ready"), sem("log_f")
        s_cp = sem("chunk_copied")
        s_dd, s_ww0, s_ww, s_s, s_p = sem("decay_logs"), sem("decays"), sem("factors"), sem("scores"), sem("scores_kept")
        s_de, s_ee = sem("end_logs"), sem("end_decays")
        s_ke, s_kt, s_kts = sem("k_end"), sem("k_end_turned"), sem("k_end_stored")
        s_kq = sem("kq_ready")
        s_o, s_oev, s_st, s_stk = sem("o_ready"), sem("o_stored"), sem("state_term"), sem("state_kept")
        block = ctx.enter_context(nc.Block())
        L1, L2 = HEADS, TT
        V_GROUPS = TT + 1

        @block.sync
        def _(sp):
            sp.dma_start(wi[:, :, :], w_in[:, :, COL_I:COL_I + HW]).then_inc(s_wi, 16)
            sp.dma_start(lbt[:, :, :], ins["lb_table"].rearrange("l (h p) -> p l h", p=P),
                         allow_slow_non_contiguous=True).then_inc(s_lb, 16)
            with sp.Fori(0, L1) as i:
                for s, col in ((0, COL_F), (1, COL_Q)):
                    sp.wait_ge(s_wfree[s], i + 1)
                    sp.sem_inc(s_t, 1)
                    sp.dma_start(wbuf[s][:, :, :], w_in[:, :, bass.ds(i * P + col, P)]).then_inc(s_w[s], 16)
            with sp.Fori(0, L2) as i:
                for s, col in ((2, COL_CV), (3, COL_GB)):
                    sp.wait_ge(s_wfree[s], i + 1)
                    sp.sem_inc(s_t, 1)
                    sp.dma_start(wbuf[s][:, :, :], w_in[:, :, bass.ds(i * P + col, P)]).then_inc(s_w[s], 16)

        @block.gpsimd
        def _(pool):
            pool.memset(restart[:, :, :], 1.0).then_inc(s_cst0, 1)
            pool.memset(masks[:, :, :], 1).then_inc(s_cst0, 1)
            pool.wait_ge(s_cst0, 2)
            pool.memset(restart[:, :, 0:1], 0.0).then_inc(s_cst, 1)
            for l, half in enumerate(LEVELS):
                n = 64 // half
                m = masks[:, l, :].rearrange("p (h b r) -> p h b r", h=HEADS, r=half)
                pool.affine_select(out=m, in_=m, compare_op=ALU.is_ge, fill=0.0, base=0,
                                   pattern=[[0, HEADS], [-2 * half, n], [0, half]], channel_multiplier=1).then_inc(s_cst0, 1)
                pool.wait_ge(s_cst0, 3 + l)
                pool.affine_select(out=m, in_=m, compare_op=ALU.is_ge, fill=0.0, base=half - 1,
                                   pattern=[[0, HEADS], [2 * half, n], [0, half]], channel_multiplier=-1).then_inc(s_cst, 1)

        @block.tensor
        def _(pe):
            done = [0]

            def group(out, n, lhs, rhs):
                for t in range(KT):
                    last = pe.matmul(out, lhs(t), rhs(t), start=(t == 0), stop=(t == KT - 1))
                last.then_inc(s_mm, 1)

            pe.wait_ge(s_wi, 16)
            for j in range(V_GROUPS):
                if j >= 2:
                    pe.wait_ge(s_out, j - 1)
                n, col = (P, META + j * P) if j < TT else (META, 0)
                group(bank[j % 2][0:n, :], n, lambda t: K.xT[:, t, col:col + n], lambda t: wi[:, t, :])

            def project(s, b, base):
                cols = slice(META + 512 * b, META + 512 * b + 512)
                pe.wait_ge(s_out, base - 1)
                group(bank[b][:, :], 512, lambda t: wbuf[s][:, t, :], lambda t: K.xT[:, t, cols])

            def project_meta(s, base):
                pe.wait_ge(s_out, base - 1)
                group(bankm[:, 0:META], META, lambda t: wbuf[s][:, t, :], lambda t: K.xT[:, t, 0:META])

            pe.wait_ge(s_mm, V_GROUPS)
            for s in range(4):
                pe.sem_inc(s_wfree[s], 1)
            with pe.Fori(0, L1) as i:
                base = i * 5 + V_GROUPS
                pe.wait_ge(s_w[0], i * 16 + 16)
                project_meta(0, base)
                project(0, 0, base + 1)
                project(0, 1, base + 2)
                pe.sem_inc(s_t, 1)
                pe.wait_ge(s_mm, base + 3)
                pe.sem_inc(s_wfree[0], 1)
                pe.wait_ge(s_w[1], i * 16 + 16)
                project(1, 0, base + 3)
                project(1, 1, base + 4)
                pe.wait_ge(s_mm, base + 5)
                pe.sem_inc(s_wfree[1], 1)

            pe.wait_ge(s_ke, 1)
            for h in range(HEADS):
                last = pe.transpose(kt_ps[0:META, h, :], KE[:, h, 0:META], K.ident[:, :])
            last.then_inc(s_kt, 1)
            pe.wait_ge(s_kts, 1)
            for h in range(HEADS):
                last = pe.matmul(st_ps[:, h, :], KTS[0:META, h, :], VM[:, h * P:(h + 1) * P], start=True, stop=True)
            last.then_inc(s_st, 1)

            with pe.Fori(0, L2) as i:
                base = i * 5 + V_GROUPS + 5 * L1
                NS = len(LEVELS) + 1

                def level(l):
                    if l == 0:
                        pe.wait_ge(s_kq, i + 1)
                        pe.wait_ge(s_p, i * NS + 1)
                        for h in range(HEADS):
                            last = pe.matmul(sc[0][:, h * P:(h + 1) * P], KK[:, h, :], QS[:, h, :], start=True, stop=True)
                    else:
                        half = LEVELS[l - 1]
                        pe.wait_ge(s_ww, i * len(LEVELS) + l)
                        pe.wait_ge(s_p, i * NS + l)
                        W = WW[l % 2]
                        for h in range(HEADS):
                            late = W[:, h, :].rearrange("p (b z r) -> p b z r", z=2, r=half)[:, :, 1, :]
                            last = pe.matmul(sc[l % 2][:, h * 64:(h + 1) * 64], W[:, h, :], late, start=True, stop=True)
                    last.then_inc(s_s, 1)

                pe.wait_ge(s_w[2], i * 16 + 16)
                project_meta(2, base)
                project(2, 0, base + 1)
                level(0)
                level(1)
                project(2, 1, base + 2)
                pe.wait_ge(s_mm, base + 3)
                pe.sem_inc(s_wfree[2], 1)
                level(2)
                level(3)
                pe.wait_ge(s_w[3], i * 16 + 16)
                project(3, 0, base + 3)
                level(4)
                level(5)
                level(6)
                pe.wait_ge(s_ke, i + 2)
                for h in range(HEADS):
                    last = pe.transpose(kt_ps[:, h, :], KE[:, h, :], K.ident[:, :])
                last.then_inc(s_kt, 1)
                project(3, 1, base + 4)
                pe.wait_ge(s_mm, base + 5)
                pe.sem_inc(s_wfree[3], 1)
                level(7)
                pe.wait_ge(s_kts, i + 2)
                for h in range(HEADS):
                    last = pe.matmul(st_ps[:, h, :], KTS[:, h, :], VC[:, h, :], start=True, stop=True)
                last.then_inc(s_st, 1)
                pe.wait_ge(s_p, i * NS + NS + 1)
                pe.wait_ge(s_stk, i + 1)
                for h in range(HEADS):
                    pe.matmul(o_ps[:, h, :], VC[:, h, :], SCT[:, h, :], start=True, stop=False)
                    last = pe.matmul(o_ps[:, h, :], ST[:, h, :], QE[:, h, :], start=False, stop=True)
                last.then_inc(s_o, 1)

        @block.scalar
        def _(act):
            for j in range(V_GROUPS):
                act.wait_ge(s_mm, j + 1)
                if j < TT:
                    act.copy(VT[:, j, :], bank[j % 2][:, :]).then_inc(s_out, 1)
                else:
                    act.copy(VM[:, :], bank[j % 2][0:META, :]).then_inc(s_out, 1)
            act.wait_ge(s_lbx, 1)
            act.activation(lbw[:, 0:2, :], lbw[:, 0:2, :], ACT.Exp).then_inc(s_lbe, 1)

            def store(base, k, out, src):
                act.wait_ge(s_mm, base + k)
                act.sem_inc(s_t, 1)
                act.copy(out, src).then_inc(s_out, 1)

            with act.Fori(0, L1) as i:
                base = i * 5 + V_GROUPS
                store(base, 1, FP[:, bass.ds(i, 1), 0:META], bankm[:, 0:META])
                store(base, 2, FP[:, bass.ds(i, 1), META:META + 512], bank[0][:, :])
                store(base, 3, FP[:, bass.ds(i, 1), META + 512:ALL], bank[1][:, :])
                store(base, 4, K.QO[:, bass.ds(i, 1), 0:512], bank[0][:, :])
                store(base, 5, K.QO[:, bass.ds(i, 1), 512:T], bank[1][:, :])

            def logs(n, turn):
                act.wait_ge(s_zz, turn)
                act.activation(EZ[:, :, 0:n], Z[:, :, 0:n], ACT.Exp, scale=-1.0).then_inc(s_ez, 1)
                act.wait_ge(s_fv, turn)
                act.activation(LF[:, :, 0:n], FV[:, :, 0:n], ACT.Ln).then_inc(s_lf, 1)

            logs(META, 1)
            act.wait_ge(s_de, 1)
            act.activation(DK[:, :, 0:META], DK[:, :, 0:META], ACT.Exp).then_inc(s_ee, 1)
            act.wait_ge(s_kt, 1)
            act.copy(KTS[0:META, :, :], kt_ps[0:META, :, :]).then_inc(s_kts, 1)

            with act.Fori(0, L2) as i:
                base = i * 5 + V_GROUPS + 5 * L1
                act.wait_ge(s_oev, i + 1)
                act.sem_inc(s_t, 1)
                act.copy(QS[:, :, :], K.QO[:, :, bass.ds(i * P, P)]).then_inc(s_cp, 1)
                act.copy(VC[:, :, :].rearrange("p h v -> p (h v)"), VT[:, bass.ds(i, 1), :]).then_inc(s_cp, 1)
                logs(P, i + 2)
                store(base, 1, K.CV[:, bass.ds(i, 1), 0:META], bankm[:, 0:META])
                act.wait_ge(s_de, i + 2)
                act.activation(DK[:, :, :], DK[:, :, :], ACT.Exp)
                act.activation(QE[:, :, :], BB[:, :, :], ACT.Exp).then_inc(s_ee, 1)

                def decays(l):
                    act.wait_ge(s_dd, i * len(LEVELS) + l + 1)
                    if l >= 2:
                        act.wait_ge(s_s, i * (len(LEVELS) + 1) + l)
                    act.activation(WW[(l + 1) % 2][:, :, :], DD[l % 2][:, :, :], ACT.Exp).then_inc(s_ww0, 1)

                decays(0)
                store(base, 2, K.CV[:, bass.ds(i, 1), META:META + 512], bank[0][:, :])
                decays(1)
                decays(2)
                store(base, 3, K.CV[:, bass.ds(i, 1), META + 512:ALL], bank[1][:, :])
                decays(3)
                decays(4)
                store(base, 4, K.GB[:, bass.ds(i, 1), 0:512], bank[0][:, :])
                decays(5)
                decays(6)
                act.wait_ge(s_kt, i + 2)
                act.copy(KTS[:, :, :], kt_ps[:, :, :]).then_inc(s_kts, 1)
                store(base, 5, K.GB[:, bass.ds(i, 1), 512:T], bank[1][:, :])
                act.wait_ge(s_o, i + 1)
                act.sem_inc(s_t, 1)
                act.copy(K.QO[:, :, bass.ds(i * P, P)], o_ps[:, :, :]).then_inc(s_oev, 1)

        @block.vector
        def _(dve):
            step = Chain(dve, s_d)
            tt, ts, stt = nc.vector.tensor_tensor, nc.vector.tensor_scalar, nc.vector.scalar_tensor_tensor
            dve.wait_ge(s_lb, 16)
            step(tt(lbw[:, 4, :], lbt[:, 0, :], lbt[:, 1, :], ALU.max))
            tt(lbw[:, 0, :], lbt[:, 0, :], lbw[:, 4, :], ALU.subtract)
            tt(lbw[:, 1, :], lbt[:, 1, :], lbw[:, 4, :], ALU.subtract).then_inc(s_lbx, 1)
            dve.wait_ge(s_lbe, 1)
            step(tt(lbw[:, 4, :], lbw[:, 0, :], lbw[:, 1, :], ALU.add))
            step(nc.vector.reciprocal(lbw[:, 4, :], lbw[:, 4, :]))
            step(tt(lbw[:, 2, :], lbw[:, 0, :], lbw[:, 4, :], ALU.mult))
            step(ts(lbw[:, 3, :], lbw[:, 2, :], -1.0, 1.0, ALU.mult, ALU.add))

            def gates(n, src, turn):
                step(ts(Z[:, :, 0:n], src, Z_LOW, None, ALU.max))
                dve.sem_inc(s_zz, 1)
                dve.wait_ge(s_ez, turn)
                step(ts(SG[:, :, 0:n], EZ[:, :, 0:n], 1.0, None, ALU.add))
                step(nc.vector.reciprocal(SG[:, :, 0:n], SG[:, :, 0:n]))
                tt(FV[:, :, 0:n], SG[:, :, 0:n], bcast(oml, n), ALU.mult)
                step(tt(KK[:, :, 0:n], EZ[:, :, 0:n], SG[:, :, 0:n], ALU.mult))
                tt(FV[:, :, 0:n], FV[:, :, 0:n], bcast(lb, n), ALU.add).then_inc(s_fv, 1)
                step(tt(KK[:, :, 0:n], KK[:, :, 0:n], bcast(oml, n), ALU.mult))
                dve.wait_ge(s_lf, turn)

            def end_log(n):
                step(tt(DK[:, :, 0:n], BB[:, :, n - 1:n].to_broadcast([P, HEADS, n]), BB[:, :, 0:n], ALU.subtract))
                dve.sem_inc(s_de, 1)

            dve.wait_ge(s_out, V_GROUPS + 5 * L1)
            dve.wait_ge(s_cst, 1 + len(LEVELS))
            gates(META, FP[:, :, 0:META], 1)
            for h in range(HEADS):
                last = nc.vector.tensor_tensor_scan(BB[:, h, 0:META], restart[:, h, 0:META], LF[:, h, 0:META], 0.0,
                                                    ALU.mult, ALU.add)
            step(last)
            end_log(META)
            dve.wait_ge(s_ee, 1)
            step(tt(KE[:, :, 0:META], KK[:, :, 0:META], DK[:, :, 0:META], ALU.mult))
            dve.sem_inc(s_ke, 1)
            dve.wait_ge(s_st, 1)
            step(nc.vector.tensor_copy(ST[:, :, :], st_ps[:, :, :]))
            dve.sem_inc(s_stk, 1)
            dve.sem_inc(s_oev, 1)
            dve.sem_inc(s_p, 1)

            def halves(x, half):
                v = x.rearrange("p h (b z r) -> p (h b) z r", z=2, r=half)
                return v[:, :, 0, :], v[:, :, 1, :]

            with dve.Fori(0, L2) as i:
                step.enter(i, 18)
                NL = len(LEVELS)
                dve.wait_ge(s_oev, i + 1)
                dve.sem_inc(s_t, 1)
                gates(P, FP[:, :, bass.ds(i * P + META, P)], i + 2)
                step(nc.vector.tensor_tensor_scan(BB[:, :, :].rearrange("p h t -> p (h t)"),
                                                  restart[:, :, :].rearrange("p h t -> p (h t)"),
                                                  LF[:, :, :].rearrange("p h t -> p (h t)"), 0.0, ALU.mult, ALU.add))
                dve.wait_ge(s_cp, i * 2 + 2)
                dve.sem_inc(s_kq, 1)
                end_log(P)

                def logs(l):
                    half = LEVELS[l]
                    n = HEADS * 64 // half
                    (b0, b1), (d0, d1) = halves(BB[:, :, :], half), halves(DD[l % 2], half)
                    ref = b0[:, :, half - 1:half].to_broadcast([P, n, half])
                    tt(d0, ref, b0, ALU.subtract)
                    tt(d1, b1, ref, ALU.subtract).then_inc(s_dd, 1)

                def factors(l):
                    half = LEVELS[l]
                    w0, w1 = halves(WW[(l + 1) % 2], half)
                    dve.wait_ge(s_ww0, i * NL + l + 1)
                    tt(w0, w0, halves(KK[:, :, :], half)[0], ALU.mult)
                    tt(w1, w1, halves(QS[:, :, :], half)[1], ALU.mult).then_inc(s_ww, 1)

                def keep_scores(l):
                    half = LEVELS[l]
                    dve.wait_ge(s_s, i * (NL + 1) + l + 2)
                    dve.sem_inc(s_t, 1)
                    _, late = halves(SCT[:, :, :], half)
                    bank_v = sc[(l + 1) % 2][:, 0:HEADS * 64].rearrange("p (b r) -> p b r", r=half)
                    mask_v = masks[:, l, :].rearrange("p (b r) -> p b r", r=half)
                    step(nc.vector.copy_predicated(late, mask_v, bank_v))
                    dve.sem_inc(s_p, 1)

                logs(0)
                logs(1)
                dve.wait_ge(s_s, i * (NL + 1) + 1)
                step(tt(SCT[:, :, :], sc[0][:, :].rearrange("p (h t) -> p h t", h=HEADS),
                        K.ident[:, :].rearrange("p (o t) -> p o t", o=1).to_broadcast([P, HEADS, P]), ALU.mult))
                dve.sem_inc(s_p, 1)
                dve.wait_ge(s_ee, i + 2)
                step(nc.vector.tensor_copy(blast[:, :].rearrange("p (h o) -> p h o", o=1), QE[:, :, P - 1:P]))
                tt(QE[:, :, :], QE[:, :, :], QS[:, :, :], ALU.mult)
                step(tt(KE[:, :, :], KK[:, :, :], DK[:, :, :], ALU.mult))
                dve.sem_inc(s_ke, 1)
                for l in range(NL):
                    factors(l)
                    if l + 2 < NL:
                        logs(l + 2)
                    if l >= 1:
                        keep_scores(l - 1)
                keep_scores(NL - 1)
                dve.wait_ge(s_st, i + 2)
                dve.wait_ge(s_o, i + 1)
                for h in range(HEADS):
                    last = stt(ST[:, h, :], ST[:, h, :], blast[:, h:h + 1], st_ps[:, h, :], ALU.mult, ALU.add)
                step(last)
                dve.sem_inc(s_stk, 1)
            step.leave(L2)


def phase_out(nc, ins, K, h2_d, xn2_d):
    w_out = ins["w_out"].rearrange("l (c p) n -> p (l c) n", p=P)
    x = ins["x"].rearrange("b (j p) n -> p (b j) n", p=P)
    G, B = K.GB[:, 0:HEADS, :], K.GB[:, HEADS:2 * HEADS, :]
    C, V = K.CV[:, 0:HEADS, :], K.CV[:, HEADS:2 * HEADS, :]
    with ExitStack() as ctx:
        def sb(name, shape, dt=F32):
            return ctx.enter_context(nc.sbuf_tensor(name, shape, dt))

        def ps(name, shape):
            return ctx.enter_context(nc.psum_tensor(name, shape, F32))
        sem = lambda n: ctx.enter_context(nc.semaphore(n))
        wo = sb("wo", [P, KT, D])
        gffn = sb("gffn", [P, D])
        cw = sb("cw", [P, 3, HEADS])
        ng = sb("ng", [P, 2, HEADS])
        H = [sb(f"H{i}", [P, D]) for i in range(2)]
        X2 = [sb(f"X2{i}", [P, D]) for i in range(2)]
        sg = sb("sg", [P, D])
        zrow = sb("zrow", [P, D])
        Y = [sb(f"Y{i}", [P, 2 * HEADS, P]) for i in range(2)]
        SQ = sb("SQ", [P, 2 * HEADS, P])
        RT = sb("RT", [P, 2 * HEADS, P])
        taps = [sb(f"tap{i}", [P, HEADS, P]) for i in range(3)]
        sh = sb("sh", [P, 2 * TT])
        junk = sb("junk2", [P, D])
        ms = [ps(f"ms{i}", [P, HEADS, P]) for i in range(2)]
        op = [ps(f"op{i}", [P, 512]) for i in range(2)]
        tr = [ps(f"tr{i}", [P, 4, P]) for i in range(2)]
        s_wo, s_c, s_z = sem("wo_in"), sem("vectors_in"), sem("zero_row")
        s_h = [sem(f"h_in{i}") for i in range(2)]
        s_sig, s_gate = sem("sigmoids"), sem("gates_on")
        s_pool, s_u, s_conv = sem("pool_steps"), sem("u_ready"), sem("conv_ready")
        s_yc, s_sq, s_ms, s_rt = sem("conv_gated"), sem("squares"), sem("mean_squares"), sem("roots")
        s_y, s_op, s_h2 = sem("mixed"), sem("out_projected"), sem("residual_added")
        s_s2, s_r2, s_x2 = sem("squares_summed2"), sem("root2"), sem("xn2_ready")
        s_t2, s_e2, s_st = sem("xn2_turned"), sem("xn2_kept"), sem("rows_written")
        s_d = sem("dve_steps2")
        block = ctx.enter_context(nc.Block())
        h2v = h2_d[0:T, :].rearrange("(j p) n -> p j n", p=P)
        xn2v = xn2_d[0:T, :].rearrange("(j p) n -> p j n", p=P)

        @block.sync
        def _(sp):
            for k in range(2):
                sp.dma_start(H[k][:, :], x[:, k, :]).then_inc(s_h[k], 16)
            sp.dma_start(cw[:, :, :].rearrange("p k h -> p (k h)"), ins["conv_w"].rearrange("l k (h p) -> p (l k h)", p=P),
                         allow_slow_non_contiguous=True).then_inc(s_c, 16)
            for k, name in enumerate(("hgrn_norm_g", "conv_norm_g")):
                sp.dma_start(ng[:, k, :], ins[name].rearrange("l (h p) -> p (l h)", p=P),
                             allow_slow_non_contiguous=True).then_inc(s_c, 16)
            sp.dma_start(wo[:, :, :], w_out).then_inc(s_wo, 16)
            sp.dma_start(gffn[:, :], ins["norm_ffn_g"].to_broadcast([P, D])).then_inc(s_c, 16)
            sp.wait_ge(s_z, 1)
            for base in range(T, T + CAP, P):
                n = min(P, T + CAP - base)
                sp.dma_start(xn2_d[base:base + n, :], zrow[0:n, :]).then_inc(s_st, 16)
                sp.dma_start(h2_d[base:base + n, :], zrow[0:n, :]).then_inc(s_st, 16)
            for j in range(TT):
                sp.wait_ge(s_x2, j + 1)
                sp.dma_start(h2v[:, j, :], H[j % 2][:, :]).then_inc(s_st, 16)
                sp.dma_start(xn2v[:, j, :], X2[j % 2][:, :]).then_inc(s_st, 16)
                if j + 2 < TT:
                    sp.wait_ge(s_st, 16 * (4 + 2 * (j + 1)))
                    sp.dma_start(H[j % 2][:, :], x[:, j + 2, :]).then_inc(s_h[j % 2], 16)
            sp.wait_ge(s_st, 16 * (4 + 2 * TT))

        @block.gpsimd
        def _(pool):
            pool.memset(zrow[:, :], 0.0).then_inc(s_z, 1)
            pool.wait_ge(s_c, 64)
            n = 0
            last = None
            for a in range(META - 2, ALL, 257):
                u = slice(a, min(a + 257, ALL))
                last = pool.tensor_tensor(C[:, :, u], C[:, :, u], V[:, :, u], ALU.mult)
            last.then_inc(s_pool, 1)
            n += 1
            for j in range(TT):
                pool.wait_ge(s_pool, n)
                if j:
                    pool.wait_ge(s_yc, j)
                for k in range(3):
                    u = C[:, :, META - 2 + k + j * P:META - 2 + k + j * P + P]
                    pool.tensor_tensor(taps[k][:, :, :], u, bcast(cw[:, k, :], P), ALU.mult).then_inc(s_pool, 1)
                n += 3
                pool.wait_ge(s_pool, n)
                pool.tensor_tensor(taps[0][:, :, :], taps[0][:, :, :], taps[1][:, :, :], ALU.add).then_inc(s_pool, 1)
                n += 1
                pool.wait_ge(s_pool, n)
                pool.tensor_tensor(taps[2][:, :, :], taps[0][:, :, :], taps[2][:, :, :], ALU.add).then_inc(s_conv, 1)

        @block.tensor
        def _(pe):
            def means(j):
                pe.wait_ge(s_sq, 2 * (j + 1))
                if j:
                    pe.wait_ge(s_rt, j)
                for k in range(2):
                    last = pe.matmul(ms[k][:, :, :].rearrange("p h t -> p (h t)"), K.ones[:, :],
                                     SQ[:, HEADS * k:HEADS * k + HEADS, :].rearrange("p h t -> p (h t)"), start=True, stop=True)
                last.then_inc(s_ms, 1)

            def turn(j):
                pe.wait_ge(s_x2, j + 1)
                if j:
                    pe.wait_ge(s_e2, j)
                rows = X2[j % 2][:, :].rearrange("p (k t) -> p t k", t=KT)
                for t in range(KT):
                    last = pe.transpose(tr[t // 4][:, t % 4, :], rows[:, t, :], K.ident[:, :])
                last.then_inc(s_t2, 1)

            means(0)
            pe.wait_ge(s_wo, 16)
            for j in range(TT):
                if j + 1 < TT:
                    means(j + 1)
                pe.wait_ge(s_y, j + 1)
                if j:
                    pe.wait_ge(s_h2, j)
                for half in range(2):
                    for c in range(KT):
                        last = pe.matmul(op[half][:, :], Y[j % 2][:, c, :], wo[:, c, 512 * half:512 * half + 512],
                                         start=(c == 0), stop=(c == KT - 1))
                last.then_inc(s_op, 1)
                if j:
                    turn(j - 1)
            turn(TT - 1)

        @block.scalar
        def _(act):
            for h in range(HEADS):
                if h:
                    act.wait_ge(s_gate, h)
                act.activation(sg[:, :], G[:, h, :], ACT.Sigmoid).then_inc(s_sig, 1)

            def squares(j):
                if j:
                    act.wait_ge(s_ms, j)
                act.activation(SQ[:, 0:HEADS, :], K.QO[:, :, j * P:j * P + P], ACT.Square).then_inc(s_sq, 1)
                act.wait_ge(s_yc, j + 1)
                act.activation(SQ[:, HEADS:2 * HEADS, :], Y[j % 2][:, HEADS:2 * HEADS, :], ACT.Square).then_inc(s_sq, 1)

            def roots(j):
                act.wait_ge(s_ms, j + 1)
                if j:
                    act.wait_ge(s_y, j)
                for k in range(2):
                    last = act.activation(RT[:, HEADS * k:HEADS * k + HEADS, :], ms[k][:, :, :], ACT.Sqrt,
                                          bias=K.eps[:, 0:1], scale=1.0 / P)
                last.then_inc(s_rt, 1)

            squares(0)
            roots(0)
            for j in range(TT):
                if j + 1 < TT:
                    squares(j + 1)
                    roots(j + 1)
                if j:
                    act.wait_ge(s_t2, j)
                    for k in range(2):
                        last = act.copy(K.xT[:, 4 * k:4 * k + 4, (j - 1) * P:j * P], tr[k][:, :, :])
                    last.then_inc(s_e2, 1)
                act.wait_ge(s_h2, j + 1)
                if j:
                    act.wait_ge(s_s2, j)
                act.activation(junk[:, :], H[j % 2][:, :], ACT.Square, accum_out=sh[:, j:j + 1]).then_inc(s_s2, 1)
                act.wait_ge(s_s2, j + 1)
                act.activation(sh[:, TT + j:TT + j + 1], sh[:, j:j + 1], ACT.Sqrt, bias=K.eps[:, 0:1], scale=1.0 / D).then_inc(s_r2, 1)
            act.wait_ge(s_t2, TT)
            for k in range(2):
                last = act.copy(K.xT[:, 4 * k:4 * k + 4, (TT - 1) * P:T], tr[k][:, :, :])
            last.then_inc(s_e2, 1)

        @block.vector
        def _(dve):
            step = Chain(dve, s_d)
            tt, stt = nc.vector.tensor_tensor, nc.vector.scalar_tensor_tensor
            dve.wait_ge(s_c, 64)
            for h in range(HEADS):
                dve.wait_ge(s_sig, h + 1)
                stt(G[:, h, :], G[:, h, :], ng[:, 0, h:h + 1], sg[:, :], ALU.mult, ALU.mult).then_inc(s_gate, 1)

            def conv_gate(j):
                dve.wait_ge(s_conv, j + 1)
                if j >= 2:
                    dve.wait_ge(s_op, j - 1)
                tt(Y[j % 2][:, HEADS:2 * HEADS, :], taps[2][:, :, :], B[:, :, j * P:j * P + P], ALU.mult).then_inc(s_yc, 1)

            def mix(j):
                dve.wait_ge(s_rt, j + 1)
                tt_y = Y[j % 2]
                nc.vector.reciprocal(RT[:, 0:HEADS, :], RT[:, 0:HEADS, :])
                step(nc.vector.reciprocal(RT[:, HEADS:, :], RT[:, HEADS:, :]))
                tt(tt_y[:, 0:HEADS, :], K.QO[:, :, j * P:j * P + P], RT[:, 0:HEADS, :], ALU.mult)
                step(tt(tt_y[:, HEADS:, :], tt_y[:, HEADS:, :], RT[:, HEADS:, :], ALU.mult))
                tt(tt_y[:, 0:HEADS, :], tt_y[:, 0:HEADS, :], G[:, :, j * P:j * P + P], ALU.mult)
                tt(tt_y[:, HEADS:, :], tt_y[:, HEADS:, :], bcast(ng[:, 1, :], P), ALU.mult).then_inc(s_y, 1)

            conv_gate(0)
            dve.wait_ge(s_gate, HEADS)
            mix(0)
            for j in range(TT):
                if j + 1 < TT:
                    conv_gate(j + 1)
                    mix(j + 1)
                dve.wait_ge(s_op, j + 1)
                dve.wait_ge(s_h[j % 2], 16 * (j // 2 + 1))
                for half in range(2):
                    cols = slice(512 * half, 512 * half + 512)
                    last = tt(H[j % 2][:, cols], H[j % 2][:, cols], op[half][:, :], ALU.add)
                last.then_inc(s_h2, 1)
                dve.wait_ge(s_r2, j + 1)
                step(nc.vector.reciprocal(sh[:, TT + j:TT + j + 1], sh[:, TT + j:TT + j + 1]))
                if j >= 2:
                    dve.wait_ge(s_t2, j - 1)
                    dve.wait_ge(s_st, 16 * (4 + 2 * (j - 1)))
                stt(X2[j % 2][:, :], H[j % 2][:, :], sh[:, TT + j:TT + j + 1], gffn[:, :], ALU.mult, ALU.mult).then_inc(s_x2, 1)


def phase_route(nc, ins, K, h2_d, acc_d, tbl_d):
    NE = TT * E_N
    with ExitStack() as ctx:
        def sb(name, shape, dt=F32):
            return ctx.enter_context(nc.sbuf_tensor(name, shape, dt))

        def ps(name, shape):
            return ctx.enter_context(nc.psum_tensor(name, shape, F32))
        sem = lambda n: ctx.enter_context(nc.semaphore(n))
        wr = sb("wr", [P, KT, E_N])
        bias = sb("bias", [P, E_N])
        wgs, wus = sb("wgs", [P, KT, FF]), sb("wus", [P, KT, FF])
        wds = sb("wds", [P, 2, D])
        SC, BI, RE, MK, GT, SL, T1 = (sb(n, [P, TT, E_N]) for n in ("SC", "BI", "RE", "MK", "GT", "SL", "T1"))
        MS = sb("MS", [P, TT, E_N])
        m8 = sb("m8", [P, TT, TOPK])
        s8 = sb("s8", [P, TT, TOPK])
        si = sb("si", [P, TT * TOPK], I32)
        junk = sb("junk3", [P, E_N])
        pay = sb("pay", [P, TT, TOPK, 2])
        gs = sb("gs", [P, TT])
        before = sb("before", [P, P])
        cnt, ext, inc, b0, ba = (sb(n, [P, E_N]) for n in ("cnt", "ext", "inc", "b0", "ba"))
        e0 = sb("e0", [P, E_N])
        zero = sb("zero", [P, E_N])
        pidx = sb("pidx", [P, 1])
        tex = sb("tex", [P, 1])
        exrow = sb("exrow", [1, ITEMS])
        twos = sb("twos", [1, 32])
        pr = sb("pr", [1, 1])
        tj = sb("tj", [1, 32])
        fill = sb("fill", [ITEMS, CAP, 2])
        tbl = sb("tbl", [ITEMS, CAP, 2])
        hs = sb("hs", [P, 2, T])
        sgs = sb("sgs", [P, 512])
        H = [sb(f"HH{i}", [P, D]) for i in range(2)]
        lg, rk, ct = ps("lg", [P, TT, E_N]), ps("rk", [P, TT, E_N]), ps("ct", [P, 512])
        gp, up = ps("gp", [P, 512]), ps("up", [P, 512])
        yp = [ps(f"yp{i}", [P, 512]) for i in range(2)]
        tp = ps("tp", [P, 512])
        s_w, s_ws, s_wd = sem("router_in"), sem("shared_in"), sem("shared_down_in")
        s_k0, s_k = sem("patterns_cleared"), sem("patterns_set")
        s_fi, s_fo = sem("table_blank"), sem("table_blank_written")
        s_lg, s_sc, s_mk, s_rk = sem("logits"), sem("sigmoids_r"), sem("chosen"), sem("ranks")
        s_pay, s_sca, s_ti = sem("payload"), sem("table_scattered"), sem("table_in")
        s_tp, s_tk, s_ex, s_er = sem("table_turned"), sem("table_kept"), sem("experts_counted"), sem("experts_row")
        s_gu, s_sg, s_gv, s_hs = sem("gate_up"), sem("sig_shared"), sem("silu_shared"), sem("hidden_shared")
        s_y, s_a, s_ao = sem("shared_out"), sem("acc_tile"), sem("acc_written")
        s_h = [sem(f"h2_in{i}") for i in range(2)]
        s_d = sem("dve_steps3")
        s_up = sem("up_done")
        block = ctx.enter_context(nc.Block())
        h2v = h2_d[0:T, :].rearrange("(j p) n -> p j n", p=P)
        accv = acc_d[0:T, :].rearrange("(j p) n -> p j n", p=P)
        tbl_rows = tbl_d.rearrange("(i c) w -> i (c w)", c=CAP)

        @block.sync
        def _(sp):
            sp.dma_start(wr[:, :, :], ins["w_router"].rearrange("l (p t) n -> p (l t) n", t=KT)).then_inc(s_w, 16)
            sp.dma_start(bias[:, :], ins["router_bias"].to_broadcast([P, E_N])).then_inc(s_w, 16)
            sp.dma_start(wgs[:, :, :], ins["w_gate_s"].rearrange("l (p t) n -> p (l t) n", t=KT)).then_inc(s_ws, 16)
            sp.dma_start(wus[:, :, :], ins["w_up_s"].rearrange("l (p t) n -> p (l t) n", t=KT)).then_inc(s_ws, 16)
            sp.dma_start(wds[:, :, :], ins["w_down_s"].rearrange("l (f p) n -> p (l f) n", p=P)).then_inc(s_wd, 16)
            sp.wait_ge(s_fi, 2)
            sp.dma_start(tbl_rows, fill[:, :, :].rearrange("i c w -> i (c w)")).then_inc(s_fo, 16)
            sp.dma_start(acc_d[T:T + CAP, :], h2_d[T:T + CAP, :]).then_inc(s_ao, 16)
            for j in range(TT):
                if j >= 2:
                    sp.wait_ge(s_ao, 16 * j)
                sp.dma_start(H[j % 2][:, :], h2v[:, j, :]).then_inc(s_h[j % 2], 16)
                if j:
                    sp.wait_ge(s_a, j)
                    sp.dma_start(accv[:, j - 1, :], H[(j - 1) % 2][:, :]).then_inc(s_ao, 16)
            sp.wait_ge(s_a, TT)
            sp.dma_start(accv[:, TT - 1, :], H[(TT - 1) % 2][:, :]).then_inc(s_ao, 16)
            sp.wait_ge(s_ao, 16 * (TT + 1))
            sp.wait_ge(s_sca, 16 * TT * TOPK)
            sp.dma_start(tbl[:, :, :].rearrange("i c w -> i (c w)"), tbl_rows).then_inc(s_ti, 16)
            sp.wait_ge(s_ti, 16)

        @block.gpsimd
        def _(pool):
            pool.memset(before[:, :], 1.0).then_inc(s_k0, 1)
            pool.memset(fill[:, :, 1:2], 0.0).then_inc(s_fi, 1)
            pool.iota(fill[:, :, 0], [[1, CAP]], base=T, channel_multiplier=0, allow_small_or_imprecise_dtypes=True).then_inc(s_fi, 1)
            pool.memset(zero[:, :], 0.0).then_inc(s_k, 1)
            pool.iota(e0[:, :], [[CAP, E_N]], base=0, channel_multiplier=0, allow_small_or_imprecise_dtypes=True).then_inc(s_k, 1)
            pool.iota(pidx[:, :], [[0, 1]], base=0, channel_multiplier=1, allow_small_or_imprecise_dtypes=True).then_inc(s_k, 1)
            pool.iota(exrow[:, 0:E_N], [[1, E_N]], base=0, channel_multiplier=0, allow_small_or_imprecise_dtypes=True).then_inc(s_k, 1)
            pool.iota(twos[:, :], [[2, 32]], base=0, channel_multiplier=0, allow_small_or_imprecise_dtypes=True).then_inc(s_k, 1)
            pool.iota(pay[:, :, :, 0], [[P, TT], [0, TOPK]], base=0, channel_multiplier=1,
                      allow_small_or_imprecise_dtypes=True).then_inc(s_k, 1)
            pool.wait_ge(s_k0, 1)
            pool.affine_select(out=before[:, :], in_=before[:, :], compare_op=ALU.is_gt, fill=0.0,
                               base=0, pattern=[[1, P]], channel_multiplier=-1).then_inc(s_k, 1)
            pool.wait_ge(s_fo, 16)
            for j in range(TT):
                pool.wait_ge(s_pay, j + 1)
                for k in range(TOPK):
                    pool.indirect_dma_start(tbl_d, bass.IndirectOffsetOnAxis(ap=si[:, j * TOPK + k:j * TOPK + k + 1], axis=0),
                                            pay[:, j, k, :], None).then_inc(s_sca, 16)
            pool.wait_ge(s_sca, 16 * TT * TOPK)

        @block.tensor
        def _(pe):
            pe.wait_ge(s_w, 32)
            for j in range(TT):
                for t in range(KT):
                    last = pe.matmul(lg[:, j, :], K.xT[:, t, j * P:j * P + P], wr[:, t, :], start=(t == 0), stop=(t == KT - 1))
            last.then_inc(s_lg, 1)

            def hidden(b, f):
                g = 2 * b + f
                if g:
                    pe.wait_ge(s_hs, g)
                for w, out in ((wgs, gp), (wus, up)):
                    for t in range(KT):
                        last = pe.matmul(out[:, :], w[:, t, f * P:f * P + P], K.xT[:, t, 512 * b:512 * b + 512],
                                         start=(t == 0), stop=(t == KT - 1))
                    last.then_inc(s_gu if out is gp else s_up, 1)

            pe.wait_ge(s_ws, 32)
            hidden(0, 0)
            pe.wait_ge(s_k, 7)
            pe.wait_ge(s_mk, 1)
            for j in range(TT):
                last = pe.matmul(rk[:, j, :], before[:, :], MK[:, j, :], start=True, stop=(j == 0))
                if j:
                    last = pe.matmul(rk[:, j, :], K.ones[:, :], MS[:, j - 1, :], start=False, stop=True)
            last = pe.matmul(ct[:, 0:E_N], K.ones[:, :], MS[:, TT - 1, :], start=True, stop=True)
            last.then_inc(s_rk, 1)
            hidden(0, 1)
            pe.wait_ge(s_ex, 1)
            pe.matmul(tp[0:1, 0:ITEMS - E_N], tex[:, 0:1], K.ident[:, 0:ITEMS - E_N], start=True, stop=True).then_inc(s_er, 1)
            hidden(1, 0)
            hidden(1, 1)
            pe.wait_ge(s_wd, 16)
            for j in range(TT):
                if j % 4 == 0:
                    pe.wait_ge(s_hs, 2 * (j // 4) + 2)
                if j:
                    pe.wait_ge(s_a, j)
                for half in range(2):
                    for f in range(2):
                        last = pe.matmul(yp[half][:, :], hs[:, f, j * P:j * P + P], wds[:, f, 512 * half:512 * half + 512],
                                         start=(f == 0), stop=(f == 1))
                last.then_inc(s_y, 1)
            pe.wait_ge(s_ti, 16)
            pe.wait_ge(s_tk, 1)
            for k in range(2):
                pe.transpose(tp[0:P, k * ITEMS:(k + 1) * ITEMS], tbl[:, 0:P, k], K.ident[0:ITEMS, 0:ITEMS])
                last = pe.transpose(tp[0:CAP1, (2 + k) * ITEMS:(3 + k) * ITEMS], tbl[:, P:CAP, k], K.ident[0:ITEMS, 0:ITEMS])
            last.then_inc(s_tp, 1)

        @block.scalar
        def _(act):
            act.wait_ge(s_lg, 1)
            act.activation(SC[:, :, :], lg[:, :, :], ACT.Sigmoid).then_inc(s_sc, 1)
            for g in range(4):
                act.wait_ge(s_gu, g + 1)
                if g:
                    act.wait_ge(s_gv, g)
                act.activation(sgs[:, :], gp[:, :], ACT.Sigmoid).then_inc(s_sg, 1)

        @block.vector
        def _(dve):
            step = Chain(dve, s_d)
            tt, ts, stt = nc.vector.tensor_tensor, nc.vector.tensor_scalar, nc.vector.scalar_tensor_tensor

            def shared(g):
                b, f = divmod(g, 2)
                dve.wait_ge(s_sg, g + 1)
                tt(sgs[:, :], sgs[:, :], gp[:, :], ALU.mult).then_inc(s_gv, 1)
                dve.wait_ge(s_gv, g + 1)
                dve.wait_ge(s_up, g + 1)
                tt(hs[:, f, 512 * b:512 * b + 512], sgs[:, :], up[:, :], ALU.mult).then_inc(s_hs, 1)

            def over_tiles(v):
                return v[:, :].rearrange("p (o e) -> p o e", o=1).to_broadcast([P, TT, E_N])

            dve.wait_ge(s_k, 7)
            dve.wait_ge(s_w, 32)
            dve.wait_ge(s_sc, 1)
            step(tt(BI[:, :, :], SC[:, :, :], over_tiles(bias), ALU.add))
            for j in range(TT):
                last = nc.vector.max(m8[:, j, :], BI[:, j, :])
            step(last)
            for j in range(TT):
                last = nc.vector.match_replace(RE[:, j, :], m8[:, j, :], BI[:, j, :], -1e30)
            step(last)
            step(tt(MK[:, :, :], RE[:, :, :], BI[:, :, :], ALU.not_equal))
            step(nc.vector.tensor_copy(MS[:, 0, :], MK[:, 0, :]))
            for j in range(1, TT):
                step(tt(MS[:, j, :], MS[:, j - 1, :], MK[:, j, :], ALU.add))
            dve.sem_inc(s_mk, 1)
            step(tt(GT[:, :, :], SC[:, :, :], MK[:, :, :], ALU.mult))
            step(nc.vector.reduce_sum(gs[:, :], GT[:, :, :], mybir.AxisListType.X))
            step(nc.vector.reciprocal(gs[:, :], gs[:, :]))
            step(tt(GT[:, :, :], GT[:, :, :], bcast(gs[:, :], E_N), ALU.mult))
            step(ts(GT[:, :, :], GT[:, :, :], ROUTED_SCALE, None, ALU.mult))
            dve.wait_ge(s_rk, 1)
            step(nc.vector.tensor_copy(cnt[:, :], ct[:, 0:E_N]))
            step(ts(ext[:, :], cnt[:, :], float(CAP), None, ALU.is_gt))
            for m in range(2, MORE + 1):
                step(stt(ext[:, :], cnt[:, :], float(m * CAP), ext[:, :], ALU.is_gt, ALU.add))
            step(nc.vector.tensor_tensor_scan(inc[:, :], ext[:, :], zero[:, :], 0.0, ALU.add, ALU.add))
            step(tt(b0[:, :], inc[:, :], ext[:, :], ALU.subtract))
            step(ts(b0[:, :], b0[:, :], float(CAP), float((E_N - 1) * CAP), ALU.mult, ALU.add))
            step(tt(ba[:, :], b0[:, :], e0[:, :], ALU.subtract))
            step(ts(T1[:, :, :], rk[:, :, :], float(CAP), None, ALU.is_ge))
            step(tt(T1[:, :, :], T1[:, :, :], over_tiles(ba), ALU.mult))
            step(tt(T1[:, :, :], T1[:, :, :], over_tiles(e0), ALU.add))
            step(tt(SL[:, :, :], rk[:, :, :], T1[:, :, :], ALU.add))
            step(stt(SL[:, :, :], SL[:, :, :], 1.0, MK[:, :, :], ALU.add, ALU.mult))
            step(ts(SL[:, :, :], SL[:, :, :], -1.0, None, ALU.add))
            for j in range(TT):
                last = nc.vector.max(s8[:, j, :], SL[:, j, :])
            step(last)
            step(nc.vector.tensor_copy(si[:, :], s8[:, :, :].rearrange("p j k -> p (j k)")))
            for j in range(TT):
                for k in range(TOPK):
                    step(stt(junk[:, :], SL[:, j, :], s8[:, j, k:k + 1], GT[:, j, :], ALU.is_equal, ALU.mult,
                             accum_out=pay[:, j, k, 1:2]))
                dve.sem_inc(s_pay, 1)
                if j == 0:
                    step(ts(junk[:, :], inc[:, :], pidx[:, 0:1], None, ALU.is_le))
                    step(nc.vector.reduce_sum(tex[:, :], junk[:, :], mybir.AxisListType.X))
                    step(ts(tex[:, :], tex[:, :], float(E_N - 1), None, ALU.min))
                    dve.sem_inc(s_ex, 1)
                    shared(0)
                if j == 3:
                    shared(1)
            dve.wait_ge(s_er, 1)
            step(nc.vector.tensor_copy(exrow[:, E_N:ITEMS], tp[0:1, 0:ITEMS - E_N]))
            step(nc.vector.tensor_copy(K.expert[:, :], exrow[:, :]))
            step(ts(tj[:, :], twos[:, :], inc[0:1, E_N - 1:E_N], None, ALU.is_lt))
            step(nc.vector.reduce_sum(pr[:, :], tj[:, :], mybir.AxisListType.X))
            step(ts(pr[:, :], pr[:, :], float(E_N // 2 - 1), None, ALU.add))
            step(nc.vector.tensor_copy(K.pairs[:, :], pr[:, :]))
            dve.sem_inc(s_tk, 1)
            shared(2)
            shared(3)
            for j in range(TT):
                dve.wait_ge(s_y, j + 1)
                dve.wait_ge(s_h[j % 2], 16 * (j // 2 + 1))
                for half in range(2):
                    cols = slice(512 * half, 512 * half + 512)
                    last = tt(H[j % 2][:, cols], H[j % 2][:, cols], yp[half][:, :], ALU.add)
                last.then_inc(s_a, 1)
            dve.wait_ge(s_tp, 1)
            for k, n in ((0, P), (1, CAP1)):
                nc.vector.tensor_copy(K.idx[k][:, :], tp[0:n, 2 * k * ITEMS:(2 * k + 1) * ITEMS])
                step(nc.vector.tensor_copy(K.gate[k][:, :], tp[0:n, (2 * k + 1) * ITEMS:(2 * k + 2) * ITEMS]))


def phase_experts(nc, ins, K, xn2_d, acc_d):
    wg_d = ins["w_gate_e"].rearrange("l e (p t) f -> p (l e) t f", t=KT)
    wu_d = ins["w_up_e"].rearrange("l e (p t) f -> p (l e) t f", t=KT)
    wd_d = ins["w_down_e"].rearrange("l e (f p) n -> p (l e) f n", p=P)
    with ExitStack() as ctx:
        def sb(name, shape, dt=F32):
            return ctx.enter_context(nc.sbuf_tensor(name, shape, dt))

        def ps(name, shape):
            return ctx.enter_context(nc.psum_tensor(name, shape, F32))
        sem = lambda n: ctx.enter_context(nc.semaphore(n))
        two = range(2)
        WR = [[sb(f"WR{i}{k}", [P, KT * FF]) for k in range(3)] for i in two]
        WH = [[sb(f"WH{i}{k}", [P, KT * FF], F32R) for k in range(3)] for i in two]
        WL = [[sb(f"WL{i}{k}", [P, KT * FF], F32R) for k in range(3)] for i in two]
        XG = [(sb(f"XG{i}", [P, D]), sb(f"XH{i}", [CAP1, D])) for i in two]
        XS = [sb(f"XS{i}", [P, KT, 2, CAP], F32R) for i in two]
        GS, US, SS, HF = (sb(n, [P, 2, CAP]) for n in ("GS", "US", "SS", "HF"))
        HH = [sb(f"hidh{i}", [P, 2, 2 * P], F32R) for i in two]
        HL = [sb(f"hidr{i}", [P, 2, 2 * P], F32R) for i in two]
        YE = (sb("YE", [P, D]), sb("YF", [CAP1, D]))
        gi = [(sb(f"gi{i}", [P, 1], I32), sb(f"gj{i}", [CAP1, 1], I32)) for i in two]
        si = [(sb(f"sia{i}", [P, 1], I32), sb(f"sib{i}", [CAP1, 1], I32)) for i in two]
        gt = [(sb(f"gta{i}", [P, 1]), sb(f"gtb{i}", [CAP1, 1])) for i in two]
        gu = [ps(f"gu{f}", [P, 2, CAP]) for f in range(3)]
        gu.append(gu[0])
        xp = [ps(f"xp{i}", [P, 3, CAP]) for i in two]
        yp = [ps(f"ype{h}", [P, 512]) for h in range(3)]
        yp.append(yp[0])
        s_raw = [[sem(f"weights_in{i}{k}") for k in range(3)] for i in two]
        s_hi, s_lo = sem("gate_up_high"), sem("gate_up_low")
        s_dhi, s_dlo = sem("down_high"), sem("down_low")
        s_pi, s_g = sem("pool_copies"), [sem(f"gathered{i}") for i in two]
        s_gt, s_ad, s_free = sem("gates_set"), sem("rows_added"), sem("rows_free")
        s_tp, s_xh, s_xl = sem("x_turned"), sem("x_high"), sem("x_low")
        s_gu, s_ss, s_he, s_hc, s_z = sem("gate_up_done"), sem("sig_e"), sem("hidden_e"), sem("hidden_steps"), sem("hidden_zeroed")
        s_y, s_ya, s_gk = sem("y_done"), sem("y_kept"), sem("gate_up_kept")
        turn = {e: sem(f"turn_{e}") for e in ("sp", "pool")}
        block = ctx.enter_context(nc.Block())
        LIMIT = ITEMS // 2 - 1
        WIDE = KT * FF
        PIECES = [(0, 0, WIDE), (1, 0, WIDE // 2), (1, WIDE // 2, WIDE)]
        NP = len(PIECES)

        def pairs(engine):
            return engine.value_load(K.pairs[0:1, 0:1], min_val=E_N // 2 - 1, max_val=LIMIT - 1)

        @block.sync
        def _(sp):
            def load(n, q, matrices):
                e = sp.value_load(K.expert[0:1, bass.ds(n, 1)], min_val=0, max_val=E_N - 1)
                for k in matrices:
                    src, tiles = ((wg_d, KT), (wu_d, KT), (wd_d, 2))[k]
                    if k == 2:
                        if not (isinstance(n, int) and n < 2):
                            sp.wait_ge(s_dlo, n - 1)
                            sp.sem_inc(turn["sp"], 1)
                    elif not (isinstance(n, int) and n < 2):
                        sp.wait_ge(s_lo, n * NP - 2 * NP + (1, 3)[k])
                        sp.sem_inc(turn["sp"], 1)
                    sp.dma_start(WR[q][k][:, :].rearrange("p (o t f) -> p o t f", o=1, t=tiles), src[:, bass.ds(e, 1), :, :]) \
                        .then_inc(s_raw[q][k], 16)

            load(0, 0, (0, 1))
            load(1, 1, (0, 1))
            load(0, 0, (2,))
            load(1, 1, (2,))
            load(2, 0, (0, 1))
            last = pairs(sp)
            with sp.Fori(0, last) as i:
                for q in two:
                    load(i * 2 + (q + 3), 1 - q, (0, 1))
                    load(i * 2 + (q + 2), q, (2,))
            for k in two:
                sp.wait_ge(s_raw[0][k], last * 16 + 32)
                sp.sem_inc(turn["sp"], 1)

        @block.gpsimd
        def _(pool):
            def gather(q, n, first):
                for r in two:
                    pool.tensor_copy(gi[q][r][:, :], K.idx[r][:, bass.ds(n, 1)]).then_inc(s_pi, 1)
                pool.wait_ge(s_pi, first + 2)
                pool.sem_inc(turn["pool"], 1)
                for r in two:
                    pool.indirect_dma_start(XG[q][r][:, :], None, xn2_d, bass.IndirectOffsetOnAxis(ap=gi[q][r][:, :], axis=0)) \
                        .then_inc(s_g[q], 16)

            def add_rows(i, q, copies, ahead):
                n = i * 2 + q
                pool.wait_ge(s_ya, n * 4 + 5)
                pool.sem_inc(turn["pool"], 1)
                for r in two:
                    pool.tensor_copy(si[q][r][:, :], K.idx[r][:, bass.ds(n, 1)]).then_inc(s_pi, 1)
                pool.wait_ge(s_pi, copies + 2)
                pool.sem_inc(turn["pool"], 1)
                for r in two:
                    pool.indirect_dma_start(acc_d, bass.IndirectOffsetOnAxis(ap=si[q][r][:, :], axis=0), YE[r][:, :], None,
                                            compute_op=ALU.add).then_inc(s_ad, 16)
                if ahead:
                    pool.wait_ge(s_g[q], i * 32 + 64)
                    pool.sem_inc(turn["pool"], 1)
                    pool.wait_ge(s_tp, n * 3 + 9)
                    pool.sem_inc(turn["pool"], 1)
                    gather(q, n + 4, copies + 2)
                pool.wait_ge(s_ad, n * 32 + 32)
                pool.sem_inc(s_free, 1)

            def gates(i, q):
                for r in two:
                    last = pool.tensor_copy(gt[q][r][:, :], K.gate[r][:, bass.ds(i * 2 + q, 1)])
                last.then_inc(s_gt, 1)

            gather(0, 0, 0)
            gather(1, 1, 2)
            for q in two:
                for part in (HH, HL):
                    pool.memset(part[q][:, :, CAP:].bitcast(F32), 0.0).then_inc(s_z, 1)
            pool.sem_inc(s_free, 1)
            for q in two:
                pool.wait_ge(s_g[q], 32)
                pool.wait_ge(s_tp, 3 * q + 3)
                gather(q, 2 + q, 4 + 2 * q)
            last = pairs(pool)
            with pool.Fori(0, last) as i:
                for q in two:
                    gates(i, q)
                    add_rows(i, q, i * 8 + (8 + 4 * q), True)
            for q in two:
                gates(last, q)
                add_rows(last, q, last * 8 + (8 + 2 * q), False)
            for q in two:
                pool.wait_ge(s_g[q], last * 32 + 64)
                pool.sem_inc(turn["pool"], 1)

        @block.tensor
        def _(pe):
            pe.sem_inc(s_y, 1)

            def turned(q, n, c):
                pe.wait_ge(s_xl, n * 3 + (3, 2, 4)[c])
                for t in range(3 * c, min(3 * c + 3, KT)):
                    for r, (a, b) in enumerate(((0, P), (P, CAP))):
                        rows = XG[q][r][:, :].rearrange("p (k t) -> p t k", t=KT)
                        last = pe.transpose(xp[c % 2][:, t - 3 * c, a:b], rows[:, t, :], K.ident[0:b - a, 0:b - a])
                last.then_inc(s_tp, 1)

            def gate_up(q, n, g):
                f, k = divmod(g, 2)
                if f == 0:
                    pe.wait_ge(s_lo, n * NP + (1, 3)[k])
                if g in (0, 3):
                    pe.wait_ge(s_gk, n * 4 + 1 + g // 3)
                high, low = (W[q][k][:, :].rearrange("p (t f) -> p t f", t=KT) for W in (WH, WL))
                cols = slice(f * P, f * P + P)
                for t in range(KT):
                    pe.matmul(gu[g][:, :, :], high[:, t, cols], XS[q][:, t, :, :], start=(t == 0), stop=False)
                    last = pe.matmul(gu[g][:, 0, :], low[:, t, cols], XS[q][:, t, 0, :], start=False, stop=(t == KT - 1))
                last.then_inc(s_gu, 1)

            def down(q, n, g):
                r, half = divmod(g, 2)
                if g in (0, 3):
                    pe.wait_ge(s_ya, n * 4 + 1 + g // 3)
                if g == 0:
                    pe.wait_ge(s_dlo, n + 1)
                    pe.wait_ge(s_he, n * 2 + 2)
                high, low = (W[q][2][:, :].rearrange("p (f n) -> p f n", f=2) for W in (WH, WL))
                rows, cols = slice(r * P, r * P + P), slice(512 * half, 512 * half + 512)
                for f in two:
                    hh, hl = HH[q][:, f, rows], HL[q][:, f, rows]
                    pe.matmul(yp[g][:, :], hh, high[:, f, cols], start=(f == 0), stop=False)
                    pe.matmul(yp[g][:, :], hh, low[:, f, cols], start=False, stop=False)
                    last = pe.matmul(yp[g][:, :], hl, high[:, f, cols], start=False, stop=(f == 1))
                last.then_inc(s_y, 1)

            def turn_(i, q, ahead):
                n = i * 2 + q
                if ahead >= 1:
                    pe.wait_ge(s_xl, n * 3 + 9)
                    gate_up(1 - q, n + 1, 0)
                    gate_up(1 - q, n + 1, 1)
                if ahead >= 2:
                    pe.wait_ge(s_g[q], i * 32 + 64)
                    turned(q, n + 2, 0)
                if ahead >= 1:
                    gate_up(1 - q, n + 1, 2)
                if ahead >= 2:
                    turned(q, n + 2, 1)
                if ahead >= 1:
                    gate_up(1 - q, n + 1, 3)
                down(q, n, 0)
                if ahead >= 2:
                    turned(q, n + 2, 2)
                for g in (1, 2, 3):
                    down(q, n, g)

            pe.wait_ge(s_g[0], 32)
            for c in range(3):
                turned(0, 0, c)
            pe.wait_ge(s_g[1], 32)
            pe.wait_ge(s_xl, 6)
            for g in range(4):
                gate_up(0, 0, g)
                if g < 3:
                    turned(1, 1, g)
            pe.wait_ge(s_z, 4)
            last = pairs(pe)
            with pe.Fori(0, last) as i:
                for q in two:
                    turn_(i, q, 2)
            for q in two:
                turn_(last, q, 1 - q)

        @block.scalar
        def _(act):
            act.sem_inc(s_ya, 1)

            def high(k, q, n, loads):
                m, a, b = PIECES[k]
                if not (isinstance(n, int) and n < 2):
                    act.wait_ge(s_gu, n * 4 - 4)
                act.wait_ge(s_raw[q][m], loads * 16)
                act.activation(WH[q][m][:, a:b], WR[q][m][:, a:b], ACT.Copy).then_inc(s_hi, 1)

            def high_down(q, n, loads):
                if not isinstance(n, int):
                    act.wait_ge(s_y, n * 4 - 3)
                act.wait_ge(s_raw[q][2], loads * 16)
                act.activation(WH[q][2][:, :], WR[q][2][:, :], ACT.Copy).then_inc(s_dhi, 1)

            def keep(c, q, n):
                act.wait_ge(s_tp, n * 3 + c + 1)
                tiles = slice(3 * c, min(3 * c + 3, KT))
                act.activation(XS[q][:, tiles, 0, :], xp[c % 2][:, 0:tiles.stop - tiles.start, :], ACT.Copy).then_inc(s_xh, 1)

            def sigmoid(f, n):
                act.wait_ge(s_gk, n * 4 + 2 * f + 2)
                act.activation(SS[:, f, :], GS[:, f, :], ACT.Sigmoid).then_inc(s_ss, 1)

            def turn_(i, q, ahead):
                n = i * 2 + q
                for k in range(3):
                    if ahead >= 2:
                        high(k, q, n + 2, i + 2)
                    if ahead >= 1 and k == 1:
                        sigmoid(0, n + 1)
                if ahead >= 2:
                    keep(0, q, n + 2)
                if ahead >= 1:
                    high_down(1 - q, n + 1, i + (1 + q))
                if ahead >= 2:
                    keep(1, q, n + 2)
                if ahead >= 1:
                    sigmoid(1, n + 1)
                act.wait_ge(s_gt, n + 1)
                act.wait_ge(s_free, n + 1)
                for g in range(4):
                    r, half = divmod(g, 2)
                    act.wait_ge(s_y, n * 4 + g + 2)
                    act.activation(YE[r][:, 512 * half:512 * half + 512], yp[g][0:(P, CAP1)[r], :], ACT.Copy,
                                   scale=gt[q][r][:, 0:1]).then_inc(s_ya, 1)
                    if g == 0 and ahead >= 2:
                        keep(2, q, n + 2)

            for k in range(3):
                high(k, 0, 0, 1)
            for c in range(3):
                keep(c, 0, 0)
            for k in range(3):
                high(k, 1, 1, 1)
            keep(0, 1, 1)
            sigmoid(0, 0)
            keep(1, 1, 1)
            keep(2, 1, 1)
            high_down(0, 0, 1)
            sigmoid(1, 0)
            last = pairs(act)
            with act.Fori(0, last) as i:
                for q in two:
                    turn_(i, q, 2)
            for q in two:
                turn_(last, q, 1 - q)

        @block.vector
        def _(dve):
            step = Chain(dve, s_hc)
            tt = nc.vector.tensor_tensor
            dve.sem_inc(s_xl, 3)
            dve.sem_inc(s_gk, 1)

            def low(k, q, n):
                m, a, b = PIECES[k]
                dve.wait_ge(s_hi, n * NP + k + 1)
                tt(WL[q][m][:, a:b], WR[q][m][:, a:b], WH[q][m][:, a:b].bitcast(F32), ALU.subtract).then_inc(s_lo, 1)

            def low_down(q, n):
                dve.wait_ge(s_dhi, n + 1)
                tt(WL[q][2][:, :], WR[q][2][:, :], WH[q][2][:, :].bitcast(F32), ALU.subtract).then_inc(s_dlo, 1)

            def keep(c, q, n):
                dve.wait_ge(s_xh, n * 3 + c + 1)
                tiles = slice(3 * c, min(3 * c + 3, KT))
                tt(XS[q][:, tiles, 1, :], xp[c % 2][:, 0:tiles.stop - tiles.start, :], XS[q][:, tiles, 0, :].bitcast(F32), ALU.subtract) \
                    .then_inc(s_xl, 1)

            def total(out, g, n):
                dve.wait_ge(s_gu, n * 4 + g + 1)
                step(nc.vector.tensor_copy(out, gu[g][:, 1, :]))
                tt(out, out, gu[g][:, 0, :], ALU.add).then_inc(s_gk, 1)

            def hidden(f, q, n):
                dve.wait_ge(s_ss, n * 2 + f + 1)
                step(tt(SS[:, f, :], SS[:, f, :], GS[:, f, :], ALU.mult))
                if f == 0 and not isinstance(n, int):
                    dve.wait_ge(s_y, n * 4 - 3)
                dve.wait_ge(s_gk, n * 4 + 2 * f + 3)
                step(tt(HF[:, f, :], SS[:, f, :], US[:, f, :], ALU.mult))
                step(nc.vector.tensor_copy(HH[q][:, f, 0:CAP], HF[:, f, :]))
                tt(HL[q][:, f, 0:CAP], HF[:, f, :], HH[q][:, f, 0:CAP].bitcast(F32), ALU.subtract).then_inc(s_he, 1)

            def turn_(i, q, ahead):
                n, o = i * 2 + q, 1 - q
                if ahead >= 2:
                    low(0, q, n + 2)
                if ahead >= 1:
                    total(GS[:, 0, :], 0, n + 1)
                if ahead >= 2:
                    low(1, q, n + 2)
                if ahead >= 1:
                    total(US[:, 0, :], 1, n + 1)
                    hidden(0, o, n + 1)
                if ahead >= 2:
                    low(2, q, n + 2)
                    keep(0, q, n + 2)
                if ahead >= 1:
                    total(GS[:, 1, :], 2, n + 1)
                    low_down(o, n + 1)
                if ahead >= 2:
                    keep(1, q, n + 2)
                if ahead >= 1:
                    total(US[:, 1, :], 3, n + 1)
                    hidden(1, o, n + 1)
                if ahead >= 2:
                    keep(2, q, n + 2)

            for k in range(3):
                low(k, 0, 0)
            for c in range(3):
                keep(c, 0, 0)
            for k in range(3):
                low(k, 1, 1)
            total(GS[:, 0, :], 0, 0)
            total(US[:, 0, :], 1, 0)
            keep(0, 1, 1)
            hidden(0, 0, 0)
            total(GS[:, 1, :], 2, 0)
            keep(1, 1, 1)
            total(US[:, 1, :], 3, 0)
            keep(2, 1, 1)
            low_down(0, 0)
            hidden(1, 0, 0)
            last = pairs(dve)
            with dve.Fori(0, last) as i:
                step.enter(i, 20)
                for q in two:
                    turn_(i, q, 2)
            step.leave(last)
            turn_(last, 0, 1)


def phase_final(nc, ins, K, acc_d, out):
    with ExitStack() as ctx:
        def sb(name, shape, dt=F32):
            return ctx.enter_context(nc.sbuf_tensor(name, shape, dt))
        sem = lambda n: ctx.enter_context(nc.semaphore(n))
        A = [sb(f"A{j}", [P, D]) for j in range(TT)]
        junk = [sb(f"junkf{i}", [P, D]) for i in range(2)]
        ss, rt = sb("ssf", [P, TT]), sb("rtf", [P, TT])
        gf = sb("gf", [P, D])
        s_a = [sem(f"acc_in{j}") for j in range(TT)]
        s_gf, s_s, s_r, s_rc, s_o, s_out = sem("gfinal_in"), sem("squares_f"), sem("roots_f"), sem("recips_f"), sem("rows_f"), sem("out_written")
        block = ctx.enter_context(nc.Block())
        accv = acc_d[0:T, :].rearrange("(j p) n -> p j n", p=P)
        outv = out.rearrange("b (j p) n -> p (b j) n", p=P)

        @block.sync
        def _(sp):
            for j in range(TT):
                sp.dma_start(A[j][:, :], accv[:, j, :]).then_inc(s_a[j], 16)
                if j == 0:
                    sp.dma_start(gf[:, :], ins["norm_final_g"].rearrange("(o n) -> o n", o=1).to_broadcast([P, D])).then_inc(s_gf, 16)
            for j in range(TT):
                sp.wait_ge(s_o, j + 1)
                sp.dma_start(outv[:, j, :], A[j][:, :]).then_inc(s_out, 16)
            sp.wait_ge(s_out, 16 * TT)

        @block.scalar
        def _(act):
            for j in range(TT):
                act.wait_ge(s_a[j], 16)
                if j >= 2:
                    act.wait_ge(s_s, j - 1)
                act.activation(junk[j % 2][:, :], A[j][:, :], ACT.Square, accum_out=ss[:, j:j + 1]).then_inc(s_s, 1)
                act.wait_ge(s_s, j + 1)
                act.activation(rt[:, j:j + 1], ss[:, j:j + 1], ACT.Sqrt, bias=K.eps[:, 0:1], scale=1.0 / D).then_inc(s_r, 1)

        @block.vector
        def _(dve):
            dve.wait_ge(s_gf, 16)
            for j in range(TT):
                dve.wait_ge(s_r, j + 1)
                nc.vector.reciprocal(rt[:, j:j + 1], rt[:, j:j + 1]).then_inc(s_rc, 1)
                dve.wait_ge(s_rc, j + 1)
                nc.vector.scalar_tensor_tensor(A[j][:, :], A[j][:, :], rt[:, j:j + 1], gf[:, :], ALU.mult, ALU.mult).then_inc(s_o, 1)


def build(nc, ins, out):
    h2_d = nc.dram_tensor("h2_rows", (T + CAP, D), F32, kind="Internal").ap()
    xn2_d = nc.dram_tensor("xn2_rows", (T + CAP, D), F32, kind="Internal").ap()
    acc_d = nc.dram_tensor("acc_rows", (T + CAP, D), F32, kind="Internal").ap()
    tbl_d = nc.dram_tensor("slot_table", (ITEMS * CAP, 2), F32, kind="Internal").ap()

    class Kept:
        pass
    K = Kept()
    with ExitStack() as ctx:
        setup(nc, ctx, ins, K)
        with ExitStack() as wide:
            K.xT = wide.enter_context(nc.sbuf_tensor("xT", [P, KT, ALL], F32))
            with ExitStack() as mix:
                phase_norm(nc, ins, K)
                phase_mix(nc, mix, ins, K)
                phase_out(nc, ins, K, h2_d, xn2_d)
            phase_route(nc, ins, K, h2_d, acc_d, tbl_d)
        phase_experts(nc, ins, K, xn2_d, acc_d)
        phase_final(nc, ins, K, acc_d, out)


_INS = ["x", "meta_tokens", "norm_mix_g", "w_in", "lb_table", "hgrn_norm_g", "conv_w", "conv_norm_g", "w_out", "norm_ffn_g",
        "w_router", "router_bias", "w_gate_e", "w_up_e", "w_down_e", "w_gate_s", "w_up_s", "w_down_s", "norm_final_g"]


def kernel(**inputs):
    import numpy as np
    import concourse.bacc as bacc
    from concourse.bass_utils import run_bass_kernel_spmd

    nc = bacc.Bacc("TRN2", target_bir_lowering=False, num_devices=1)
    arrays, ins = {}, {}
    for name in _INS:
        a = np.ascontiguousarray(inputs[name])
        arrays[f"in_{name}"] = a
        ins[name] = nc.dram_tensor(f"in_{name}", a.shape, mybir.dt.from_np(a.dtype), kind="ExternalInput").ap()
    out = nc.dram_tensor("out_0", (1, T, D), F32, kind="ExternalOutput").ap()
    build(nc, ins, out)
    r = run_bass_kernel_spmd(nc, [arrays], core_ids=[0])
    return r.results[0]["out_0"]
```

```python
import concourse.bass as bass
from concourse import mybir
from contextlib import ExitStack

F32 = mybir.dt.float32
F32R = mybir.dt.float32r
I32 = mybir.dt.int32
ALU = mybir.AluOpType
ACT = mybir.ActivationFunctionType

P = 128
D = 1024
KT = D // P
T = 1024
TT = T // P
META = 16
ALL = META + T
HEADS = 4
HW = HEADS * P
E_N = 64
TOPK = 8
FF = 256
EPS = 1e-6
LEVELS = [64, 32, 16, 8, 4, 2, 1]
CAP = 168
CAP1 = CAP - P
ITEMS = E_N + (T * TOPK) // CAP + 3
MORE = -(-T // CAP) - 1
ROUTED_SCALE = 2.5
COL_Q, COL_F, COL_I, COL_GB, COL_CV = 0, HW, 2 * HW, 3 * HW, 5 * HW
Z_LOW = -80.0


class Chain:

    def __init__(self, engine, sem):
        self.engine, self.sem, self.base, self.k = engine, sem, 0, 0

    def __call__(self, ins):
        ins.then_inc(self.sem, 1)
        self.k += 1
        self.engine.wait_ge(self.sem, self.base + self.k)

    def enter(self, i, steps):
        self.start = self.base + self.k
        self.steps, self.base, self.k = steps, i * steps + self.start, 0

    def leave(self, turns):
        assert self.k == self.steps, (self.k, self.steps)
        self.base, self.k = self.start + turns * self.steps, 0


def bcast(ap, n):
    return ap.rearrange("p (a o) -> p a o", o=1).to_broadcast([ap.shape[0], ap.shape[1], n])


def shared(nc, tensors):
    with ExitStack() as ctx:
        return [ctx.enter_context(nc.sbuf_tensor(name, shape, F32R)) for name, shape in tensors]


def setup(nc, ctx, ins, K):
    def sb(name, shape, dt=F32):
        return ctx.enter_context(nc.sbuf_tensor(name, shape, dt))
    K.ident = sb("ident", [P, P])
    K.ones = sb("ones", [P, P])
    K.idx = [sb("idx0", [P, ITEMS], I32), sb("idx1", [CAP1, ITEMS], I32)]
    K.gate = [sb("gate0", [P, ITEMS]), sb("gate1", [CAP1, ITEMS])]
    K.expert = sb("expert", [1, ITEMS], I32)
    K.pairs = sb("pairs", [1, 1], I32)
    K.eps = sb("eps", [P, 1])
    cv = 2 * HEADS * ALL
    K.XHP, K.WQ = shared(nc, (("xT_high", [P, cv]), ("wq_parts", [P, 2, D])))
    K.XH = K.XHP[:, 0:KT * T].rearrange("p (t n) -> p t n", t=KT)
    K.place = sb("place", [P, 2 * 3 * KT * FF])
    K.WR = [[K.place[:, (3 * i + k) * KT * FF:(3 * i + k + 1) * KT * FF] for k in range(3)] for i in range(2)]


def phase_norm(nc, ins, K):
    x = ins["x"].rearrange("b (j p) n -> p (b j) n", p=P)
    with ExitStack() as ctx:
        def sb(name, shape, dt=F32):
            return ctx.enter_context(nc.sbuf_tensor(name, shape, dt))
        xt = sb("xt", [P, TT + 1, D])
        junk = [sb(f"junk{i}", [P, D]) for i in range(2)]
        ss = sb("ss", [P, TT + 1])
        rstd = sb("rstd", [P, TT + 1])
        xs = [sb(f"xs{i}", [P, D]) for i in range(2)]
        gmix = sb("gmix", [P, KT])
        pt = [ctx.enter_context(nc.psum_tensor(f"pt{i}", [P, 4, P], F32)) for i in range(4)]
        sem = lambda n: ctx.enter_context(nc.semaphore(n))
        s_x = [sem(f"x_in{j}") for j in range(4)]
        s_m = sem("meta_in")
        s_g = sem("gmix_in")
        s_c = sem("consts_set")
        s_c0 = sem("consts_cleared")
        s_ss = sem("squares_summed")
        s_rt = sem("root")
        s_rs = sem("rstd_ready")
        s_xs = sem("x_scaled")
        s_wi = sem("wi_in")
        s_tr = sem("x_transposed")
        s_ev, s_hi, s_lo = sem("xT_stored"), sem("xT_high"), sem("xT_low")
        block = ctx.enter_context(nc.Block())
        order = [TT] + list(range(TT))

        @block.sync
        def _(sp):
            sp.dma_start(xt[0:META, TT, :], ins["meta_tokens"]).then_inc(s_m, 16)
            for j in range(TT):
                if j >= 4:
                    sp.wait_ge(s_x[j - 4], 16)
                sp.dma_start(xt[:, j, :], x[:, j, :]).then_inc(s_x[j % 4], 16)
                if j == 0:
                    sp.dma_start(gmix[:, :], ins["norm_mix_g"].rearrange("l (p t) -> p (l t)", t=KT)).then_inc(s_g, 16)
            sp.dma_start(K.wi[:, :, :], ins["w_in"].rearrange("l (p t) n -> p (l t) n", t=KT)[:, :, COL_I:COL_I + HW]).then_inc(s_wi, 16)
            sp.wait_ge(s_wi, 16)

        @block.gpsimd
        def _(pool):
            pool.memset(K.ident[:, :], 0.0).then_inc(s_c0, 1)
            pool.memset(K.ones[:, :], 1.0).then_inc(s_c, 1)
            pool.memset(K.eps[:, :], EPS).then_inc(s_c, 1)
            pool.wait_ge(s_c0, 1)
            pool.affine_select(out=K.ident[:, :], in_=K.ident[:, :], compare_op=ALU.not_equal, fill=1.0,
                               base=0, pattern=[[-1, P]], channel_multiplier=1).then_inc(s_c, 1)

        @block.scalar
        def _(act):
            act.wait_ge(s_c, 3)

            def root(c):
                j = order[c]
                n = META if j == TT else P
                if j == TT:
                    act.wait_ge(s_m, 16)
                else:
                    act.wait_ge(s_x[j % 4], 16 * (j // 4 + 1))
                if c >= 2:
                    act.wait_ge(s_ss, c - 1)
                act.activation(junk[c % 2][0:n, :], xt[0:n, j, :], ACT.Square,
                               accum_out=ss[0:n, j:j + 1]).then_inc(s_ss, 1)
                act.wait_ge(s_ss, c + 1)
                act.activation(rstd[0:n, j:j + 1], ss[0:n, j:j + 1], ACT.Sqrt, bias=K.eps[0:n, 0:1], scale=1.0 / D).then_inc(s_rt, 1)

            def high(c):
                act.wait_ge(s_ev, c + 1)
                cols = slice((c - 1) * P, c * P)
                act.activation(K.XH[:, :, cols], K.xT[:, :, META + cols.start:META + cols.stop], ACT.Copy).then_inc(s_hi, 1)

            root(0)
            for c, j in enumerate(order):
                if c < TT:
                    root(c + 1)
                n = META if j == TT else P
                act.wait_ge(s_rs, c + 1)
                if c >= 2:
                    act.wait_ge(s_tr, c - 1)
                act.activation(xs[c % 2][0:n, :], xt[0:n, j, :], ACT.Copy, scale=rstd[0:n, j:j + 1]).then_inc(s_xs, 1)
                if c >= 2:
                    high(c - 1)
            high(TT)

        @block.vector
        def _(dve):
            def recip(c):
                j = order[c]
                n = META if j == TT else P
                dve.wait_ge(s_rt, c + 1)
                dve.reciprocal(rstd[0:n, j:j + 1], rstd[0:n, j:j + 1]).then_inc(s_rs, 1)

            def low(c):
                dve.wait_ge(s_hi, c)
                cols = slice((c - 1) * P, c * P)
                dve.tensor_tensor(K.XL[:, :, cols], K.xT[:, :, META + cols.start:META + cols.stop],
                                  K.XH[:, :, cols].bitcast(F32), ALU.subtract).then_inc(s_lo, 1)

            recip(0)
            dve.wait_ge(s_g, 16)
            for c, j in enumerate(order):
                if c < TT:
                    recip(c + 1)
                n = META if j == TT else P
                col = 0 if j == TT else META + j * P
                dve.wait_ge(s_tr, c + 1)
                for half in range(2):
                    last = dve.tensor_tensor(K.xT[:, 4 * half:4 * half + 4, col:col + n],
                                             pt[2 * (c % 2) + half][:, :, 0:n],
                                             bcast(gmix[:, 4 * half:4 * half + 4], n), ALU.mult)
                last.then_inc(s_ev, 1)
                if c >= 2:
                    low(c - 1)
            low(TT)

        @block.tensor
        def _(pe):
            pe.wait_ge(s_c, 3)
            for c, j in enumerate(order):
                n = META if j == TT else P
                pe.wait_ge(s_xs, c + 1)
                if c >= 2:
                    pe.wait_ge(s_ev, c - 1)
                rows = xs[c % 2][0:n, :].rearrange("p (k t) -> p t k", t=KT)
                for t in range(KT):
                    last = pe.transpose(pt[2 * (c % 2) + t // 4][:, t % 4, 0:n], rows[:, t, :], K.ident[0:n, 0:n])
                last.then_inc(s_tr, 1)


def phase_mix(nc, ctx_out, ins, K):
    w_in = ins["w_in"].rearrange("l (p t) n -> p (l t) n", t=KT)

    def keep(name, shape, dt=F32):
        return ctx_out.enter_context(nc.sbuf_tensor(name, shape, dt))
    (WI1,) = shared(nc, (("wi_low", [P, KT, HW]),))
    K.QO = keep("QO", [P, HEADS, T])
    K.CV = K.place[:, 0:2 * HEADS * ALL].rearrange("p (c t) -> p c t", t=ALL)
    K.ng = keep("ng", [P, 2, HEADS])
    with ExitStack() as ctx:
        def sb(name, shape, dt=F32):
            return ctx.enter_context(nc.sbuf_tensor(name, shape, dt))

        def ps(name, shape):
            return ctx.enter_context(nc.psum_tensor(name, shape, F32))
        sem = lambda n: ctx.enter_context(nc.semaphore(n))
        (WI0,) = shared(nc, (("wi_high", [P, KT, HW]),))
        FP = sb("FP", [P, HEADS, ALL])
        VT = sb("VT", [P, TT, HW])
        VM = sb("VM", [META, HW])
        wi = K.wi
        spare = wi[:, :, :].rearrange("p t n -> p (t n)")
        WI = (WI0, WI1)
        WS = [[m[:, k, :].rearrange("p (t n) -> p t n", t=KT) for k in two] for two, m in (((2, 3), K.WF), ((0, 1), K.WQ))]
        wbuf = [sb(f"wbuf{i}", [P, KT, P])[:, :, :] for i in range(2)] + \
            [spare[:, D * i:D * i + D].rearrange("p (t n) -> p t n", t=KT) for i in range(2)]
        masks = sb("masks", [P, len(LEVELS), HEADS * 64], mybir.dt.int16)
        restart = sb("restart", [P, HEADS, P])
        cw = sb("cw", [P, 3, HEADS])
        names = ("Z", "EZ", "SG", "KK", "BB", "QS", "QE", "DK", "KE", "KTS", "VC", "ST", "SCT")
        placed = (6 * KT * FF - 2 * HEADS * ALL) // HW

        def tile(k, name):
            if k >= placed:
                return sb(name, [P, HEADS, P])
            start = 2 * HEADS * ALL + k * HW
            return K.place[:, start:start + HW].rearrange("p (h t) -> p h t", h=HEADS)
        rest = K.place[:, 2 * HEADS * ALL + placed * HW:]
        term = rest[:, 0:256]
        lbw = rest[:, 256:256 + 5 * HEADS].rearrange("p (k h) -> p k h", h=HEADS)
        lbt = rest[:, 288:288 + 2 * HEADS].rearrange("p (k h) -> p k h", h=HEADS)
        Z, EZ, SG, KK, BB, QS, QE, DK, KE, KTS, VC, ST, SCT = (tile(k, n) for k, n in enumerate(names))
        FV, LF = Z, EZ
        DD, WW = ([spare[:, 2 * D + HW * (2 * k + i):2 * D + HW * (2 * k + i + 1)].rearrange("p (h t) -> p h t", h=HEADS)
                   for i in range(2)] for k in range(2))
        blast = sb("blast", [P, HEADS])
        oml, lb = lbw[:, 3, :], lbw[:, 2, :]
        bank = [ps(f"bank{i}", [P, 512]) for i in range(2)]
        bankm = ps("bankm", [P, 512])
        sc = [ps(f"sc{i}", [P, HEADS * P]) for i in range(2)]
        kt_ps, o_ps, st_ps = ps("kt_ps", [P, HEADS, P]), ps("o_ps", [P, HEADS, P]), ps("st_ps", [P, HEADS, P])

        s_lb = sem("lb_in")
        s_w = [sem(f"w_in{i}") for i in range(4)]
        s_wfree = [sem(f"w_free{i}") for i in range(4)]
        s_mm, s_out = sem("projected"), sem("projection_stored")
        s_cst0, s_cst = sem("masks_cleared"), sem("masks_set")
        s_d, s_t = sem("dve_steps"), sem("turns")
        s_vec, s_conv = sem("vectors_in"), sem("conv_steps")
        s_lbx, s_lbe = sem("lb_shifted"), sem("lb_exp")
        s_wsh, s_wsl = sem("w_high"), sem("w_low")
        s_ez, s_zz, s_fv, s_lf = sem("exp_z"), sem("z_held"), sem("f_ready"), sem("log_f")
        s_cp = sem("chunk_copied")
        s_dd, s_ww0, s_ww, s_s, s_p = sem("decay_logs"), sem("decays"), sem("factors"), sem("scores"), sem("scores_kept")
        s_de, s_ee = sem("end_logs"), sem("end_decays")
        s_ke, s_kt, s_kts = sem("k_end"), sem("k_end_turned"), sem("k_end_stored")
        s_kq = sem("kq_ready")
        s_o, s_oev, s_st, s_stk = sem("o_ready"), sem("o_stored"), sem("state_term"), sem("state_kept")
        block = ctx.enter_context(nc.Block())
        L1, L2 = HEADS, TT
        V_GROUPS = TT + 1
        NI = KT // 2

        @block.sync
        def _(sp):
            sp.dma_start(lbt[:, :, :], ins["lb_table"].rearrange("l (h p) -> p l h", p=P),
                         allow_slow_non_contiguous=True).then_inc(s_lb, 16)
            sp.dma_start(cw[:, :, :].rearrange("p k h -> p (k h)"), ins["conv_w"].rearrange("l k (h p) -> p (l k h)", p=P),
                         allow_slow_non_contiguous=True).then_inc(s_vec, 16)
            for k, name in enumerate(("hgrn_norm_g", "conv_norm_g")):
                sp.dma_start(K.ng[:, k, :], ins[name].rearrange("l (h p) -> p (l h)", p=P),
                             allow_slow_non_contiguous=True).then_inc(s_vec, 16)
            with sp.Fori(0, L1) as i:
                for s, col in ((0, COL_F), (1, COL_Q)):
                    sp.wait_ge(s_wfree[s], i + 1)
                    sp.sem_inc(s_t, 1)
                    sp.dma_start(wbuf[s][:, :, :], w_in[:, :, bass.ds(i * P + col, P)]).then_inc(s_w[s], 16)
            with sp.Fori(0, L2) as i:
                for s, col in ((2, COL_CV), (3, COL_GB)):
                    sp.wait_ge(s_wfree[s], i + 1)
                    sp.sem_inc(s_t, 1)
                    sp.dma_start(wbuf[s][:, :, :], w_in[:, :, bass.ds(i * P + col, P)]).then_inc(s_w[s], 16)

        @block.gpsimd
        def _(pool):
            pool.memset(restart[:, :, :], 1.0).then_inc(s_cst0, 1)
            pool.memset(masks[:, :, :], 1).then_inc(s_cst0, 1)
            pool.wait_ge(s_cst0, 2)
            pool.memset(restart[:, :, 0:1], 0.0).then_inc(s_cst, 1)
            for l, half in enumerate(LEVELS):
                n = 64 // half
                m = masks[:, l, :].rearrange("p (h b r) -> p h b r", h=HEADS, r=half)
                pool.affine_select(out=m, in_=m, compare_op=ALU.is_ge, fill=0.0, base=0,
                                   pattern=[[0, HEADS], [-2 * half, n], [0, half]], channel_multiplier=1).then_inc(s_cst0, 1)
                pool.wait_ge(s_cst0, 3 + l)
                pool.affine_select(out=m, in_=m, compare_op=ALU.is_ge, fill=0.0, base=half - 1,
                                   pattern=[[0, HEADS], [2 * half, n], [0, half]], channel_multiplier=-1).then_inc(s_cst, 1)
            pool.wait_ge(s_vec, 48)
            step = Chain(pool, s_conv)
            for h in range(HEADS):
                stored = V_GROUPS + 5 * L1 + 5 * (HEADS + h)
                C, V, B = K.CV[:, h, :], K.CV[:, HEADS + h, :], K.GB[:, HEADS + h, :]
                y = V[:, META:ALL]
                half = T // 2
                for k in range(2):
                    pool.wait_ge(s_out, stored + 2 + k)
                    u = slice(META - 2 if k == 0 else META + half, META + half * (k + 1))
                    step(pool.tensor_tensor(C[:, u], C[:, u], V[:, u], ALU.mult))
                    tokens = slice(k * half, k * half + half)
                    step(pool.tensor_scalar(y[:, tokens], C[:, META - 2 + k * half:META - 2 + k * half + half], cw[:, 0, h:h + 1], None, ALU.mult))
                    for tap in (1, 2):
                        for a in range(k * half, k * half + half, 256):
                            u = C[:, META - 2 + tap + a:META - 2 + tap + a + 256]
                            step(pool.tensor_scalar(term[:, :], u, cw[:, tap, h:h + 1], None, ALU.mult))
                            step(pool.tensor_tensor(y[:, a:a + 256], y[:, a:a + 256], term[:, :], ALU.add))
                for k in range(2):
                    tokens = slice(k * half, k * half + half)
                    pool.wait_ge(s_out, stored + 4 + k)
                    step(pool.tensor_tensor(y[:, tokens], y[:, tokens], B[:, tokens], ALU.mult))

        @block.tensor
        def _(pe):
            def group(out, n, lhs, rhs):
                for t in range(KT):
                    last = pe.matmul(out, lhs(t), rhs(t), start=(t == 0), stop=(t == KT - 1))
                last.then_inc(s_mm, 1)

            def products(out, lhs, rhs, t):
                pe.matmul(out, lhs[0], rhs[0], start=(t == 0), stop=False)
                pe.matmul(out, lhs[0], rhs[1], start=False, stop=False)
                return pe.matmul(out, lhs[1], rhs[0], start=False, stop=(t == KT - 1))

            for j in range(V_GROUPS):
                if j >= 2:
                    pe.wait_ge(s_out, j - 1)
                if j == TT:
                    group(bank[j % 2][0:META, :], META, lambda t: K.xT[:, t, 0:META], lambda t: wi[:, t, :])
                    break
                for t in range(KT):
                    if j == 0 and t % 2 == 0:
                        pe.wait_ge(s_wsl, t // 2 + 1)
                    last = products(bank[j % 2][:, :], [x[:, t, j * P:j * P + P] for x in (K.XH, K.XL)],
                                    [w[:, t, :] for w in WI], t)
                last.then_inc(s_mm, 1)

            def project(s, b, base):
                cols = slice(512 * b, 512 * b + 512)
                pe.wait_ge(s_out, base - 1)
                for t in range(KT):
                    last = products(bank[b][:, :], [w[:, t, :] for w in WS[s]], [x[:, t, cols] for x in (K.XH, K.XL)], t)
                last.then_inc(s_mm, 1)

            def project_meta(s, base):
                pe.wait_ge(s_out, base - 1)
                group(bankm[:, 0:META], META, lambda t: wbuf[s][:, t, :], lambda t: K.xT[:, t, 0:META])

            pe.wait_ge(s_mm, V_GROUPS)
            for s in range(4):
                pe.sem_inc(s_wfree[s], 1)
            with pe.Fori(0, L1) as i:
                base = i * 5 + V_GROUPS
                pe.wait_ge(s_w[0], i * 16 + 16)
                project_meta(0, base)
                pe.wait_ge(s_wsl, i * 2 + (NI + 1))
                project(0, 0, base + 1)
                project(0, 1, base + 2)
                pe.sem_inc(s_t, 1)
                pe.wait_ge(s_mm, base + 3)
                pe.sem_inc(s_wfree[0], 1)
                pe.wait_ge(s_wsl, i * 2 + (NI + 2))
                project(1, 0, base + 3)
                project(1, 1, base + 4)
                pe.wait_ge(s_mm, base + 5)
                pe.sem_inc(s_wfree[1], 1)

            pe.wait_ge(s_ke, 1)
            for h in range(HEADS):
                last = pe.transpose(kt_ps[0:META, h, :], KE[:, h, 0:META], K.ident[:, :])
            last.then_inc(s_kt, 1)
            pe.wait_ge(s_kts, 1)
            for h in range(HEADS):
                last = pe.matmul(st_ps[:, h, :], KTS[0:META, h, :], VM[:, h * P:(h + 1) * P], start=True, stop=True)
            last.then_inc(s_st, 1)

            with pe.Fori(0, L2) as i:
                base = i * 5 + V_GROUPS + 5 * L1
                NS = len(LEVELS) + 1

                def level(l):
                    if l == 0:
                        pe.wait_ge(s_kq, i + 1)
                        pe.wait_ge(s_p, i * NS + 1)
                        for h in range(HEADS):
                            last = pe.matmul(sc[0][:, h * P:(h + 1) * P], KK[:, h, :], QS[:, h, :], start=True, stop=True)
                    else:
                        half = LEVELS[l - 1]
                        pe.wait_ge(s_ww, i * len(LEVELS) + l)
                        pe.wait_ge(s_p, i * NS + l)
                        W = WW[l % 2]
                        for h in range(HEADS):
                            late = W[:, h, :].rearrange("p (b z r) -> p b z r", z=2, r=half)[:, :, 1, :]
                            last = pe.matmul(sc[l % 2][:, h * 64:(h + 1) * 64], W[:, h, :], late, start=True, stop=True)
                    last.then_inc(s_s, 1)

                def pieces():
                    for s, blk, k in ((2, 0, 1), (2, 1, 2), (3, 0, 3), (3, 1, 4)):
                        pe.wait_ge(s_out, base + k - 1)
                        if (s, blk) == (3, 0):
                            pe.wait_ge(s_w[3], i * 16 + 16)
                        cols = slice(META + 512 * blk, META + 512 * blk + 512)
                        for t in range(KT):
                            last = pe.matmul(bank[blk][:, :], wbuf[s][:, t, :], K.xT[:, t, cols], start=(t == 0), stop=(t == KT - 1))
                            if t == KT - 1:
                                last.then_inc(s_mm, 1)
                            yield
                rest = pieces()

                def project_some(n):
                    for _ in range(n):
                        next(rest)

                pe.wait_ge(s_w[2], i * 16 + 16)
                project_meta(2, base)
                project_some(3)
                level(0)
                project_some(5)
                level(1)
                project_some(3)
                level(2)
                project_some(3)
                level(3)
                project_some(3)
                level(4)
                pe.wait_ge(s_mm, base + 3)
                pe.sem_inc(s_wfree[2], 1)
                project_some(3)
                level(5)
                project_some(3)
                level(6)
                project_some(2)
                pe.wait_ge(s_ke, i + 2)
                for h in range(HEADS):
                    last = pe.transpose(kt_ps[:, h, :], KE[:, h, :], K.ident[:, :])
                last.then_inc(s_kt, 1)
                level(7)
                project_some(7)
                pe.wait_ge(s_kts, i + 2)
                for h in range(HEADS):
                    last = pe.matmul(st_ps[:, h, :], KTS[:, h, :], VC[:, h, :], start=True, stop=True)
                last.then_inc(s_st, 1)
                pe.wait_ge(s_mm, base + 5)
                pe.sem_inc(s_wfree[3], 1)
                pe.wait_ge(s_p, i * NS + NS + 1)
                pe.wait_ge(s_stk, i + 1)
                for h in range(HEADS):
                    pe.matmul(o_ps[:, h, :], VC[:, h, :], SCT[:, h, :], start=True, stop=False)
                    last = pe.matmul(o_ps[:, h, :], ST[:, h, :], QE[:, h, :], start=False, stop=True)
                last.then_inc(s_o, 1)

        @block.scalar
        def _(act):
            for k in range(NI):
                pair = slice(2 * k, 2 * k + 2)
                act.activation(WI[0][:, pair, :], wi[:, pair, :], ACT.Copy).then_inc(s_wsh, 1)
            for j in range(V_GROUPS):
                act.wait_ge(s_mm, j + 1)
                if j < TT:
                    act.copy(VT[:, j, :], bank[j % 2][:, :]).then_inc(s_out, 1)
                else:
                    act.copy(VM[:, :], bank[j % 2][0:META, :]).then_inc(s_out, 1)
            act.wait_ge(s_lbx, 1)
            act.activation(lbw[:, 0:2, :], lbw[:, 0:2, :], ACT.Exp).then_inc(s_lbe, 1)

            def store(base, k, out, src):
                act.wait_ge(s_mm, base + k)
                act.sem_inc(s_t, 1)
                act.copy(out, src).then_inc(s_out, 1)

            with act.Fori(0, L1) as i:
                base = i * 5 + V_GROUPS
                for s in range(2):
                    act.wait_ge(s_w[s], i * 16 + 16)
                    act.sem_inc(s_t, 1)
                    act.activation(WS[s][0], wbuf[s], ACT.Copy).then_inc(s_wsh, 1)
                store(base, 1, FP[:, bass.ds(i, 1), 0:META], bankm[:, 0:META])
                store(base, 2, FP[:, bass.ds(i, 1), META:META + 512], bank[0][:, :])
                store(base, 3, FP[:, bass.ds(i, 1), META + 512:ALL], bank[1][:, :])
                store(base, 4, K.QO[:, bass.ds(i, 1), 0:512], bank[0][:, :])
                store(base, 5, K.QO[:, bass.ds(i, 1), 512:T], bank[1][:, :])

            def exp_z(n, turn):
                act.wait_ge(s_zz, turn)
                act.activation(EZ[:, :, 0:n], Z[:, :, 0:n], ACT.Exp, scale=-1.0).then_inc(s_ez, 1)

            def log_f(n, turn):
                act.wait_ge(s_fv, turn)
                act.activation(LF[:, :, 0:n], FV[:, :, 0:n], ACT.Ln).then_inc(s_lf, 1)

            exp_z(META, 1)
            log_f(META, 1)
            act.wait_ge(s_de, 1)
            act.activation(DK[:, :, 0:META], DK[:, :, 0:META], ACT.Exp).then_inc(s_ee, 1)
            act.wait_ge(s_kt, 1)
            act.copy(KTS[0:META, :, :], kt_ps[0:META, :, :]).then_inc(s_kts, 1)

            exp_z(P, 2)
            log_f(P, 2)

            def turn(i, ahead):
                base = i * 5 + V_GROUPS + 5 * L1

                def decays(l):
                    act.wait_ge(s_dd, i * len(LEVELS) + l + 1)
                    if l >= 2:
                        act.wait_ge(s_s, i * (len(LEVELS) + 1) + l)
                    act.activation(WW[(l + 1) % 2][:, :, :], DD[l % 2][:, :, :], ACT.Exp).then_inc(s_ww0, 1)

                act.wait_ge(s_oev, i + 1)
                act.sem_inc(s_t, 1)
                act.copy(QS[:, :, :], K.QO[:, :, bass.ds(i * P, P)]).then_inc(s_cp, 1)
                act.copy(VC[:, :, :].rearrange("p h v -> p (h v)"), VT[:, bass.ds(i, 1), :]).then_inc(s_cp, 1)
                store(base, 1, K.CV[:, bass.ds(i, 1), 0:META], bankm[:, 0:META])
                decays(0)
                act.wait_ge(s_de, i + 2)
                act.activation(DK[:, :, :], DK[:, :, :], ACT.Exp)
                act.activation(QE[:, :, :], BB[:, :, :], ACT.Exp).then_inc(s_ee, 1)

                decays(1)
                store(base, 2, K.CV[:, bass.ds(i, 1), META:META + 512], bank[0][:, :])
                decays(2)
                decays(3)
                if ahead:
                    exp_z(P, i + 3)
                decays(4)
                store(base, 3, K.CV[:, bass.ds(i, 1), META + 512:ALL], bank[1][:, :])
                decays(5)
                decays(6)
                store(base, 4, K.GB[:, bass.ds(i, 1), 0:512], bank[0][:, :])
                act.wait_ge(s_kt, i + 2)
                act.copy(KTS[:, :, :], kt_ps[:, :, :]).then_inc(s_kts, 1)
                if ahead:
                    log_f(P, i + 3)
                store(base, 5, K.GB[:, bass.ds(i, 1), 512:T], bank[1][:, :])
                act.wait_ge(s_o, i + 1)
                act.sem_inc(s_t, 1)
                act.copy(K.QO[:, :, bass.ds(i * P, P)], o_ps[:, :, :]).then_inc(s_oev, 1)

            with act.Fori(0, L2 - 1) as i:
                turn(i, True)
            turn(L2 - 1, False)

        @block.vector
        def _(dve):
            step = Chain(dve, s_d)
            tt, ts, stt = nc.vector.tensor_tensor, nc.vector.tensor_scalar, nc.vector.scalar_tensor_tensor
            for k in range(NI):
                pair = slice(2 * k, 2 * k + 2)
                dve.wait_ge(s_wsh, k + 1)
                tt(WI[1][:, pair, :], wi[:, pair, :], WI[0][:, pair, :].bitcast(F32), ALU.subtract).then_inc(s_wsl, 1)
            dve.wait_ge(s_lb, 16)
            step(tt(lbw[:, 4, :], lbt[:, 0, :], lbt[:, 1, :], ALU.max))
            tt(lbw[:, 0, :], lbt[:, 0, :], lbw[:, 4, :], ALU.subtract)
            tt(lbw[:, 1, :], lbt[:, 1, :], lbw[:, 4, :], ALU.subtract).then_inc(s_lbx, 1)
            dve.wait_ge(s_lbe, 1)
            step(tt(lbw[:, 4, :], lbw[:, 0, :], lbw[:, 1, :], ALU.add))
            step(nc.vector.reciprocal(lbw[:, 4, :], lbw[:, 4, :]))
            step(tt(lbw[:, 2, :], lbw[:, 0, :], lbw[:, 4, :], ALU.mult))
            step(ts(lbw[:, 3, :], lbw[:, 2, :], -1.0, 1.0, ALU.mult, ALU.add))

            def clamp(n, src):
                step(ts(Z[:, :, 0:n], src, Z_LOW, None, ALU.max))
                dve.sem_inc(s_zz, 1)

            def sigmoid(n, turn):
                dve.wait_ge(s_ez, turn)
                step(ts(SG[:, :, 0:n], EZ[:, :, 0:n], 1.0, None, ALU.add))
                step(nc.vector.reciprocal(SG[:, :, 0:n], SG[:, :, 0:n]))

            def gate(n):
                step(tt(FV[:, :, 0:n], SG[:, :, 0:n], bcast(oml, n), ALU.mult))
                step(tt(SG[:, :, 0:n], EZ[:, :, 0:n], SG[:, :, 0:n], ALU.mult))
                tt(FV[:, :, 0:n], FV[:, :, 0:n], bcast(lb, n), ALU.add).then_inc(s_fv, 1)

            def sums(n, turn):
                step(tt(KK[:, :, 0:n], SG[:, :, 0:n], bcast(oml, n), ALU.mult))
                dve.wait_ge(s_lf, turn)
                for h in range(HEADS) if n < P else ():
                    last = nc.vector.tensor_tensor_scan(BB[:, h, 0:n], restart[:, h, 0:n], LF[:, h, 0:n], 0.0, ALU.mult, ALU.add)
                if n == P:
                    last = nc.vector.tensor_tensor_scan(BB[:, :, :].rearrange("p h t -> p (h t)"),
                                                        restart[:, :, :].rearrange("p h t -> p (h t)"),
                                                        LF[:, :, :].rearrange("p h t -> p (h t)"), 0.0, ALU.mult, ALU.add)
                step(last)

            def end_log(n):
                step(tt(DK[:, :, 0:n], BB[:, :, n - 1:n].to_broadcast([P, HEADS, n]), BB[:, :, 0:n], ALU.subtract))
                dve.sem_inc(s_de, 1)

            with dve.Fori(0, L1) as i:
                for s in range(2):
                    dve.wait_ge(s_wsh, i * 2 + (NI + s + 1))
                    dve.sem_inc(s_t, 1)
                    tt(WS[s][1], wbuf[s], WS[s][0].bitcast(F32), ALU.subtract).then_inc(s_wsl, 1)

            dve.wait_ge(s_out, V_GROUPS + 5 * L1)
            dve.wait_ge(s_cst, 1 + len(LEVELS))
            clamp(META, FP[:, :, 0:META])
            sigmoid(META, 1)
            gate(META)
            sums(META, 1)
            end_log(META)
            dve.wait_ge(s_ee, 1)
            step(tt(KE[:, :, 0:META], KK[:, :, 0:META], DK[:, :, 0:META], ALU.mult))
            dve.sem_inc(s_ke, 1)
            clamp(P, FP[:, :, META:META + P])
            sigmoid(P, 2)
            gate(P)
            dve.wait_ge(s_st, 1)
            step(nc.vector.tensor_copy(ST[:, :, :], st_ps[:, :, :]))
            dve.sem_inc(s_stk, 1)
            dve.sem_inc(s_oev, 1)
            dve.sem_inc(s_p, 1)

            def halves(x, half):
                v = x.rearrange("p h (b z r) -> p (h b) z r", z=2, r=half)
                return v[:, :, 0, :], v[:, :, 1, :]

            def turn(i, ahead):
                NL = len(LEVELS)
                dve.wait_ge(s_oev, i + 1)
                dve.sem_inc(s_t, 1)
                sums(P, i + 2)
                dve.wait_ge(s_cp, i * 2 + 2)
                dve.sem_inc(s_kq, 1)

                def logs(l):
                    half = LEVELS[l]
                    n = HEADS * 64 // half
                    (b0, b1), (d0, d1) = halves(BB[:, :, :], half), halves(DD[l % 2], half)
                    ref = b0[:, :, half - 1:half].to_broadcast([P, n, half])
                    tt(d0, ref, b0, ALU.subtract)
                    tt(d1, b1, ref, ALU.subtract).then_inc(s_dd, 1)

                def factors(l):
                    half = LEVELS[l]
                    w0, w1 = halves(WW[(l + 1) % 2], half)
                    dve.wait_ge(s_ww0, i * NL + l + 1)
                    tt(w0, w0, halves(KK[:, :, :], half)[0], ALU.mult)
                    tt(w1, w1, halves(QS[:, :, :], half)[1], ALU.mult).then_inc(s_ww, 1)

                def keep_scores(l):
                    half = LEVELS[l]
                    dve.wait_ge(s_s, i * (NL + 1) + l + 2)
                    dve.sem_inc(s_t, 1)
                    _, late = halves(SCT[:, :, :], half)
                    bank_v = sc[(l + 1) % 2][:, 0:HEADS * 64].rearrange("p (b r) -> p b r", r=half)
                    mask_v = masks[:, l, :].rearrange("p (b r) -> p b r", r=half)
                    step(nc.vector.copy_predicated(late, mask_v, bank_v))
                    dve.sem_inc(s_p, 1)

                logs(0)
                end_log(P)
                logs(1)
                factors(0)
                logs(2)
                dve.wait_ge(s_s, i * (NL + 1) + 1)
                step(tt(SCT[:, :, :], sc[0][:, :].rearrange("p (h t) -> p h t", h=HEADS),
                        K.ident[:, :].rearrange("p (o t) -> p o t", o=1).to_broadcast([P, HEADS, P]), ALU.mult))
                dve.sem_inc(s_p, 1)
                dve.wait_ge(s_ee, i + 2)
                step(nc.vector.tensor_copy(blast[:, :].rearrange("p (h o) -> p h o", o=1), QE[:, :, P - 1:P]))
                tt(QE[:, :, :], QE[:, :, :], QS[:, :, :], ALU.mult)
                step(tt(KE[:, :, :], KK[:, :, :], DK[:, :, :], ALU.mult))
                dve.sem_inc(s_ke, 1)
                for l in range(1, NL):
                    factors(l)
                    if l + 2 < NL:
                        logs(l + 2)
                    keep_scores(l - 1)
                    if ahead and l == 1:
                        clamp(P, FP[:, :, bass.ds(i * P + (META + P), P)])
                    if ahead and l == 3:
                        sigmoid(P, i + 3)
                    if ahead and l == 4:
                        gate(P)
                keep_scores(NL - 1)
                dve.wait_ge(s_st, i + 2)
                dve.wait_ge(s_o, i + 1)
                for h in range(HEADS):
                    last = stt(ST[:, h, :], ST[:, h, :], blast[:, h:h + 1], st_ps[:, h, :], ALU.mult, ALU.add)
                step(last)
                dve.sem_inc(s_stk, 1)

            with dve.Fori(0, L2 - 1) as i:
                step.enter(i, 19)
                turn(i, True)
            step.leave(L2 - 1)
            turn(L2 - 1, False)


def phase_out(nc, ins, K, h2_d, xn2_d):
    w_out = ins["w_out"].rearrange("l (c p) n -> p (l c) n", p=P)
    x = ins["x"].rearrange("b (j p) n -> p (b j) n", p=P)
    G, YC = K.GB[:, 0:HEADS, :], K.CV[:, HEADS:2 * HEADS, META:ALL]
    with ExitStack() as ctx:
        def sb(name, shape, dt=F32):
            return ctx.enter_context(nc.sbuf_tensor(name, shape, dt))

        def ps(name, shape):
            return ctx.enter_context(nc.psum_tensor(name, shape, F32))
        sem = lambda n: ctx.enter_context(nc.semaphore(n))
        wo = sb("wo", [P, KT, D])
        gffn = sb("gffn", [P, D])
        spare = K.wi[:, :, :].rearrange("p t n -> p (t n)")
        H = [spare[:, i * D:i * D + D] for i in range(2)]
        X2 = [spare[:, (2 + i) * D:(3 + i) * D] for i in range(2)]
        sg = [K.place[:, 2 * HEADS * ALL + i * D:2 * HEADS * ALL + i * D + D] for i in range(2)]
        zrow = K.GB[:, HEADS, :]
        Y = [sb(f"Y{i}", [P, 2 * HEADS, P]) for i in range(2)]
        SQ = sb("SQ", [P, 2 * HEADS, P])
        RT = [sb(f"RT{i}", [P, 2 * HEADS, P]) for i in range(2)]
        sh = sb("sh", [P, 2 * TT])
        junk = K.place[:, 2 * HEADS * ALL + 2 * D:2 * HEADS * ALL + 3 * D]
        ms = [ps(f"ms{i}", [P, HEADS, P]) for i in range(2)]
        op = [[ps(f"op{i}{k}", [P, 512]) for k in range(2)] for i in range(2)]
        tr = [ps(f"tr{i}", [P, 4, P]) for i in range(2)]
        s_w = sem("router_in")
        s_wo, s_c, s_z = [sem(f"wo_in{i}") for i in range(2)], sem("gffn_in"), sem("zero_row")
        s_h = [sem(f"h_in{i}") for i in range(2)]
        s_sig, s_gate = sem("sigmoids"), sem("gates_on")
        s_sq, s_ms, s_rt = sem("squares"), sem("mean_squares"), sem("roots")
        s_y, s_op, s_h2 = sem("mixed"), sem("out_projected"), sem("residual_added")
        s_s2, s_r2, s_x2 = sem("squares_summed2"), sem("root2"), sem("xn2_ready")
        s_t2, s_e2, s_st = sem("xn2_turned"), sem("xn2_kept"), sem("rows_written")
        s_d = sem("dve_steps2")
        block = ctx.enter_context(nc.Block())
        tail = K.place[:, 2 * HEADS * ALL + 3 * D:]
        K.wr = tail[:, 0:KT * E_N].rearrange("p (t n) -> p t n", t=KT)
        K.bias = tail[:, KT * E_N:(KT + 1) * E_N]
        h2v = h2_d[0:T, :].rearrange("(j p) n -> p j n", p=P)
        xn2v = xn2_d[0:T, :].rearrange("(j p) n -> p j n", p=P)

        @block.sync
        def _(sp):
            for k in range(2):
                sp.dma_start(wo[:, :, 512 * k:512 * k + 512], w_out[:, :, 512 * k:512 * k + 512]).then_inc(s_wo[k], 16)
            for k in range(2):
                sp.dma_start(H[k][:, :], x[:, k, :]).then_inc(s_h[k], 16)
            sp.dma_start(gffn[:, :], ins["norm_ffn_g"].to_broadcast([P, D])).then_inc(s_c, 16)
            sp.dma_start(K.wr, ins["w_router"].rearrange("l (p t) n -> p (l t) n", t=KT)).then_inc(s_w, 16)
            sp.dma_start(K.bias, ins["router_bias"].to_broadcast([P, E_N])).then_inc(s_w, 16)
            sp.wait_ge(s_z, 1)
            for base in range(T, T + CAP, P):
                n = min(P, T + CAP - base)
                sp.dma_start(xn2_d[base:base + n, :], zrow[0:n, :]).then_inc(s_st, 16)
                sp.dma_start(h2_d[base:base + n, :], zrow[0:n, :]).then_inc(s_st, 16)
            for j in range(TT):
                sp.wait_ge(s_x2, j + 1)
                sp.dma_start(h2v[:, j, :], H[j % 2][:, :]).then_inc(s_st, 16)
                sp.dma_start(xn2v[:, j, :], X2[j % 2][:, :]).then_inc(s_st, 16)
                if j + 2 < TT:
                    sp.wait_ge(s_st, 16 * (4 + 2 * (j + 1)))
                    sp.dma_start(H[j % 2][:, :], x[:, j + 2, :]).then_inc(s_h[j % 2], 16)
            sp.wait_ge(s_st, 16 * (4 + 2 * TT))
            sp.wait_ge(s_w, 32)

        @block.gpsimd
        def _(pool):
            pool.memset(zrow[:, :], 0.0).then_inc(s_z, 1)

        @block.tensor
        def _(pe):
            def means(j):
                pe.wait_ge(s_sq, j + 1)
                if j:
                    pe.wait_ge(s_rt, j)
                for k in range(2):
                    last = pe.matmul(ms[k][:, :, :].rearrange("p h t -> p (h t)"), K.ones[:, :],
                                     SQ[:, HEADS * k:HEADS * k + HEADS, :].rearrange("p h t -> p (h t)"), start=True, stop=True)
                last.then_inc(s_ms, 1)

            def turn(j):
                pe.wait_ge(s_x2, j + 1)
                if j:
                    pe.wait_ge(s_e2, j)
                rows = X2[j % 2][:, :].rearrange("p (k t) -> p t k", t=KT)
                for t in range(KT):
                    last = pe.transpose(tr[t // 4][:, t % 4, :], rows[:, t, :], K.ident[:, :])
                last.then_inc(s_t2, 1)

            means(0)
            means(1)
            for j in range(TT):
                pe.wait_ge(s_y, j + 1)
                if j >= 2:
                    pe.wait_ge(s_h2, j - 1)
                for half in range(2):
                    if half == 1 and j + 2 < TT:
                        means(j + 2)
                    if j == 0:
                        pe.wait_ge(s_wo[half], 16)
                    for c in range(KT):
                        last = pe.matmul(op[j % 2][half][:, :], Y[j % 2][:, c, :], wo[:, c, 512 * half:512 * half + 512],
                                         start=(c == 0), stop=(c == KT - 1))
                last.then_inc(s_op, 1)
                if j:
                    turn(j - 1)
            turn(TT - 1)

        @block.scalar
        def _(act):
            def squares(j):
                if j:
                    act.wait_ge(s_ms, j)
                act.activation(SQ[:, 0:HEADS, :], K.QO[:, :, j * P:j * P + P], ACT.Square)
                act.activation(SQ[:, HEADS:2 * HEADS, :], YC[:, :, j * P:j * P + P], ACT.Square).then_inc(s_sq, 1)

            def roots(j):
                act.wait_ge(s_ms, j + 1)
                if j >= 2:
                    act.wait_ge(s_y, j - 1)
                for k in range(2):
                    last = act.activation(RT[j % 2][:, HEADS * k:HEADS * k + HEADS, :], ms[k][:, :, :], ACT.Sqrt,
                                          bias=K.eps[:, 0:1], scale=1.0 / P)
                last.then_inc(s_rt, 1)

            def keep(j):
                act.wait_ge(s_t2, j + 1)
                for k in range(2):
                    last = act.copy(K.xT[:, 4 * k:4 * k + 4, j * P:j * P + P], tr[k][:, :, :])
                last.then_inc(s_e2, 1)

            squares(0)
            for h in range(HEADS):
                if h >= 2:
                    act.wait_ge(s_gate, h - 1)
                act.activation(sg[h % 2][:, :], G[:, h, :], ACT.Sigmoid).then_inc(s_sig, 1)
            roots(0)
            squares(1)
            roots(1)
            for j in range(TT):
                if j + 2 < TT:
                    squares(j + 2)
                    roots(j + 2)
                if j:
                    act.wait_ge(s_s2, j)
                act.wait_ge(s_h2, j + 1)
                act.activation(junk[:, :], H[j % 2][:, :], ACT.Square, accum_out=sh[:, j:j + 1]).then_inc(s_s2, 1)
                act.wait_ge(s_s2, j + 1)
                act.activation(sh[:, TT + j:TT + j + 1], sh[:, j:j + 1], ACT.Sqrt, bias=K.eps[:, 0:1], scale=1.0 / D).then_inc(s_r2, 1)
                if j:
                    keep(j - 1)
            keep(TT - 1)

        @block.vector
        def _(dve):
            step = Chain(dve, s_d)
            tt, stt = nc.vector.tensor_tensor, nc.vector.scalar_tensor_tensor
            for h in range(HEADS):
                dve.wait_ge(s_sig, h + 1)
                stt(G[:, h, :], G[:, h, :], K.ng[:, 0, h:h + 1], sg[h % 2][:, :], ALU.mult, ALU.mult).then_inc(s_gate, 1)

            def mix(j):
                dve.wait_ge(s_rt, j + 1)
                if j >= 2:
                    dve.wait_ge(s_op, j - 1)
                y, R, cols = Y[j % 2], RT[j % 2], slice(j * P, j * P + P)
                step(nc.vector.reciprocal(R[:, :, :], R[:, :, :]))
                step(tt(y[:, 0:HEADS, :], K.QO[:, :, cols], R[:, 0:HEADS, :], ALU.mult))
                for h in range(HEADS):
                    stt(y[:, HEADS + h, :], YC[:, h, cols], K.ng[:, 1, h:h + 1], R[:, HEADS + h, :], ALU.mult, ALU.mult)
                tt(y[:, 0:HEADS, :], y[:, 0:HEADS, :], G[:, :, cols], ALU.mult).then_inc(s_y, 1)

            dve.wait_ge(s_gate, HEADS)
            mix(0)
            for j in range(TT):
                if j + 1 < TT:
                    mix(j + 1)
                dve.wait_ge(s_op, j + 1)
                dve.wait_ge(s_h[j % 2], 16 * (j // 2 + 1))
                for half in range(2):
                    cols = slice(512 * half, 512 * half + 512)
                    last = tt(H[j % 2][:, cols], H[j % 2][:, cols], op[j % 2][half][:, :], ALU.add)
                last.then_inc(s_h2, 1)
                if j == 0:
                    dve.wait_ge(s_c, 16)
                dve.wait_ge(s_r2, j + 1)
                step(nc.vector.reciprocal(sh[:, TT + j:TT + j + 1], sh[:, TT + j:TT + j + 1]))
                if j >= 2:
                    dve.wait_ge(s_t2, j - 1)
                    dve.wait_ge(s_st, 16 * (4 + 2 * (j - 1)))
                stt(X2[j % 2][:, :], H[j % 2][:, :], sh[:, TT + j:TT + j + 1], gffn[:, :], ALU.mult, ALU.mult).then_inc(s_x2, 1)


def phase_route(nc, ins, K, h2_d, acc_d, tbl_d):
    with ExitStack() as ctx:
        def sb(name, shape, dt=F32):
            return ctx.enter_context(nc.sbuf_tensor(name, shape, dt))

        def ps(name, shape):
            return ctx.enter_context(nc.psum_tensor(name, shape, F32))
        sem = lambda n: ctx.enter_context(nc.semaphore(n))
        wr, bias = K.wr, K.bias
        wgs, wus = sb("wgs", [P, KT, FF]), sb("wus", [P, KT, FF])
        wds = sb("wds", [P, 2, D])
        SC, BI, RE, MK, GT, SL, T1 = (sb(n, [P, TT, E_N]) for n in ("SC", "BI", "RE", "MK", "GT", "SL", "T1"))
        MS = sb("MS", [P, TT, E_N])
        m8 = sb("m8", [P, TT, TOPK])
        s8 = sb("s8", [P, TT, TOPK])
        si = sb("si", [P, TT * TOPK], I32)
        junk = sb("junk3", [P, E_N])
        pay = sb("pay", [P, TT, TOPK, 2])
        gs = sb("gs", [P, TT])
        before = sb("before", [P, P])
        cnt, ext, inc, b0, ba = (sb(n, [P, E_N]) for n in ("cnt", "ext", "inc", "b0", "ba"))
        e0 = sb("e0", [P, E_N])
        zero = sb("zero", [P, E_N])
        pidx = sb("pidx", [P, 1])
        tex = sb("tex", [P, 1])
        exrow = sb("exrow", [1, ITEMS])
        twos = sb("twos", [1, 32])
        pr = sb("pr", [1, 1])
        tj = sb("tj", [1, 32])
        fill = sb("fill", [ITEMS, CAP, 2])
        tbl = sb("tbl", [ITEMS, CAP, 2])
        hs = sb("hs", [P, 2, T])
        LT = sb("LT", [E_N, T])
        sgs = sb("sgs", [P, 512])
        H = [sb(f"HH{i}", [P, D]) for i in range(2)]
        lg, rk, ct = ps("lg", [P, TT, E_N]), ps("rk", [P, TT, E_N]), ps("ct", [P, 512])
        pair = [[ps(f"pair{i}{k}", [P, 512]) for k in range(2)] for i in range(2)]
        tp = ps("tp", [P, 512])
        s_ws, s_wd = sem("shared_in"), sem("shared_down_in")
        s_k0, s_k = sem("patterns_cleared"), sem("patterns_set")
        s_fi, s_fo = sem("table_blank"), sem("table_blank_written")
        s_lg, s_sc, s_mk, s_rk = sem("logits"), sem("sigmoids_r"), sem("chosen"), sem("ranks")
        s_pay, s_sca, s_ti = sem("payload"), sem("table_scattered"), sem("table_in")
        s_tp, s_tk, s_ex, s_er = sem("table_turned"), sem("table_kept"), sem("experts_counted"), sem("experts_row")
        s_gu, s_sg, s_gv, s_hs = sem("gate_up"), sem("sig_shared"), sem("silu_shared"), sem("hidden_shared")
        s_y, s_a, s_ao = sem("shared_out"), sem("acc_tile"), sem("acc_written")
        s_h = [sem(f"h2_in{i}") for i in range(2)]
        s_d = sem("dve_steps3")
        s_pre = sem("first_weights_in")
        s_up, s_lt, s_lk = sem("up_done"), sem("logits_by_expert"), sem("logits_kept")
        block = ctx.enter_context(nc.Block())
        h2v = h2_d[0:T, :].rearrange("(j p) n -> p j n", p=P)
        accv = acc_d[0:T, :].rearrange("(j p) n -> p j n", p=P)
        tbl_rows = tbl_d.rearrange("(i c) w -> i (c w)", c=CAP)

        @block.sync
        def _(sp):
            sp.dma_start(wgs[:, :, :], ins["w_gate_s"].rearrange("l (p t) n -> p (l t) n", t=KT)).then_inc(s_ws, 16)
            sp.dma_start(wus[:, :, :], ins["w_up_s"].rearrange("l (p t) n -> p (l t) n", t=KT)).then_inc(s_ws, 16)
            sp.dma_start(wds[:, :, :], ins["w_down_s"].rearrange("l (f p) n -> p (l f) n", p=P)).then_inc(s_wd, 16)
            for e in range(2):
                for k, src in enumerate(expert_weights(ins)[:3 - e]):
                    sp.dma_start(K.WR[e][k][:, :].rearrange("p (o t f) -> p o t f", o=1, t=src.shape[2]), src[:, e:e + 1, :, :]) \
                        .then_inc(s_pre, 16)
            sp.wait_ge(s_fi, 2)
            sp.dma_start(tbl_rows, fill[:, :, :].rearrange("i c w -> i (c w)")).then_inc(s_fo, 16)
            sp.dma_start(acc_d[T:T + CAP, :], h2_d[T:T + CAP, :]).then_inc(s_ao, 16)
            for j in range(TT):
                if j >= 2:
                    sp.wait_ge(s_ao, 16 * j)
                sp.dma_start(H[j % 2][:, :], h2v[:, j, :]).then_inc(s_h[j % 2], 16)
                if j:
                    sp.wait_ge(s_a, j)
                    sp.dma_start(accv[:, j - 1, :], H[(j - 1) % 2][:, :]).then_inc(s_ao, 16)
            sp.wait_ge(s_a, TT)
            sp.dma_start(accv[:, TT - 1, :], H[(TT - 1) % 2][:, :]).then_inc(s_ao, 16)
            sp.wait_ge(s_ao, 16 * (TT + 1))
            sp.wait_ge(s_pre, 16 * 5)
            sp.wait_ge(s_sca, 16 * TT * TOPK)
            sp.dma_start(tbl[:, :, :].rearrange("i c w -> i (c w)"), tbl_rows).then_inc(s_ti, 16)
            sp.wait_ge(s_ti, 16)

        @block.gpsimd
        def _(pool):
            pool.memset(before[:, :], 1.0).then_inc(s_k0, 1)
            pool.memset(fill[:, :, 1:2], 0.0).then_inc(s_fi, 1)
            pool.iota(fill[:, :, 0], [[1, CAP]], base=T, channel_multiplier=0, allow_small_or_imprecise_dtypes=True).then_inc(s_fi, 1)
            pool.memset(zero[:, :], 0.0).then_inc(s_k, 1)
            pool.iota(e0[:, :], [[CAP, E_N]], base=0, channel_multiplier=0, allow_small_or_imprecise_dtypes=True).then_inc(s_k, 1)
            pool.iota(pidx[:, :], [[0, 1]], base=0, channel_multiplier=1, allow_small_or_imprecise_dtypes=True).then_inc(s_k, 1)
            pool.iota(exrow[:, 0:E_N], [[1, E_N]], base=0, channel_multiplier=0, allow_small_or_imprecise_dtypes=True).then_inc(s_k, 1)
            pool.iota(twos[:, :], [[2, 32]], base=0, channel_multiplier=0, allow_small_or_imprecise_dtypes=True).then_inc(s_k, 1)
            pool.iota(pay[:, :, :, 0], [[P, TT], [0, TOPK]], base=0, channel_multiplier=1,
                      allow_small_or_imprecise_dtypes=True).then_inc(s_k, 1)
            pool.wait_ge(s_k0, 1)
            pool.affine_select(out=before[:, :], in_=before[:, :], compare_op=ALU.is_gt, fill=0.0,
                               base=0, pattern=[[1, P]], channel_multiplier=-1).then_inc(s_k, 1)
            pool.wait_ge(s_fo, 16)
            for j in range(TT):
                pool.wait_ge(s_pay, j + 1)
                for k in range(TOPK):
                    pool.indirect_dma_start(tbl_d, bass.IndirectOffsetOnAxis(ap=si[:, j * TOPK + k:j * TOPK + k + 1], axis=0),
                                            pay[:, j, k, :], None).then_inc(s_sca, 16)
            pool.wait_ge(s_sca, 16 * TT * TOPK)

        @block.tensor
        def _(pe):
            for b in range(2):
                for t in range(KT):
                    last = pe.matmul(pair[1][b][0:E_N, :], wr[:, t, :], K.xT[:, t, 512 * b:512 * b + 512], start=(t == 0), stop=(t == KT - 1))
                last.then_inc(s_lt, 1)
            for b in range(2):
                pe.wait_ge(s_lk, b + 1)
                for j in range(4 * b, 4 * b + 4):
                    last = pe.transpose(lg[:, j, :], LT[:, j * P:j * P + P], K.ident[0:E_N, 0:E_N])
            last.then_inc(s_lg, 1)

            def hidden(b, f):
                g = 2 * b + f
                if g >= 2:
                    pe.wait_ge(s_hs, g - 1)
                for w, out, s in ((wgs, pair[g % 2][0], s_gu), (wus, pair[g % 2][1], s_up)):
                    for t in range(KT):
                        last = pe.matmul(out[:, :], w[:, t, f * P:f * P + P], K.xT[:, t, 512 * b:512 * b + 512],
                                         start=(t == 0), stop=(t == KT - 1))
                    last.then_inc(s, 1)

            pe.wait_ge(s_ws, 32)
            hidden(0, 0)
            pe.wait_ge(s_k, 7)
            pe.wait_ge(s_mk, 1)
            for j in range(TT):
                last = pe.matmul(rk[:, j, :], before[:, :], MK[:, j, :], start=True, stop=(j == 0))
                if j:
                    last = pe.matmul(rk[:, j, :], K.ones[:, :], MS[:, j - 1, :], start=False, stop=True)
            last = pe.matmul(ct[:, 0:E_N], K.ones[:, :], MS[:, TT - 1, :], start=True, stop=True)
            last.then_inc(s_rk, 1)
            hidden(0, 1)
            pe.wait_ge(s_ex, 1)
            pe.matmul(tp[0:1, 0:ITEMS - E_N], tex[:, 0:1], K.ident[:, 0:ITEMS - E_N], start=True, stop=True).then_inc(s_er, 1)
            hidden(1, 0)
            hidden(1, 1)
            pe.wait_ge(s_wd, 16)
            for j in range(TT):
                if j < 2:
                    pe.wait_ge(s_hs, j + 3)
                if j >= 2:
                    pe.wait_ge(s_a, j - 1)
                for half in range(2):
                    for f in range(2):
                        last = pe.matmul(pair[j % 2][half][:, :], hs[:, f, j * P:j * P + P], wds[:, f, 512 * half:512 * half + 512],
                                         start=(f == 0), stop=(f == 1))
                last.then_inc(s_y, 1)
            pe.wait_ge(s_ti, 16)
            pe.wait_ge(s_tk, 1)
            for k in range(2):
                pe.transpose(tp[0:P, k * ITEMS:(k + 1) * ITEMS], tbl[:, 0:P, k], K.ident[0:ITEMS, 0:ITEMS])
                last = pe.transpose(tp[0:CAP1, (2 + k) * ITEMS:(3 + k) * ITEMS], tbl[:, P:CAP, k], K.ident[0:ITEMS, 0:ITEMS])
            last.then_inc(s_tp, 1)

        @block.scalar
        def _(act):
            for b in range(2):
                act.wait_ge(s_lt, b + 1)
                act.copy(LT[:, 512 * b:512 * b + 512], pair[1][b][0:E_N, :]).then_inc(s_lk, 1)
            act.wait_ge(s_lg, 1)
            act.activation(SC[:, :, :], lg[:, :, :], ACT.Sigmoid).then_inc(s_sc, 1)
            for g in range(4):
                act.wait_ge(s_gu, g + 1)
                if g:
                    act.wait_ge(s_hs, g)
                act.activation(sgs[:, :], pair[g % 2][0][:, :], ACT.Sigmoid).then_inc(s_sg, 1)

        @block.vector
        def _(dve):
            step = Chain(dve, s_d)
            tt, ts, stt = nc.vector.tensor_tensor, nc.vector.tensor_scalar, nc.vector.scalar_tensor_tensor

            def shared(g):
                b, f = divmod(g, 2)
                dve.wait_ge(s_sg, g + 1)
                tt(sgs[:, :], sgs[:, :], pair[g % 2][0][:, :], ALU.mult).then_inc(s_gv, 1)
                dve.wait_ge(s_gv, g + 1)
                dve.wait_ge(s_up, g + 1)
                tt(hs[:, f, 512 * b:512 * b + 512], sgs[:, :], pair[g % 2][1][:, :], ALU.mult).then_inc(s_hs, 1)

            def over_tiles(v):
                return v[:, :].rearrange("p (o e) -> p o e", o=1).to_broadcast([P, TT, E_N])

            dve.wait_ge(s_k, 7)
            dve.wait_ge(s_sc, 1)
            step(tt(BI[:, :, :], SC[:, :, :], over_tiles(bias), ALU.add))
            for j in range(TT):
                last = nc.vector.max(m8[:, j, :], BI[:, j, :])
            step(last)
            for j in range(TT):
                last = nc.vector.match_replace(RE[:, j, :], m8[:, j, :], BI[:, j, :], -1e30)
            step(last)
            step(tt(MK[:, :, :], RE[:, :, :], BI[:, :, :], ALU.not_equal))
            step(nc.vector.tensor_copy(MS[:, 0, :], MK[:, 0, :]))
            for j in range(1, TT):
                step(tt(MS[:, j, :], MS[:, j - 1, :], MK[:, j, :], ALU.add))
            dve.sem_inc(s_mk, 1)
            step(tt(GT[:, :, :], SC[:, :, :], MK[:, :, :], ALU.mult))
            step(nc.vector.reduce_sum(gs[:, :], GT[:, :, :], mybir.AxisListType.X))
            step(nc.vector.reciprocal(gs[:, :], gs[:, :]))
            step(tt(GT[:, :, :], GT[:, :, :], bcast(gs[:, :], E_N), ALU.mult))
            step(ts(GT[:, :, :], GT[:, :, :], ROUTED_SCALE, None, ALU.mult))
            dve.wait_ge(s_rk, 1)
            step(nc.vector.tensor_copy(cnt[:, :], ct[:, 0:E_N]))
            step(ts(ext[:, :], cnt[:, :], float(CAP), None, ALU.is_gt))
            for m in range(2, MORE + 1):
                step(stt(ext[:, :], cnt[:, :], float(m * CAP), ext[:, :], ALU.is_gt, ALU.add))
            step(nc.vector.tensor_tensor_scan(inc[:, :], ext[:, :], zero[:, :], 0.0, ALU.add, ALU.add))
            step(tt(b0[:, :], inc[:, :], ext[:, :], ALU.subtract))
            step(ts(b0[:, :], b0[:, :], float(CAP), float((E_N - 1) * CAP), ALU.mult, ALU.add))
            step(tt(ba[:, :], b0[:, :], e0[:, :], ALU.subtract))
            step(ts(T1[:, :, :], rk[:, :, :], float(CAP), None, ALU.is_ge))
            step(tt(T1[:, :, :], T1[:, :, :], over_tiles(ba), ALU.mult))
            step(tt(T1[:, :, :], T1[:, :, :], over_tiles(e0), ALU.add))
            step(tt(SL[:, :, :], rk[:, :, :], T1[:, :, :], ALU.add))
            step(stt(SL[:, :, :], SL[:, :, :], 1.0, MK[:, :, :], ALU.add, ALU.mult))
            step(ts(SL[:, :, :], SL[:, :, :], -1.0, None, ALU.add))
            for j in range(TT):
                last = nc.vector.max(s8[:, j, :], SL[:, j, :])
            step(last)
            step(nc.vector.tensor_copy(si[:, :], s8[:, :, :].rearrange("p j k -> p (j k)")))
            for j in range(TT):
                for k in range(TOPK):
                    step(stt(junk[:, :], SL[:, j, :], s8[:, j, k:k + 1], GT[:, j, :], ALU.is_equal, ALU.mult,
                             accum_out=pay[:, j, k, 1:2]))
                dve.sem_inc(s_pay, 1)
                if j == 0:
                    step(ts(junk[:, :], inc[:, :], pidx[:, 0:1], None, ALU.is_le))
                    step(nc.vector.reduce_sum(tex[:, :], junk[:, :], mybir.AxisListType.X))
                    step(ts(tex[:, :], tex[:, :], float(E_N - 1), None, ALU.min))
                    dve.sem_inc(s_ex, 1)
                    shared(0)
                if j == 3:
                    shared(1)
            dve.wait_ge(s_er, 1)
            step(nc.vector.tensor_copy(exrow[:, E_N:ITEMS], tp[0:1, 0:ITEMS - E_N]))
            step(nc.vector.tensor_copy(K.expert[:, :], exrow[:, :]))
            step(ts(tj[:, :], twos[:, :], inc[0:1, E_N - 1:E_N], None, ALU.is_lt))
            step(nc.vector.reduce_sum(pr[:, :], tj[:, :], mybir.AxisListType.X))
            step(ts(pr[:, :], pr[:, :], float(E_N // 2 - 1), None, ALU.add))
            step(nc.vector.tensor_copy(K.pairs[:, :], pr[:, :]))
            dve.sem_inc(s_tk, 1)
            shared(2)
            shared(3)
            for j in range(TT):
                dve.wait_ge(s_y, j + 1)
                dve.wait_ge(s_h[j % 2], 16 * (j // 2 + 1))
                for half in range(2):
                    cols = slice(512 * half, 512 * half + 512)
                    last = tt(H[j % 2][:, cols], H[j % 2][:, cols], pair[j % 2][half][:, :], ALU.add)
                last.then_inc(s_a, 1)
            dve.wait_ge(s_tp, 1)
            for k, n in ((0, P), (1, CAP1)):
                nc.vector.tensor_copy(K.idx[k][:, :], tp[0:n, 2 * k * ITEMS:(2 * k + 1) * ITEMS])
                step(nc.vector.tensor_copy(K.gate[k][:, :], tp[0:n, (2 * k + 1) * ITEMS:(2 * k + 2) * ITEMS]))


def expert_weights(ins):
    return (ins["w_gate_e"].rearrange("l e (p t) f -> p (l e) t f", t=KT),
            ins["w_up_e"].rearrange("l e (p t) f -> p (l e) t f", t=KT),
            ins["w_down_e"].rearrange("l e (f p) n -> p (l e) f n", p=P))


def phase_experts(nc, ins, K, xn2_d, acc_d):
    weights = expert_weights(ins)
    WR = K.WR
    with ExitStack() as ctx:
        def sb(name, shape, dt=F32):
            return ctx.enter_context(nc.sbuf_tensor(name, shape, dt))

        def ps(name, shape):
            return ctx.enter_context(nc.psum_tensor(name, shape, F32))
        sem = lambda n: ctx.enter_context(nc.semaphore(n))
        two = range(2)
        WH = [[sb(f"WH{i}{k}", [P, KT * FF], F32R) for k in range(3)] for i in two]
        WL = [[sb(f"WL{i}{k}", [P, KT * FF], F32R) for k in range(3)] for i in two]
        XG = [(sb(f"XG{i}", [P, D]), sb(f"XH{i}", [CAP1, D])) for i in two]
        XS = [sb(f"XS{i}", [P, KT, 2, CAP], F32R) for i in two]
        GS, US, SS, HF = (sb(n, [P, 2, CAP]) for n in ("GS", "US", "SS", "HF"))
        HH = [sb(f"hidh{i}", [P, 2, 2 * P], F32R) for i in two]
        HL = [sb(f"hidr{i}", [P, 2, 2 * P], F32R) for i in two]
        YE = (sb("YE", [P, D]), sb("YF", [CAP1, D]))
        gi = [(sb(f"gi{i}", [P, 1], I32), sb(f"gj{i}", [CAP1, 1], I32)) for i in two]
        si = [(sb(f"sia{i}", [P, 1], I32), sb(f"sib{i}", [CAP1, 1], I32)) for i in two]
        gt = [(sb(f"gta{i}", [P, 1]), sb(f"gtb{i}", [CAP1, 1])) for i in two]
        gu = [ps(f"gu{f}", [P, 2, CAP]) for f in range(3)]
        gu.append(gu[0])
        xp = [ps(f"xp{i}", [P, 3, CAP]) for i in two]
        yp = [ps(f"ype{h}", [P, 512]) for h in range(3)]
        yp.append(yp[0])
        s_raw = [[sem(f"weights_in{i}{k}") for k in range(3)] for i in two]
        s_hi, s_lo = sem("gate_up_high"), sem("gate_up_low")
        s_dhi, s_dlo = sem("down_high"), sem("down_low")
        s_pi, s_g = sem("pool_copies"), [sem(f"gathered{i}") for i in two]
        s_gt, s_ad, s_free = sem("gates_set"), sem("rows_added"), sem("rows_free")
        s_tp, s_xh, s_xl = sem("x_turned"), sem("x_high"), sem("x_low")
        s_gu, s_ss, s_he, s_hc, s_z = sem("gate_up_done"), sem("sig_e"), sem("hidden_e"), sem("hidden_steps"), sem("hidden_zeroed")
        s_y, s_ya, s_gk = sem("y_done"), sem("y_kept"), sem("gate_up_kept")
        turn = {e: sem(f"turn_{e}") for e in ("sp", "pool")}
        block = ctx.enter_context(nc.Block())
        LIMIT = ITEMS // 2 - 1
        WIDE = KT * FF
        PIECES = [(0, 0, WIDE), (1, 0, WIDE // 2), (1, WIDE // 2, WIDE)]
        NP = len(PIECES)

        def pairs(engine):
            return engine.value_load(K.pairs[0:1, 0:1], min_val=E_N // 2 - 1, max_val=LIMIT - 1)

        @block.sync
        def _(sp):
            def load(n, q, matrices):
                e = sp.value_load(K.expert[0:1, bass.ds(n, 1)], min_val=0, max_val=E_N - 1)
                for k in matrices:
                    src = weights[k]
                    if k == 2 and not isinstance(n, int):
                        sp.wait_ge(s_dlo, n - 1)
                        sp.sem_inc(turn["sp"], 1)
                    elif k < 2:
                        sp.wait_ge(s_lo, n * NP - 2 * NP + (1, 3)[k])
                        sp.sem_inc(turn["sp"], 1)
                    sp.dma_start(WR[q][k][:, :].rearrange("p (o t f) -> p o t f", o=1, t=src.shape[2]), src[:, bass.ds(e, 1), :, :]) \
                        .then_inc(s_raw[q][k], 16)

            load(2, 0, (0, 1))
            load(1, 1, (2,))
            last = pairs(sp)
            with sp.Fori(0, last) as i:
                for q in two:
                    load(i * 2 + (q + 3), 1 - q, (0, 1))
                    load(i * 2 + (q + 2), q, (2,))
            for k in two:
                sp.wait_ge(s_raw[0][k], last * 16 + 16)
                sp.sem_inc(turn["sp"], 1)

        @block.gpsimd
        def _(pool):
            def gather(q, n, first):
                for r in two:
                    pool.tensor_copy(gi[q][r][:, :], K.idx[r][:, bass.ds(n, 1)]).then_inc(s_pi, 1)
                pool.wait_ge(s_pi, first + 2)
                pool.sem_inc(turn["pool"], 1)
                for r in two:
                    pool.indirect_dma_start(XG[q][r][:, :], None, xn2_d, bass.IndirectOffsetOnAxis(ap=gi[q][r][:, :], axis=0)) \
                        .then_inc(s_g[q], 16)

            def add_rows(i, q, copies, ahead):
                n = i * 2 + q
                pool.wait_ge(s_ya, n * 4 + 5)
                pool.sem_inc(turn["pool"], 1)
                for r in two:
                    pool.tensor_copy(si[q][r][:, :], K.idx[r][:, bass.ds(n, 1)]).then_inc(s_pi, 1)
                pool.wait_ge(s_pi, copies + 2)
                pool.sem_inc(turn["pool"], 1)
                for r in two:
                    pool.indirect_dma_start(acc_d, bass.IndirectOffsetOnAxis(ap=si[q][r][:, :], axis=0), YE[r][:, :], None,
                                            compute_op=ALU.add).then_inc(s_ad, 16)
                if ahead:
                    pool.wait_ge(s_g[q], i * 32 + 64)
                    pool.sem_inc(turn["pool"], 1)
                    pool.wait_ge(s_tp, n * 3 + 9)
                    pool.sem_inc(turn["pool"], 1)
                    gather(q, n + 4, copies + 2)
                pool.wait_ge(s_ad, n * 32 + 32)
                pool.sem_inc(s_free, 1)

            def gates(i, q):
                for r in two:
                    last = pool.tensor_copy(gt[q][r][:, :], K.gate[r][:, bass.ds(i * 2 + q, 1)])
                last.then_inc(s_gt, 1)

            gather(0, 0, 0)
            gather(1, 1, 2)
            for q in two:
                for part in (HH, HL):
                    pool.memset(part[q][:, :, CAP:].bitcast(F32), 0.0).then_inc(s_z, 1)
            pool.sem_inc(s_free, 1)
            for q in two:
                pool.wait_ge(s_g[q], 32)
                pool.wait_ge(s_tp, 3 * q + 3)
                gather(q, 2 + q, 4 + 2 * q)
            last = pairs(pool)
            with pool.Fori(0, last) as i:
                for q in two:
                    gates(i, q)
                    add_rows(i, q, i * 8 + (8 + 4 * q), True)
            for q in two:
                gates(last, q)
                add_rows(last, q, last * 8 + (8 + 2 * q), False)
            for q in two:
                pool.wait_ge(s_g[q], last * 32 + 64)
                pool.sem_inc(turn["pool"], 1)

        @block.tensor
        def _(pe):
            pe.sem_inc(s_y, 1)

            def turned(q, n, c):
                pe.wait_ge(s_xl, n * 3 + (3, 2, 4)[c])
                for t in range(3 * c, min(3 * c + 3, KT)):
                    for r, (a, b) in enumerate(((0, P), (P, CAP))):
                        rows = XG[q][r][:, :].rearrange("p (k t) -> p t k", t=KT)
                        last = pe.transpose(xp[c % 2][:, t - 3 * c, a:b], rows[:, t, :], K.ident[0:b - a, 0:b - a])
                last.then_inc(s_tp, 1)

            def gate_up(q, n, g):
                f, k = divmod(g, 2)
                if f == 0:
                    pe.wait_ge(s_lo, n * NP + (1, 3)[k])
                if g in (0, 3):
                    pe.wait_ge(s_gk, n * 4 + 1 + g // 3)
                high, low = (W[q][k][:, :].rearrange("p (t f) -> p t f", t=KT) for W in (WH, WL))
                cols = slice(f * P, f * P + P)
                for t in range(KT):
                    pe.matmul(gu[g][:, :, :], high[:, t, cols], XS[q][:, t, :, :], start=(t == 0), stop=False)
                    last = pe.matmul(gu[g][:, 0, :], low[:, t, cols], XS[q][:, t, 0, :], start=False, stop=(t == KT - 1))
                last.then_inc(s_gu, 1)

            def down(q, n, g):
                r, half = divmod(g, 2)
                if g in (0, 3):
                    pe.wait_ge(s_ya, n * 4 + 1 + g // 3)
                if g == 0:
                    pe.wait_ge(s_dlo, n + 1)
                    pe.wait_ge(s_he, n * 2 + 2)
                high, low = (W[q][2][:, :].rearrange("p (f n) -> p f n", f=2) for W in (WH, WL))
                rows, cols = slice(r * P, r * P + P), slice(512 * half, 512 * half + 512)
                for f in two:
                    hh, hl = HH[q][:, f, rows], HL[q][:, f, rows]
                    pe.matmul(yp[g][:, :], hh, high[:, f, cols], start=(f == 0), stop=False)
                    pe.matmul(yp[g][:, :], hh, low[:, f, cols], start=False, stop=False)
                    last = pe.matmul(yp[g][:, :], hl, high[:, f, cols], start=False, stop=(f == 1))
                last.then_inc(s_y, 1)

            def turn_(i, q, ahead):
                n = i * 2 + q
                if ahead >= 1:
                    pe.wait_ge(s_xl, n * 3 + 9)
                    gate_up(1 - q, n + 1, 0)
                    gate_up(1 - q, n + 1, 1)
                if ahead >= 2:
                    pe.wait_ge(s_g[q], i * 32 + 64)
                    turned(q, n + 2, 0)
                if ahead >= 1:
                    gate_up(1 - q, n + 1, 2)
                if ahead >= 2:
                    turned(q, n + 2, 1)
                if ahead >= 1:
                    gate_up(1 - q, n + 1, 3)
                down(q, n, 0)
                if ahead >= 2:
                    turned(q, n + 2, 2)
                for g in (1, 2, 3):
                    down(q, n, g)

            pe.wait_ge(s_g[0], 32)
            for c in range(3):
                turned(0, 0, c)
            pe.wait_ge(s_g[1], 32)
            pe.wait_ge(s_xl, 6)
            for g in range(4):
                gate_up(0, 0, g)
                if g < 3:
                    turned(1, 1, g)
            pe.wait_ge(s_z, 4)
            last = pairs(pe)
            with pe.Fori(0, last) as i:
                for q in two:
                    turn_(i, q, 2)
            for q in two:
                turn_(last, q, 1 - q)

        @block.scalar
        def _(act):
            act.sem_inc(s_ya, 1)

            def high(k, q, n, loads):
                m, a, b = PIECES[k]
                if loads is not None:
                    act.wait_ge(s_gu, n * 4 - 4)
                    act.wait_ge(s_raw[q][m], loads * 16)
                act.activation(WH[q][m][:, a:b], WR[q][m][:, a:b], ACT.Copy).then_inc(s_hi, 1)

            def high_down(q, n, loads):
                if not isinstance(n, int):
                    act.wait_ge(s_y, n * 4 - 3)
                    act.wait_ge(s_raw[q][2], loads * 16)
                act.activation(WH[q][2][:, :], WR[q][2][:, :], ACT.Copy).then_inc(s_dhi, 1)

            def keep(c, q, n):
                act.wait_ge(s_tp, n * 3 + c + 1)
                tiles = slice(3 * c, min(3 * c + 3, KT))
                act.activation(XS[q][:, tiles, 0, :], xp[c % 2][:, 0:tiles.stop - tiles.start, :], ACT.Copy).then_inc(s_xh, 1)

            def sigmoid(f, n):
                act.wait_ge(s_gk, n * 4 + 2 * f + 2)
                act.activation(SS[:, f, :], GS[:, f, :], ACT.Sigmoid).then_inc(s_ss, 1)

            def turn_(i, q, ahead):
                n = i * 2 + q
                if ahead >= 2:
                    high(1, q, n + 2, i + 1)
                if ahead >= 1:
                    sigmoid(0, n + 1)
                if ahead >= 2:
                    high(2, q, n + 2, i + 1)
                if ahead >= 2:
                    keep(0, q, n + 2)
                if ahead >= 1:
                    high_down(1 - q, n + 1, i + 1)
                if ahead >= 2:
                    keep(1, q, n + 2)
                if ahead >= 1:
                    sigmoid(1, n + 1)
                act.wait_ge(s_gt, n + 1)
                act.wait_ge(s_free, n + 1)
                for g in range(4):
                    r, half = divmod(g, 2)
                    act.wait_ge(s_y, n * 4 + g + 2)
                    act.activation(YE[r][:, 512 * half:512 * half + 512], yp[g][0:(P, CAP1)[r], :], ACT.Copy,
                                   scale=gt[q][r][:, 0:1]).then_inc(s_ya, 1)
                    if g == 0 and ahead >= 2:
                        keep(2, q, n + 2)
                    if g == 1 and ahead >= 2:
                        high(0, 1 - q, n + 3, i + (1 + q))

            for k in range(3):
                high(k, 0, 0, None)
            for c in range(3):
                keep(c, 0, 0)
            for k in range(3):
                high(k, 1, 1, None)
            keep(0, 1, 1)
            sigmoid(0, 0)
            keep(1, 1, 1)
            keep(2, 1, 1)
            high_down(0, 0, 1)
            sigmoid(1, 0)
            high(0, 0, 2, 1)
            last = pairs(act)
            with act.Fori(0, last) as i:
                for q in two:
                    turn_(i, q, 2)
            for q in two:
                turn_(last, q, 1 - q)

        @block.vector
        def _(dve):
            step = Chain(dve, s_hc)
            tt = nc.vector.tensor_tensor
            dve.sem_inc(s_xl, 3)
            dve.sem_inc(s_gk, 1)

            def low(k, q, n):
                m, a, b = PIECES[k]
                dve.wait_ge(s_hi, n * NP + k + 1)
                tt(WL[q][m][:, a:b], WR[q][m][:, a:b], WH[q][m][:, a:b].bitcast(F32), ALU.subtract).then_inc(s_lo, 1)

            def low_down(q, n):
                dve.wait_ge(s_dhi, n + 1)
                tt(WL[q][2][:, :], WR[q][2][:, :], WH[q][2][:, :].bitcast(F32), ALU.subtract).then_inc(s_dlo, 1)

            def keep(c, q, n):
                dve.wait_ge(s_xh, n * 3 + c + 1)
                tiles = slice(3 * c, min(3 * c + 3, KT))
                tt(XS[q][:, tiles, 1, :], xp[c % 2][:, 0:tiles.stop - tiles.start, :], XS[q][:, tiles, 0, :].bitcast(F32), ALU.subtract) \
                    .then_inc(s_xl, 1)

            def total(out, g, n):
                dve.wait_ge(s_gu, n * 4 + g + 1)
                step(nc.vector.tensor_copy(out, gu[g][:, 1, :]))
                tt(out, out, gu[g][:, 0, :], ALU.add).then_inc(s_gk, 1)

            def hidden(f, q, n):
                dve.wait_ge(s_ss, n * 2 + f + 1)
                step(tt(SS[:, f, :], SS[:, f, :], GS[:, f, :], ALU.mult))
                if f == 0 and not isinstance(n, int):
                    dve.wait_ge(s_y, n * 4 - 3)
                dve.wait_ge(s_gk, n * 4 + 2 * f + 3)
                step(tt(HF[:, f, :], SS[:, f, :], US[:, f, :], ALU.mult))
                step(nc.vector.tensor_copy(HH[q][:, f, 0:CAP], HF[:, f, :]))
                tt(HL[q][:, f, 0:CAP], HF[:, f, :], HH[q][:, f, 0:CAP].bitcast(F32), ALU.subtract).then_inc(s_he, 1)

            def turn_(i, q, ahead):
                n, o = i * 2 + q, 1 - q
                if ahead >= 1:
                    total(GS[:, 0, :], 0, n + 1)
                if ahead >= 2:
                    low(1, q, n + 2)
                if ahead >= 1:
                    total(US[:, 0, :], 1, n + 1)
                    hidden(0, o, n + 1)
                if ahead >= 2:
                    low(2, q, n + 2)
                    keep(0, q, n + 2)
                if ahead >= 1:
                    total(GS[:, 1, :], 2, n + 1)
                    low_down(o, n + 1)
                if ahead >= 2:
                    keep(1, q, n + 2)
                if ahead >= 1:
                    total(US[:, 1, :], 3, n + 1)
                if ahead >= 2:
                    keep(2, q, n + 2)
                if ahead >= 1:
                    hidden(1, o, n + 1)
                if ahead >= 2:
                    low(0, o, n + 3)

            for k in range(3):
                low(k, 0, 0)
            for c in range(3):
                keep(c, 0, 0)
            for k in range(3):
                low(k, 1, 1)
            total(GS[:, 0, :], 0, 0)
            total(US[:, 0, :], 1, 0)
            keep(0, 1, 1)
            hidden(0, 0, 0)
            total(GS[:, 1, :], 2, 0)
            keep(1, 1, 1)
            total(US[:, 1, :], 3, 0)
            keep(2, 1, 1)
            low_down(0, 0)
            hidden(1, 0, 0)
            low(0, 0, 2)
            last = pairs(dve)
            with dve.Fori(0, last) as i:
                step.enter(i, 20)
                for q in two:
                    turn_(i, q, 2)
            step.leave(last)
            turn_(last, 0, 1)


def phase_final(nc, ins, K, acc_d, out):
    with ExitStack() as ctx:
        def sb(name, shape, dt=F32):
            return ctx.enter_context(nc.sbuf_tensor(name, shape, dt))
        sem = lambda n: ctx.enter_context(nc.semaphore(n))
        A = [sb(f"A{j}", [P, D]) for j in range(TT)]
        junk = [sb(f"junkf{i}", [P, D]) for i in range(2)]
        ss, rt = sb("ssf", [P, TT]), sb("rtf", [P, TT])
        gf = sb("gf", [P, D])
        s_a = [sem(f"acc_in{j}") for j in range(4)]
        s_gf, s_s, s_r, s_rc, s_o, s_out = sem("gfinal_in"), sem("squares_f"), sem("roots_f"), sem("recips_f"), sem("rows_f"), sem("out_written")
        block = ctx.enter_context(nc.Block())
        accv = acc_d[0:T, :].rearrange("(j p) n -> p j n", p=P)
        outv = out.rearrange("b (j p) n -> p (b j) n", p=P)

        @block.sync
        def _(sp):
            for j in range(TT):
                if j >= 4:
                    sp.wait_ge(s_a[j - 4], 16)
                sp.dma_start(A[j][:, :], accv[:, j, :]).then_inc(s_a[j % 4], 16)
                if j == 0:
                    sp.dma_start(gf[:, :], ins["norm_final_g"].rearrange("(o n) -> o n", o=1).to_broadcast([P, D])).then_inc(s_gf, 16)
            for j in range(TT):
                sp.wait_ge(s_o, j + 1)
                sp.dma_start(outv[:, j, :], A[j][:, :]).then_inc(s_out, 16)
            sp.wait_ge(s_out, 16 * TT)

        @block.scalar
        def _(act):
            for j in range(TT):
                act.wait_ge(s_a[j % 4], 16 * (j // 4 + 1))
                if j >= 2:
                    act.wait_ge(s_s, j - 1)
                act.activation(junk[j % 2][:, :], A[j][:, :], ACT.Square, accum_out=ss[:, j:j + 1]).then_inc(s_s, 1)
                act.wait_ge(s_s, j + 1)
                act.activation(rt[:, j:j + 1], ss[:, j:j + 1], ACT.Sqrt, bias=K.eps[:, 0:1], scale=1.0 / D).then_inc(s_r, 1)

        @block.vector
        def _(dve):
            dve.wait_ge(s_gf, 16)
            for j in range(TT):
                dve.wait_ge(s_r, j + 1)
                nc.vector.reciprocal(rt[:, j:j + 1], rt[:, j:j + 1]).then_inc(s_rc, 1)
                dve.wait_ge(s_rc, j + 1)
                nc.vector.scalar_tensor_tensor(A[j][:, :], A[j][:, :], rt[:, j:j + 1], gf[:, :], ALU.mult, ALU.mult).then_inc(s_o, 1)


def build(nc, ins, out):
    h2_d = nc.dram_tensor("h2_rows", (T + CAP, D), F32, kind="Internal").ap()
    xn2_d = nc.dram_tensor("xn2_rows", (T + CAP, D), F32, kind="Internal").ap()
    acc_d = nc.dram_tensor("acc_rows", (T + CAP, D), F32, kind="Internal").ap()
    tbl_d = nc.dram_tensor("slot_table", (ITEMS * CAP, 2), F32, kind="Internal").ap()

    class Kept:
        pass
    K = Kept()
    with ExitStack() as ctx:
        setup(nc, ctx, ins, K)
        with ExitStack() as wide:
            K.xT = wide.enter_context(nc.sbuf_tensor("xT", [P, KT, ALL], F32))
            with ExitStack() as mix:
                (K.WF,) = shared(nc, (("wf_parts", [P, 4, D]),))
                K.wi = mix.enter_context(nc.sbuf_tensor("wi", [P, KT, HW], F32))
                (K.XL,) = shared(nc, (("xT_low", [P, KT, T]),))
                K.GB = mix.enter_context(nc.sbuf_tensor("GB", [P, 2 * HEADS, T], F32))
                phase_norm(nc, ins, K)
                phase_mix(nc, mix, ins, K)
                phase_out(nc, ins, K, h2_d, xn2_d)
            phase_route(nc, ins, K, h2_d, acc_d, tbl_d)
        phase_experts(nc, ins, K, xn2_d, acc_d)
        phase_final(nc, ins, K, acc_d, out)


_INS = ["x", "meta_tokens", "norm_mix_g", "w_in", "lb_table", "hgrn_norm_g", "conv_w", "conv_norm_g", "w_out", "norm_ffn_g",
        "w_router", "router_bias", "w_gate_e", "w_up_e", "w_down_e", "w_gate_s", "w_up_s", "w_down_s", "norm_final_g"]


def kernel(**inputs):
    import numpy as np
    import concourse.bacc as bacc
    from concourse.bass_utils import run_bass_kernel_spmd

    nc = bacc.Bacc("TRN2", target_bir_lowering=False, num_devices=1)
    arrays, ins = {}, {}
    for name in _INS:
        a = np.ascontiguousarray(inputs[name])
        arrays[f"in_{name}"] = a
        ins[name] = nc.dram_tensor(f"in_{name}", a.shape, mybir.dt.from_np(a.dtype), kind="ExternalInput").ap()
    out = nc.dram_tensor("out_0", (1, T, D), F32, kind="ExternalOutput").ap()
    build(nc, ins, out)
    r = run_bass_kernel_spmd(nc, [arrays], core_ids=[0])
    return r.results[0]["out_0"]
```
